# Optimizing a Trainium2 kernel written in Bass

```python
import math
import jax, jax.numpy as jnp
from jax import lax
import numpy as np

D_MODEL = 1024
BATCH = 1
SEQ = 256
DEPTH = 2

N_A_LAYERS = DEPTH // 2
N_B_LAYERS = DEPTH - N_A_LAYERS
RMS_EPS = 1e-6

RET_HEADS = 4
RET_QK_DIM = D_MODEL // RET_HEADS
RET_V_DIM = 2 * D_MODEL // RET_HEADS
RET_CHUNK = 128
RET_IN = 2 * RET_HEADS * RET_QK_DIM + 2 * RET_HEADS * RET_V_DIM

FFN_HIDDEN = ((8 * D_MODEL + 3 * 256 - 1) // (3 * 256)) * 256

NSA_HEADS = 16
NSA_GROUPS = 4
NSA_REP = NSA_HEADS // NSA_GROUPS
NSA_HEAD_DIM = 64
CMP_LEN = 32
CMP_STRIDE = 16
CMP_HIDDEN = 256
SEL_LEN = 64
SEL_TOPK = 16
WINDOW = 512
Q_BLOCK = 128
NSA_IN = NSA_HEADS * NSA_HEAD_DIM + 3 * NSA_HEADS
KV_SHARED_OUT = 6 * NSA_GROUPS * NSA_HEAD_DIM

REL_BUCKETS = 32
REL_MAX_DIST = 128


def rms_norm(x, g):
    xf = x.astype(jnp.float32)
    y = xf * lax.rsqrt(jnp.mean(xf * xf, axis=-1, keepdims=True) + RMS_EPS)
    return (y * g.astype(jnp.float32)).astype(x.dtype)

def swiglu_ffn(x, w_in, w_out):
    gate, up = jnp.split(x @ w_in, 2, axis=-1)
    return (jax.nn.silu(gate) * up) @ w_out

def rotate_pairs(x, cos, sin):
    x1 = x[..., 0::2]
    x2 = x[..., 1::2]
    return jnp.stack([x1 * cos - x2 * sin, x1 * sin + x2 * cos], axis=-1).reshape(x.shape)

def t5_bucket(dist):
    n = jnp.maximum(dist, 0)
    max_exact = REL_BUCKETS // 2
    nf = jnp.maximum(n, 1).astype(jnp.float32)
    large = max_exact + (jnp.log(nf / max_exact) / math.log(REL_MAX_DIST / max_exact)
                         * (REL_BUCKETS - max_exact)).astype(jnp.int32)
    large = jnp.minimum(large, REL_BUCKETS - 1)
    return jnp.where(n < max_exact, n, large)

def masked_softmax(logits, mask):
    logits = jnp.where(mask, logits, -jnp.inf)
    m = jnp.max(logits, axis=-1, keepdims=True)
    m = jnp.where(jnp.isfinite(m), m, 0.0)
    p = jnp.exp(logits - m)
    return p / jnp.maximum(jnp.sum(p, axis=-1, keepdims=True), jnp.finfo(jnp.float32).tiny)

def retention_mixer(x, w_in, w_out):
    B, S, _ = x.shape
    h, dk, dv, C = RET_HEADS, RET_QK_DIM, RET_V_DIM, RET_CHUNK
    proj = x @ w_in
    q, k, v, g = jnp.split(proj, [h * dk, 2 * h * dk, 2 * h * dk + h * dv], axis=-1)
    q = q.reshape(B, S, h, dk).astype(jnp.float32)
    k = k.reshape(B, S, h, dk).astype(jnp.float32)
    v = v.reshape(B, S, h, dv).astype(jnp.float32)
    pos = jnp.arange(S, dtype=jnp.float32)
    theta = 1.0 / (10000.0 ** jnp.linspace(0.0, 1.0, dk // 2, dtype=jnp.float32))
    ang = pos[:, None] * theta[None, :]
    cos = jnp.cos(ang)[:, None, :]
    sin = jnp.sin(ang)[:, None, :]
    q = rotate_pairs(q, cos, sin)
    k = rotate_pairs(k, cos, sin) * (dk ** -0.5)
    log_gamma = jnp.log(1.0 - 2.0 ** (-5.0 - jnp.arange(h, dtype=jnp.float32)))
    idx = jnp.arange(C, dtype=jnp.float32)
    rel = idx[:, None] - idx[None, :]
    intra_decay = jnp.where(rel >= 0, jnp.exp(jnp.maximum(rel, 0.0) * log_gamma[:, None, None]), 0.0)
    q_decay = jnp.exp((idx + 1.0)[None, :] * log_gamma[:, None])
    k_decay = jnp.exp((C - 1.0 - idx)[None, :] * log_gamma[:, None])
    chunk_decay = jnp.exp(C * log_gamma)
    nC = S // C

    def to_chunks(t):
        return t.reshape(B, nC, C, h, t.shape[-1]).transpose(1, 0, 3, 2, 4)

    def step(state, inp):
        qc, kc, vc = inp
        scores = jnp.einsum('bhid,bhjd->bhij', qc, kc) * intra_decay
        o = (jnp.einsum('bhij,bhje->bhie', scores, vc)
             + jnp.einsum('bhid,bhde->bhie', qc * q_decay[..., None], state))
        state = (state * chunk_decay[:, None, None]
                 + jnp.einsum('bhjd,bhje->bhde', kc * k_decay[..., None], vc))
        return state, o

    state0 = jnp.zeros((B, h, dk, dv), jnp.float32)
    _, o = lax.scan(step, state0, (to_chunks(q), to_chunks(k), to_chunks(v)))
    o = o.transpose(1, 0, 3, 2, 4).reshape(B, S, h, dv)
    o = o * lax.rsqrt(jnp.mean(o * o, axis=-1, keepdims=True) + RMS_EPS)
    o = (o.reshape(B, S, h * dv) * jax.nn.silu(g.astype(jnp.float32))).astype(x.dtype)
    return o @ w_out

def nsa_shared_kv(h, kv_norm, kv_w, cmp_pe_k, cmp_w1_k, cmp_w2_k, cmp_pe_v, cmp_w1_v, cmp_w2_v):
    B, S, _ = h.shape
    G, d = NSA_GROUPS, NSA_HEAD_DIM
    kv = rms_norm(h, kv_norm) @ kv_w
    k_c, v_c, k_s, v_s, k_w, v_w = [t.reshape(B, S, G, d) for t in jnp.split(kv, 6, axis=-1)]
    n_cmp = (S - CMP_LEN) // CMP_STRIDE + 1
    blk_idx = np.arange(n_cmp)[:, None] * CMP_STRIDE + np.arange(CMP_LEN)[None, :]

    def compress(t, pe, w1, w2):
        blocks = t[:, blk_idx] + pe[:, None, :]
        blocks = blocks.transpose(0, 1, 3, 2, 4).reshape(B, n_cmp, G, CMP_LEN * d)
        return jax.nn.silu(blocks @ w1) @ w2

    kc = compress(k_c, cmp_pe_k, cmp_w1_k, cmp_w2_k)
    vc = compress(v_c, cmp_pe_v, cmp_w1_v, cmp_w2_v)
    n_sel = S // SEL_LEN
    ks = k_s.reshape(B, n_sel, SEL_LEN, G, d).transpose(0, 3, 1, 2, 4)
    vs = v_s.reshape(B, n_sel, SEL_LEN, G, d).transpose(0, 3, 1, 2, 4)
    pad = ((0, 0), (WINDOW, 0), (0, 0), (0, 0))
    kw = jnp.pad(k_w, pad)
    vw = jnp.pad(v_w, pad)
    return (kc, vc, ks, vs, kw, vw)

def nsa_mixer(x, w_in, w_out, rel_bias, shared):
    B, S, _ = x.shape
    H, G, R, d = NSA_HEADS, NSA_GROUPS, NSA_REP, NSA_HEAD_DIM
    Q = Q_BLOCK
    kc, vc, ks, vs, kw, vw = shared
    proj = x @ w_in
    q = proj[..., :H * d].reshape(B, S, G, R, d)
    gate = jax.nn.sigmoid(proj[..., H * d:].astype(jnp.float32)).reshape(B, S, G, R, 3)
    n_cmp = kc.shape[1]
    n_sel = ks.shape[2]
    n_top = min(SEL_TOPK, n_sel)
    cmp_end = jnp.arange(n_cmp, dtype=jnp.int32) * CMP_STRIDE + CMP_LEN - 1
    ratio = SEL_LEN // CMP_STRIDE
    lead = CMP_LEN // CMP_STRIDE - 1
    span = ratio + lead
    sel_map = ratio * np.arange(n_sel)[:, None] - lead + np.arange(span)[None, :]
    sel_map = np.where((sel_map >= 0) & (sel_map < n_cmp), sel_map, n_cmp)
    bias_tab = rel_bias.astype(jnp.float32)
    bias_gr = bias_tab.reshape(REL_BUCKETS, G, R).transpose(1, 0, 2)
    scale = d ** -0.5
    gather_blocks = jax.vmap(jax.vmap(lambda kb, ib: kb[ib]))
    kc32 = kc.astype(jnp.float32)
    vc32 = vc.astype(jnp.float32)
    sel_ids = jnp.arange(n_sel, dtype=jnp.int32)
    blk_start = sel_ids * SEL_LEN
    win_off = jnp.arange(WINDOW + Q, dtype=jnp.int32)
    g_ids = jnp.arange(G)[None, :, None, None, None]

    def block(qb):
        start = qb * Q
        t = start + jnp.arange(Q, dtype=jnp.int32)
        qblk = lax.dynamic_slice_in_dim(q, start, Q, 1).astype(jnp.float32) * scale
        gg = lax.dynamic_slice_in_dim(gate, start, Q, 1)
        dist_c = t[:, None] - cmp_end[None, :]
        s = jnp.einsum('bqgrd,bngd->bgrqn', qblk, kc32)
        s = s + bias_tab[t5_bucket(dist_c)].reshape(Q, n_cmp, G, R).transpose(2, 3, 0, 1)
        p_c = masked_softmax(s, dist_c >= 0)
        o_c = jnp.einsum('bgrqn,bngd->bqgrd', p_c, vc32)
        imp_c = jnp.sum(p_c, axis=2)
        imp_c = jnp.concatenate([imp_c, jnp.zeros(imp_c.shape[:-1] + (1,), imp_c.dtype)], axis=-1)
        imp = jnp.sum(imp_c[..., sel_map], axis=-1)
        cur = t // SEL_LEN
        valid = blk_start[None, :] <= t[:, None]
        forced = ((sel_ids[None, :] == 0) | (sel_ids[None, :] == cur[:, None])
                  | (sel_ids[None, :] == cur[:, None] - 1))
        imp = jnp.where(forced, jnp.inf, jnp.where(valid, imp, -jnp.inf))
        _, sel_idx = lax.top_k(imp, n_top)
        k_sel = gather_blocks(ks, sel_idx).astype(jnp.float32)
        v_sel = gather_blocks(vs, sel_idx).astype(jnp.float32)
        pos = sel_idx[..., None] * SEL_LEN + jnp.arange(SEL_LEN, dtype=jnp.int32)
        dist_s = t[None, None, :, None, None] - pos
        s = jnp.einsum('bqgrd,bgqnld->bgrqnl', qblk, k_sel)
        s = s + jnp.moveaxis(bias_gr[g_ids, t5_bucket(dist_s)], -1, 2)
        s = s.reshape(B, G, R, Q, n_top * SEL_LEN)
        mask_s = (dist_s >= 0).reshape(B, G, 1, Q, n_top * SEL_LEN)
        p_s = masked_softmax(s, mask_s).reshape(B, G, R, Q, n_top, SEL_LEN)
        o_s = jnp.einsum('bgrqnl,bgqnld->bqgrd', p_s, v_sel)
        kwin = lax.dynamic_slice_in_dim(kw, start, WINDOW + Q, 1).astype(jnp.float32)
        vwin = lax.dynamic_slice_in_dim(vw, start, WINDOW + Q, 1).astype(jnp.float32)
        kpos = start - WINDOW + win_off
        dist_w = t[:, None] - kpos[None, :]
        s = jnp.einsum('bqgrd,bkgd->bgrqk', qblk, kwin)
        s = s + bias_tab[t5_bucket(dist_w)].reshape(Q, WINDOW + Q, G, R).transpose(2, 3, 0, 1)
        mask_w = (dist_w >= 0) & (dist_w < WINDOW) & (kpos[None, :] >= 0)
        p_w = masked_softmax(s, mask_w)
        o_w = jnp.einsum('bgrqk,bkgd->bqgrd', p_w, vwin)
        o = gg[..., 0:1] * o_c + gg[..., 1:2] * o_s + gg[..., 2:3] * o_w
        return o.reshape(B, Q, H * d)

    o = lax.map(block, jnp.arange(S // Q, dtype=jnp.int32))
    o = o.transpose(1, 0, 2, 3).reshape(B, S, H * d).astype(x.dtype)
    return o @ w_out

def first_inputs(seed: int = 0) -> dict:
    key = jax.random.key(seed)
    ks = jax.random.split(key, 24)
    f32 = jnp.float32

    def dense(k, shape, fan_in):
        return jax.random.normal(k, shape, f32) * (fan_in ** -0.5)

    def gain(k, shape):
        return 1.0 + 0.1 * jax.random.normal(k, shape, f32)

    d = NSA_HEAD_DIM
    return {
        "x": jax.random.normal(ks[0], (BATCH, SEQ, D_MODEL), f32),
        "mix_norm_pre": gain(ks[1], (DEPTH, D_MODEL)),
        "mix_norm_post": gain(ks[2], (DEPTH, D_MODEL)),
        "ffn_norm_pre": gain(ks[3], (DEPTH, D_MODEL)),
        "ffn_norm_post": gain(ks[4], (DEPTH, D_MODEL)),
        "ffn_w_in": dense(ks[5], (DEPTH, D_MODEL, 2 * FFN_HIDDEN), D_MODEL),
        "ffn_w_out": dense(ks[6], (DEPTH, FFN_HIDDEN, D_MODEL), FFN_HIDDEN),
        "ret_w_in": dense(ks[7], (N_A_LAYERS, D_MODEL, RET_IN), D_MODEL),
        "ret_w_out": dense(ks[8], (N_A_LAYERS, RET_HEADS * RET_V_DIM, D_MODEL), RET_HEADS * RET_V_DIM),
        "kv_norm": gain(ks[9], (D_MODEL,)),
        "kv_w": dense(ks[10], (D_MODEL, KV_SHARED_OUT), D_MODEL),
        "cmp_pe_k": 0.5 * jax.random.normal(ks[11], (CMP_LEN, d), f32),
        "cmp_w1_k": dense(ks[12], (CMP_LEN * d, CMP_HIDDEN), CMP_LEN * d),
        "cmp_w2_k": dense(ks[13], (CMP_HIDDEN, d), CMP_HIDDEN),
        "cmp_pe_v": 0.5 * jax.random.normal(ks[14], (CMP_LEN, d), f32),
        "cmp_w1_v": dense(ks[15], (CMP_LEN * d, CMP_HIDDEN), CMP_LEN * d),
        "cmp_w2_v": dense(ks[16], (CMP_HIDDEN, d), CMP_HIDDEN),
        "nsa_w_in": dense(ks[17], (N_B_LAYERS, D_MODEL, NSA_IN), D_MODEL),
        "nsa_w_out": dense(ks[18], (N_B_LAYERS, NSA_HEADS * d, D_MODEL), NSA_HEADS * d),
        "rel_bias": 0.5 * jax.random.normal(ks[19], (REL_BUCKETS, NSA_HEADS), f32),
    }

def first_block(x, mix_norm_pre, mix_norm_post, ffn_norm_pre, ffn_norm_post, ffn_w_in, ffn_w_out,
              ret_w_in, ret_w_out, kv_norm, kv_w, cmp_pe_k, cmp_w1_k, cmp_w2_k,
              cmp_pe_v, cmp_w1_v, cmp_w2_v, nsa_w_in, nsa_w_out, rel_bias):
    h = x
    shared = None
    for layer in range(DEPTH):
        if layer == N_A_LAYERS:
            shared = nsa_shared_kv(h, kv_norm, kv_w, cmp_pe_k, cmp_w1_k, cmp_w2_k,
                                   cmp_pe_v, cmp_w1_v, cmp_w2_v)
        normed = rms_norm(h, mix_norm_pre[layer])
        if layer < N_A_LAYERS:
            mixed = retention_mixer(normed, ret_w_in[layer], ret_w_out[layer])
        else:
            j = layer - N_A_LAYERS
            mixed = nsa_mixer(normed, nsa_w_in[j], nsa_w_out[j], rel_bias, shared)
        h = h + rms_norm(mixed, mix_norm_post[layer])
        normed = rms_norm(h, ffn_norm_pre[layer])
        h = h + rms_norm(swiglu_ffn(normed, ffn_w_in[layer], ffn_w_out[layer]), ffn_norm_post[layer])
    return h


DEPTH_2 = 1

CTX_LEN = 256
GRID_W = 64
EPS = 1e-6
CHUNK = 128
A_GROUPS = 8
A_WIDTH = 1024
A_GROUP_DIM = A_WIDTH // A_GROUPS
N_HEADS = 16
N_KV_HEADS = 4
HEAD_DIM = 64
B_WIDTH = N_HEADS * HEAD_DIM
KV_WIDTH = N_KV_HEADS * HEAD_DIM
WINDOW_2 = 128
BLOCK = 128
ROPE_BASE = 10000.0
N_EXPERTS = 16
CAPACITY_FACTOR = 2
D_EXPERT = 2048
OFF_U = 0
OFF_VA = OFF_U + A_WIDTH
OFF_Q = OFF_VA + A_WIDTH
OFF_K = OFF_Q + B_WIDTH
OFF_VB = OFF_K + KV_WIDTH
OFF_GATE = OFF_VB + KV_WIDTH
IN_COLS = OFF_GATE + 2 * D_MODEL


def rmsnorm(x, g):
    xf = x.astype(jnp.float32)
    y = xf * lax.rsqrt(jnp.mean(xf * xf, axis=-1, keepdims=True) + EPS)
    return (y * g.astype(jnp.float32)).astype(x.dtype)

def layernorm(x, g, b):
    xf = x.astype(jnp.float32)
    mu = jnp.mean(xf, axis=-1, keepdims=True)
    var = jnp.mean(jnp.square(xf - mu), axis=-1, keepdims=True)
    y = (xf - mu) * lax.rsqrt(var + EPS)
    return (y * g.astype(jnp.float32) + b.astype(jnp.float32)).astype(x.dtype)

def modulate(h, shift, scale):
    return h * (1 + scale) + shift

def _axis_angles(pos, dim):
    freqs = ROPE_BASE ** (-jnp.arange(0, dim, 2, dtype=jnp.float32) / dim)
    return pos.astype(jnp.float32)[:, None] * freqs[None, :]

def _rotate(x, ang):
    x1, x2 = jnp.split(x.astype(jnp.float32), 2, axis=-1)
    cos = jnp.cos(ang)[None, :, None, :]
    sin = jnp.sin(ang)[None, :, None, :]
    return jnp.concatenate([x1 * cos - x2 * sin, x1 * sin + x2 * cos], axis=-1)

def rope_2d(x, row, col):
    half = x.shape[-1] // 2
    xr, xc = x[..., :half], x[..., half:]
    out = jnp.concatenate([_rotate(xr, _axis_angles(row, half)),
                           _rotate(xc, _axis_angles(col, half))], axis=-1)
    return out.astype(x.dtype)

def chunk_gmlp(u, v, ln_g, ln_b, w_s, b_s):
    Bn, L, _ = v.shape
    v = layernorm(v, ln_g, ln_b)
    vc = v.reshape(Bn, L // CHUNK, CHUNK, A_GROUPS, A_GROUP_DIM)
    mixed = jnp.einsum('gpq,bnqgd->bnpgd', w_s, vc) + b_s.T[None, None, :, :, None]
    return u * mixed.reshape(Bn, L, A_WIDTH)

def window_gqa(q, k, v, k_ctx, v_ctx, sink):
    Bn, L, H, Dh = q.shape
    nb = L // BLOCK
    rep = H // N_KV_HEADS
    scale = HEAD_DIM ** -0.5
    qb = q.reshape(Bn, nb, BLOCK, N_KV_HEADS, rep, Dh)

    def band(t):
        tb = t.reshape(Bn, nb, BLOCK, N_KV_HEADS, Dh)
        tp = jnp.pad(tb, ((0, 0), (1, 1), (0, 0), (0, 0), (0, 0)))
        return jnp.concatenate([tp[:, :-2], tp[:, 1:-1], tp[:, 2:]], axis=2)

    kb, vb = band(k), band(v)
    a_idx = jnp.arange(BLOCK)[:, None]
    s_idx = jnp.arange(3 * BLOCK)[None, :]
    rel = s_idx - BLOCK - a_idx
    sink_l = sink.astype(jnp.float32).reshape(N_KV_HEADS, rep)[None, :, :, None, None]
    vals_ctx = v_ctx.astype(jnp.float32)

    def one_block(args):
        n, qn, kn, vn = args
        key_pos = (n - 1) * BLOCK + s_idx
        mask = (jnp.abs(rel) <= WINDOW_2) & (key_pos >= 0) & (key_pos < L)
        s_loc = jnp.einsum('bqkrd,bskd->bkrqs', qn, kn, preferred_element_type=jnp.float32) * scale
        s_loc = jnp.where(mask, s_loc, jnp.float32(-1e30))
        s_ctx = jnp.einsum('bqkrd,bskd->bkrqs', qn, k_ctx, preferred_element_type=jnp.float32) * scale
        logits = jnp.concatenate([s_loc, s_ctx], axis=-1)
        m = jnp.maximum(jnp.max(logits, axis=-1, keepdims=True), sink_l)
        p = jnp.exp(logits - m)
        denom = jnp.sum(p, axis=-1, keepdims=True) + jnp.exp(sink_l - m)
        vals = jnp.concatenate([vn.astype(jnp.float32), vals_ctx], axis=1)
        out = jnp.einsum('bkrqs,bskd->bqkrd', p / denom, vals)
        return out.astype(q.dtype)

    xs = (jnp.arange(nb), jnp.moveaxis(qb, 1, 0), jnp.moveaxis(kb, 1, 0), jnp.moveaxis(vb, 1, 0))
    out = lax.map(one_block, xs)
    return jnp.moveaxis(out, 0, 1).reshape(Bn, L, H * Dh)

def expert_choice_ffn(h, w_router, w_gate, w_up, w_down):
    Bn, N, D = h.shape
    cap = max(1, CAPACITY_FACTOR * N // N_EXPERTS)
    logits = jnp.einsum('bnd,de->bne', h, w_router, preferred_element_type=jnp.float32)
    aff = jax.nn.softmax(logits, axis=-1)
    top_w, top_idx = lax.top_k(jnp.swapaxes(aff, 1, 2), cap)
    xe = jax.vmap(lambda hb, ib: hb[ib])(h, top_idx)
    g = jnp.einsum('becd,edf->becf', xe, w_gate)
    u = jnp.einsum('becd,edf->becf', xe, w_up)
    y = jnp.einsum('becf,efd->becd', jax.nn.silu(g) * u, w_down)
    y = y * top_w[..., None].astype(y.dtype)
    return jax.vmap(lambda ib, yb: jnp.zeros((N, D), yb.dtype).at[ib.reshape(-1)].add(yb.reshape(-1, D)))(top_idx, y)

def second_inputs(seed: int = 0) -> dict:
    key = jax.random.key(seed)
    ks = jax.random.split(key, 24)
    f32 = jnp.float32
    D = D_MODEL

    def nrm(k, shape, s):
        return jax.random.normal(k, shape, f32) * s

    return {
        "x": nrm(ks[0], (BATCH, SEQ, D), 1.0),
        "c": nrm(ks[1], (BATCH, D), 1.0),
        "ctx": nrm(ks[2], (BATCH, CTX_LEN, D), 1.0),
        "c_ctx": nrm(ks[3], (D,), 1.0),
        "w_ada": nrm(ks[4], (DEPTH_2, D, 6 * D), 0.3 * D ** -0.5),
        "b_ada": nrm(ks[5], (DEPTH_2, 6 * D), 0.02),
        "norm1_g": 1.0 + nrm(ks[6], (DEPTH_2, D), 0.05),
        "w_in": nrm(ks[7], (DEPTH_2, D, IN_COLS), D ** -0.5),
        "b_merge_gate": nrm(ks[8], (DEPTH_2, 2 * D), 0.02),
        "gmlp_ln_g": 1.0 + nrm(ks[9], (DEPTH_2, A_WIDTH), 0.05),
        "gmlp_ln_b": nrm(ks[10], (DEPTH_2, A_WIDTH), 0.02),
        "w_spatial": nrm(ks[11], (DEPTH_2, A_GROUPS, CHUNK, CHUNK), CHUNK ** -0.5),
        "b_spatial": nrm(ks[12], (DEPTH_2, A_GROUPS, CHUNK), 0.02),
        "attn_sink": nrm(ks[13], (DEPTH_2, N_HEADS), 0.5),
        "w_proj_a": nrm(ks[14], (DEPTH_2, A_WIDTH, D), A_WIDTH ** -0.5),
        "w_proj_b": nrm(ks[15], (DEPTH_2, B_WIDTH, D), B_WIDTH ** -0.5),
        "w_out": nrm(ks[16], (DEPTH_2, D, D), D ** -0.5),
        "norm2_g": 1.0 + nrm(ks[17], (DEPTH_2, D), 0.05),
        "w_router": nrm(ks[18], (DEPTH_2, D, N_EXPERTS), D ** -0.5),
        "w_exp_gate": nrm(ks[19], (DEPTH_2, N_EXPERTS, D, D_EXPERT), D ** -0.5),
        "w_exp_up": nrm(ks[20], (DEPTH_2, N_EXPERTS, D, D_EXPERT), D ** -0.5),
        "w_exp_down": nrm(ks[21], (DEPTH_2, N_EXPERTS, D_EXPERT, D), D_EXPERT ** -0.5),
        "final_g": 1.0 + nrm(ks[22], (D,), 0.05),
    }

def second_block(x, c, ctx, c_ctx, w_ada, b_ada, norm1_g, w_in, b_merge_gate, gmlp_ln_g, gmlp_ln_b,
              w_spatial, b_spatial, attn_sink, w_proj_a, w_proj_b, w_out, norm2_g, w_router,
              w_exp_gate, w_exp_up, w_exp_down, final_g):
    Bn, L, D = x.shape
    rows = L // GRID_W
    row = jnp.repeat(jnp.arange(rows), GRID_W)
    col = jnp.tile(jnp.arange(GRID_W), rows)

    for l in range(DEPTH_2):
        mod = jax.nn.silu(c) @ w_ada[l] + b_ada[l]
        sh1, sc1, g1, sh2, sc2, g2 = jnp.split(mod[:, None, :], 6, axis=-1)
        mod_ctx = jax.nn.silu(c_ctx) @ w_ada[l] + b_ada[l]
        csh1, csc1 = mod_ctx[:D], mod_ctx[D:2 * D]

        h = modulate(rmsnorm(x, norm1_g[l]), sh1, sc1)
        proj = h @ w_in[l]
        u_a, v_a, q, k, v, gates = jnp.split(proj, [OFF_VA, OFF_Q, OFF_K, OFF_VB, OFF_GATE], axis=-1)

        hc = modulate(rmsnorm(ctx, norm1_g[l]), csh1, csc1)
        kv_ctx = hc @ w_in[l][:, OFF_K:OFF_GATE]
        k_ctx, v_ctx = jnp.split(kv_ctx.reshape(Bn, -1, 2 * N_KV_HEADS, HEAD_DIM), 2, axis=2)

        y_a = chunk_gmlp(jax.nn.gelu(u_a), jax.nn.gelu(v_a), gmlp_ln_g[l], gmlp_ln_b[l],
                         w_spatial[l], b_spatial[l])

        qh = rope_2d(q.reshape(Bn, L, N_HEADS, HEAD_DIM), row, col)
        kh = rope_2d(k.reshape(Bn, L, N_KV_HEADS, HEAD_DIM), row, col)
        vh = v.reshape(Bn, L, N_KV_HEADS, HEAD_DIM)
        y_b = window_gqa(qh, kh, vh, k_ctx, v_ctx, attn_sink[l])

        g_a, g_b = jnp.split(jax.nn.sigmoid(gates + b_merge_gate[l]), 2, axis=-1)
        merged = g_a * (y_a @ w_proj_a[l]) + g_b * (y_b @ w_proj_b[l])
        x = x + g1 * (merged @ w_out[l])

        h2 = modulate(rmsnorm(x, norm2_g[l]), sh2, sc2)
        x = x + g2 * expert_choice_ffn(h2, w_router[l], w_exp_gate[l], w_exp_up[l], w_exp_down[l])

    return rmsnorm(x, final_g)


def setup_inputs(seed=0):
    out = dict(first_inputs(seed))
    for name, value in second_inputs(seed + 1).items():
        if name != "x":
            out[name + "_2"] = value
    return out


def reference(
    x, mix_norm_pre, mix_norm_post, ffn_norm_pre, ffn_norm_post, ffn_w_in, ffn_w_out, ret_w_in,
    ret_w_out, kv_norm, kv_w, cmp_pe_k, cmp_w1_k, cmp_w2_k, cmp_pe_v, cmp_w1_v, cmp_w2_v,
    nsa_w_in, nsa_w_out, rel_bias, c_2, ctx_2, c_ctx_2, w_ada_2, b_ada_2, norm1_g_2, w_in_2,
    b_merge_gate_2, gmlp_ln_g_2, gmlp_ln_b_2, w_spatial_2, b_spatial_2, attn_sink_2, w_proj_a_2,
    w_proj_b_2, w_out_2, norm2_g_2, w_router_2, w_exp_gate_2, w_exp_up_2, w_exp_down_2,
    final_g_2,
):
    x = first_block(
        x, mix_norm_pre, mix_norm_post, ffn_norm_pre, ffn_norm_post, ffn_w_in, ffn_w_out,
        ret_w_in, ret_w_out, kv_norm, kv_w, cmp_pe_k, cmp_w1_k, cmp_w2_k, cmp_pe_v, cmp_w1_v,
        cmp_w2_v, nsa_w_in, nsa_w_out, rel_bias,
    )
    return second_block(
        x, c_2, ctx_2, c_ctx_2, w_ada_2, b_ada_2, norm1_g_2, w_in_2, b_merge_gate_2,
        gmlp_ln_g_2, gmlp_ln_b_2, w_spatial_2, b_spatial_2, attn_sink_2, w_proj_a_2, w_proj_b_2,
        w_out_2, norm2_g_2, w_router_2, w_exp_gate_2, w_exp_up_2, w_exp_down_2, final_g_2,
    )


_drawn_inputs = setup_inputs


def setup_inputs(seed=0):
    import zlib

    import numpy as np

    out = dict(_drawn_inputs(seed))
    spreads = {}
    factors = {'ctx_2': 8.0,
     'c_ctx_2': 8.0,
     'b_ada_2': 8.0,
     'norm1_g_2': 8.0,
     'b_merge_gate_2': 8.0,
     'gmlp_ln_g_2': 8.0,
     'gmlp_ln_b_2': 8.0,
     'b_spatial_2': 8.0,
     'attn_sink_2': 8.0,
     'w_proj_b_2': 5.398,
     'norm2_g_2': 8.0,
     'w_router_2': 3.566,
     'w_exp_gate_2': 3.777,
     'w_exp_up_2': 3.515,
     'w_exp_down_2': 3.51}
    for name, (base, spread) in spreads.items():
        noise = np.random.default_rng([zlib.crc32(name.encode()), seed]).standard_normal(out[name].shape)
        drawn = base * np.exp(spread * noise) if base else spread * noise
        out[name] = __import__('jax').numpy.asarray(drawn.astype(out[name].dtype))
    for name, factor in factors.items():
        out[name] = (out[name] * factor).astype(out[name].dtype)
    return out
```

```python
from contextlib import ExitStack

import numpy as np

import concourse.bass as bass
from concourse import mybir

F32 = mybir.dt.float32
ALU = mybir.AluOpType
ACT = mybir.ActivationFunctionType
AX_X = mybir.AxisListType.X

P = 128
D = 1024
T = 256
DC = D // P
EPS = 1e-6

RET_HEADS = 4
RET_QK = D // RET_HEADS
RET_V = 2 * D // RET_HEADS
HID = ((8 * D + 3 * 256 - 1) // (3 * 256)) * 256
PAIRS = HID // 256

HEADS = 16
GROUPS = 4
HD = 64
CMP_LEN, CMP_STRIDE = 32, 16
N_CMP = (T - CMP_LEN) // CMP_STRIDE + 1
BUCKETS, MAX_DIST = 32, 128
NEG = -1e30
LEAST = 1e20
TINY = float(np.finfo(np.float32).tiny)

A_GROUPS = 8
EXPERTS = 16
CAP = 2 * T // EXPERTS
DE = 2048
WINDOW = 128
GRID_W = 64
IN2 = 5632

UNIT = 2048
RING = 6
EUNIT = 4096
ERING = 3
E_UNITS = 12

U_RET = 0
U_RO = U_RET + 48
U_F0 = U_RO + 8
U_KV = U_F0 + 3 * PAIRS
U_W1 = U_KV + 6
U_NQ = U_W1 + 4
U_NO = U_NQ + 4
U_F1 = U_NO + 4
U_IN2 = U_F1 + 3 * PAIRS
U_PA = U_IN2 + IN2 // 256
U_PB = U_PA + 4
U_WO = U_PB + 4
U_END = U_WO + 4

COLS = {}
_at = 0
for _name, _n in [("mix_pre0", 8), ("mix_pre1", 8), ("mix_post0", 8), ("mix_post1", 8), ("ffn_pre0", 8),
                  ("ffn_pre1", 8), ("ffn_post0", 8), ("ffn_post1", 8), ("kv_norm", 8), ("norm1", 8),
                  ("norm2", 8), ("final", 8), ("b_ada", 48), ("b_merge", 16), ("c", 8), ("c_ctx", 8),
                  ("pe_k", 16), ("pe_v", 16)]:
    COLS[_name] = (_at, _n)
    _at += _n
N_COLS = _at

TABS = {}
_at = 0
for _name, _n in [("ident", 128), ("perm", 128), ("tri", 128), ("slot", 32), ("ret_cos", T), ("ret_sin", T),
                  ("ret_nsin", T), ("rope_cos", T), ("rope_sin", T), ("band", 2 * T)]:
    TABS[_name] = (_at, _n)
    _at += _n
N_TABS = _at
N_DECAY = RET_HEADS * 384

(N_PRE0, N_POST0, N_PREF0, N_POSTF0, N_PRE1, N_POST1, N_PREF1, N_POSTF1, N_CTX, N_IN2, N_MOE, N_END) = range(12)
XN = {N_PRE0: 0, N_PREF0: 8, N_PRE1: 16, N_PREF1: 32, N_CTX: 40, N_IN2: 48, N_MOE: 56, N_END: 64}
XN_END = 72
POST = {N_POST0: 0, N_POSTF0: 8, N_POST1: 16, N_POSTF1: 24}
MODP = {N_CTX: 0, N_IN2: 8, N_MOE: 16}

FIRST_IN, REST_IN = 5 * 16, 6 * 16
LN_END = 6
R_AFF, R_MASK, R_MASKT, R_ZERO = 4, 6 + 2 * (CAP // 8), 7 + 2 * (CAP // 8), 10 + 2 * (CAP // 8)
IN2_ORDER = [4, 5, 6, 7, 0, 1, 2, 3] + list(range(8, 22))


def program(nc, a, out):
    ctx = ExitStack()
    with ctx:
        def sb(name, shape):
            return ctx.enter_context(nc.sbuf_tensor(name, shape, F32))

        def sem(name):
            return ctx.enter_context(nc.semaphore(name))

        ring = sb("dense_ring", [P, RING, UNIT])
        ering = sb("expert_ring", [P, ERING, EUNIT])
        h = sb("residual", [P, DC, T])
        xn = sb("normed", [P, DC, T])
        sq = sb("squares", [P, DC, T])
        cols = sb("cols", [P, N_COLS])
        tabs = sb("tabs", [P, N_TABS])
        ones = sb("ones", [P, P])
        cs = sb("cond_silu", [P, DC, 32])
        root = sb("root", [P, T])
        rs = sb("inv_root", [P, T])
        ada_rows = sb("ada_rows", [P, 512])
        mod = sb("mod", [P, 2, 48])
        gain = sb("mod_gain", [P, 3, DC])
        w_gate = sb("nsa_gate_w", [P, DC, 48])
        w2k = sb("cmp_w2_k2", [P, 2, 2, HD])
        w2v = sb("cmp_w2_v", [P, 2, HD])
        w_router = sb("router_w", [P, DC, EXPERTS])
        rel = sb("rel_ext", [33, HEADS])
        bucket_rows = sb("bucket_rows", [33, 384])
        bias_rows = sb("bias_rows", [HEADS, 384])
        cbias = sb("cmp_bias", [P, HEADS, 2, N_CMP])
        gates = sb("nsa_gates", [P, 2, 48])
        sink = sb("sink", [P, HEADS])
        kc = sb("cmp_keys", [P, GROUPS, N_CMP])
        vc = sb("cmp_values", [N_CMP, GROUPS, HD])
        st = sb("softmax_stats", [P, 2, 32])
        ARENA = 62 * 256
        arena = sb("arena", [P, ARENA])
        ps = ctx.enter_context(nc.psum_tensor("ps", [P, 8, 512], F32))
        bias_dram = nc.dram_tensor("bias_skew", (HEADS, P, 384), F32).ap()

        def at(kb, *dims):
            n = int(np.prod(dims))
            o = int(kb * 256)
            assert o + n <= ARENA, (kb, dims)
            v = arena[:, o:o + n]
            if len(dims) == 1:
                return v
            names = "abcd"[:len(dims)]
            return v.rearrange(f"p ({' '.join(names)}) -> p {' '.join(names)}", **dict(zip(names, dims)))

        def col(name, k=None):
            o, n = COLS[name]
            return cols[:, o:o + n] if k is None else cols[:, o + k:o + k + 1]

        def tab(name):
            o, n = TABS[name]
            return tabs[:, o:o + n]

        ident = tab("ident")

        q_r = at(0, RET_HEADS, 2, T)
        k_r = at(8, RET_HEADS, 2, T)
        v_r = at(16, 2, RET_HEADS * RET_V)
        o_r = at(32, 16, T)
        bucket_cmp = at(32, 30 * P)
        rot = at(48, 2, 2, 512)
        sT = at(48, 2, 384)
        gs = at(52, 2, 512)
        decay = at(56, RET_HEADS, 384)
        f_silu = at(0, 2, 512)
        f_hid = at(4, 2, 512)
        bias = at(8, HEADS, T)
        kv_raw = at(24, 4, 2, T)
        o_n = at(24, DC, T)
        shifted = at(32, 2, GROUPS, T)
        blocks = at(40, 2, 16, GROUPS * N_CMP)
        kd = at(48, 2, GROUPS, T)
        v_n = at(56, 2, 2, T)
        q_n = at(0, DC, T)
        cmp_hid = at(60, 512)
        n_s = at(32, 2, 800)
        n_pT = at(38.5, 2, 2, 384)
        n_pc = at(44.5, 2, T)
        hidT = ada_rows
        ctxn = at(0, DC, T)
        o_w = at(0, DC, T)
        va = at(8, 2, D)
        ln_g = at(16, D)
        ln_b = at(20, D)
        ga = at(8, DC, T)
        gb = at(16, DC, T)
        ws = at(24, A_GROUPS, P)
        bs = at(28, A_GROUPS, P)
        w_s = at(24, 2, 2, 512)
        ya = at(32, DC, T)
        q_w = at(40, DC, T)
        kd2 = at(48, GROUPS, 2, T)
        kw_raw = at(56, 2, 512)
        rot2 = at(60, 512)
        h2 = at(0, 2, D)
        pick = at(8, 2, EXPERTS * CAP)
        wpick = at(12, 2, EXPERTS * CAP)
        xe = at(16, DC, EXPERTS * CAP)
        xcur = at(32, DC, CAP)
        pcur = at(33, 2, 4, CAP)
        e_silu = at(34, 512)
        e_hid = at(36, 512)
        e_hidT = at(38, 512)
        e_y = at(40, 512)
        e_pT = at(42, T)
        aff = at(43, 2, EXPERTS)
        e_small = at(44, 2, 64)
        rank_work = at(45, 2, T)
        vw_tok = sb("window_values", [P, 4, T])

        landed = [sem(f"dense_landed{i}") for i in range(RING)]
        used = sem("dense_used")
        e_landed = [sem(f"expert_landed{i}") for i in range(ERING)]
        e_used = sem("expert_used")
        x_in = sem("x_in")
        first_in = sem("first_in")
        rest_in = sem("rest_in")
        decay_in = sem("decay_in")
        bias_out = sem("bias_out")
        bias_in = sem("bias_in")
        ones_set = sem("ones_set")
        cs_set = sem("cs_set")
        rel_set = sem("rel_set")
        brow_mm = sem("brow_mm")
        brow_ev = sem("brow_ev")
        cbias_ev = sem("cbias_ev")
        sq_ready = sem("sq_ready")
        ss_ready = sem("ss_ready")
        root_ready = sem("root_ready")
        rs_ready = sem("rs_ready")
        xn_ready = sem("xn_ready")
        scaled = sem("post_scaled")
        h_ready = sem("h_ready")
        ada_ev = sem("ada_ev")
        ada_tr = sem("ada_tr")
        ada_mod = sem("ada_mod")
        gains_set = sem("gains_set")
        qk_rot = sem("qk_rot")
        qk_done = sem("qk_done")
        v_mm = sem("v_mm")
        v_ev = sem("v_ev")
        g_mm = sem("g_mm")
        g_ev = sem("g_ev")
        og_done = sem("og_done")
        sc_mm = sem("sc_mm")
        sc_ev = sem("sc_ev")
        o_mm = sem("o_mm")
        osq = sem("osq")
        oss = sem("oss")
        oroot = sem("oroot")
        ors = sem("ors")
        on_ev = sem("on_ev")
        f_act = sem("f_act")
        f_hidden = sem("f_hidden")
        kv_ev = sem("kv_ev")
        shift_in = sem("shift_in")
        kd_in = sem("kd_in")
        blocks_set = sem("blocks_set")
        c_mm = sem("c_mm")
        c_act = sem("c_act")
        c_tr = sem("c_tr")
        c_trev = sem("c_trev")
        c_kv = sem("c_kv")
        c_kvev = sem("c_kvev")
        nq_mm = sem("nq_mm")
        nq_ev = sem("nq_ev")
        s_mm = sem("s_mm")
        s_add = sem("s_add")
        s_max = sem("s_max")
        s_neg = sem("s_neg")
        s_exp = sem("s_exp")
        s_sum = sem("s_sum")
        s_inv = sem("s_inv")
        s_fac = sem("s_fac")
        s_p = sem("s_p")
        s_tr = sem("s_tr")
        s_trev = sem("s_trev")
        s_trev2 = sem("s_trev2")
        s_pv = sem("s_pv")
        s_ov = sem("s_ov")
        ctx_in = sem("ctx_in")
        mod_scaled = sem("mod_scaled")
        w_sum = sem("w_sum")
        ln_root = sem("ln_root")
        ln_in = sem("ln_in")
        va_ev = sem("va_ev")
        ln_seq = sem("ln_seq")
        ua_ev = sem("ua_ev")
        sp_mm = sem("sp_mm")
        sp_add = sem("sp_add")
        ya_done = sem("ya_done")
        qw_ev = sem("qw_ev")
        kw_mm = sem("kw_mm")
        qp_mm = sem("qp_mm")
        q_cos = sem("q_cos")
        q_sin = sem("q_sin")
        q_rot = sem("q_rot")
        vw_mm = sem("vw_mm")
        vw_ev = sem("vw_ev")
        kd2_in = sem("kd2_in")
        gt_ev = sem("gt_ev")
        pab_ev = sem("pab_ev")
        merged = sem("merged")
        x2_done = sem("x2_done")
        tok_mm = sem("tok_mm")
        tok_ev = sem("tok_ev")
        lg_mm = sem("lg_mm")
        r_seq = sem("router_seq")
        r_exp = sem("router_exp")
        r_tr = sem("router_tr")
        r_pos = sem("router_pos")
        pick_set = sem("pick_set")
        xe_mm = sem("xe_mm")
        xe_ev = sem("xe_ev")
        cur_set = sem("cur_set")
        e_act = sem("e_act")
        e_hset = sem("e_hset")
        ep_tr = sem("ep_tr")
        ep_ev = sem("ep_ev")
        eh_tr = sem("eh_tr")
        eh_ev = sem("eh_ev")
        ed_ev = sem("ed_ev")
        moe_mm = sem("moe_mm")
        moe_done = sem("moe_done")
        out_done = sem("out_done")

        block = ctx.enter_context(nc.Block())

        def col_src(w, n0):
            return w.rearrange("(k p) n -> p k n", p=P)[:, :, n0:n0 + 256] if isinstance(n0, int) else \
                w.rearrange("(k p) n -> p k n", p=P)[:, :, bass.ds(n0, 256)]

        def row_src(w, u):
            v = w.rearrange("(c p) n -> p c n", p=P)
            return v[:, 2 * u:2 * u + 2, :] if isinstance(u, int) else v[:, bass.ds(u * 2, 2), :]

        def slot8(U):
            return ring[:, U % RING, :].rearrange("p (k n) -> p k n", k=8)

        def slot2(U):
            return ring[:, U % RING, :].rearrange("p (c n) -> p c n", c=2)

        @block.sync
        def _(sp):
            def load(U, src, k, round_=0):
                dst = slot8(U) if k == 8 else slot2(U) if k == 2 else ring[:, U % RING, :]
                if U >= RING:
                    sp.wait_ge(used, U - RING + 1 + round_ * 6)
                sp.dma_start(dst, src).then_inc(landed[U % RING], 16)

            w_in = a["ret_w_in"]
            order = [c for hd in range(4) for c in (hd, 4 + hd)] + list(range(8, 24))
            ada_v = a["w_ada_2"].rearrange("(k p) n -> p k n", p=P)

            def load_expert(e, w):
                u = w % 4
                if w < 8:
                    src = a["w_exp_gate_2" if w < 4 else "w_exp_up_2"][e].rearrange("(c p) n -> p c n", p=P)
                    src = src[:, 2 * u:2 * u + 2, :]
                    dst = ering[:, w % ERING, :].rearrange("p (c n) -> p c n", c=2)
                else:
                    src = a["w_exp_down_2"][e].rearrange("(c p) n -> p c n", p=P)[:, 4 * u:4 * u + 4, :]
                    dst = ering[:, w % ERING, :].rearrange("p (c n) -> p c n", c=4)
                sp.dma_start(dst, src).then_inc(e_landed[w % ERING], 16)

            for u in range(24):
                load(2 * u, col_src(w_in, 256 * order[u]), 8)
                load(2 * u + 1, ada_v[:, u % 8, 2048 * (u // 8):2048 * (u // 8) + 2048], 0)
                if u == 12:
                    for w in range(ERING):
                        load_expert(0, w)
            for u in range(8):
                load(U_RO + u, row_src(a["ret_w_out"], u), 2)

            def ffn(f, U0):
                w1, w2 = a[f"ffn_w_in{f}"], a[f"ffn_w_out{f}"]

                def gu(U, j, r=0):
                    load(U, col_src(w1, j * 256), 8, r)
                    load(U + 1, col_src(w1, j * 256 + HID), 8, r)

                gu(U0, 0)
                gu(U0 + 2, 1)
                load(U0 + 4, row_src(w2, 0), 2)
                with sp.Fori(0, (PAIRS - 3) // 2) as i:
                    for c in range(2):
                        gu(U0 + 5 + 3 * c, i * 2 + (2 + c), i)
                        load(U0 + 7 + 3 * c, row_src(w2, i * 2 + (1 + c)), 2, i)
                gu(U0 + 29, 10)
                load(U0 + 31, row_src(w2, 9), 2)
                load(U0 + 32, row_src(w2, 10), 2)

            ffn(0, U_F0)
            for u, c in enumerate((0, 1, 2, 4, 3, 5)):
                load(U_KV + u, col_src(a["kv_w"], 256 * c), 8)
            for kind, w in enumerate(("cmp_w1_k", "cmp_w1_v")):
                v = a[w].rearrange("(c p) n -> p c n", p=P)
                for u in range(2):
                    load(U_W1 + 2 * kind + u, v[:, 8 * u:8 * u + 8, :], 8)
            for u in range(4):
                load(U_NQ + u, col_src(a["nsa_w_in"], 256 * u), 8)
            for u in range(4):
                load(U_NO + u, row_src(a["nsa_w_out"], u), 2)
            ffn(1, U_F1)
            for u, c in enumerate(IN2_ORDER):
                load(U_IN2 + u, col_src(a["w_in_2"], 256 * c), 8)
            for U0, w in ((U_PA, "w_proj_a_2"), (U_PB, "w_proj_b_2"), (U_WO, "w_out_2")):
                for u in range(4):
                    load(U0 + u, row_src(a[w], u), 2)
            for w in range(ERING, E_UNITS):
                sp.wait_ge(e_used, w - ERING + 1)
                load_expert(0, w)
            with sp.Fori(1, EXPERTS) as e:
                for w in range(E_UNITS):
                    sp.wait_ge(e_used, e * E_UNITS + (w - ERING + 1))
                    load_expert(e, w)
            sp.wait_ge(xn_ready, XN_END)
            sp.dma_start(out.rearrange("(k p) t -> p k t", p=P), xn[:]).then_inc(out_done, 16)
            sp.wait_ge(out_done, 16)

        def taken(eng, U, r=0):
            eng.wait_ge(used, r * 6 + (U + 1) if not isinstance(r, int) else U + 1)

        def w_pT(hd):
            return sq[:, 4 * (hd % 2):4 * (hd % 2) + 4, :]

        zeros_row = e_y

        def gate_unit(f, j):
            U0 = (U_F0, U_F1)[f]
            return U0 + (2 * j if j < 2 else 3 * j - 1)

        def out_unit(f, j):
            U0 = (U_F0, U_F1)[f]
            return U0 + (3 * j + 4 if j < PAIRS - 1 else 3 * PAIRS - 1)

        def head_parts(hd):
            return slice(64 * (hd % 2), 64 * (hd % 2) + 64), hd // 2, hd // (HEADS // GROUPS)

        @block.tensor
        def _(pe):
            def take(U, r=0):
                pe.wait_ge(landed[U % RING], r * 16 + 16 * (U // RING + 1))

            def norm(n):
                for q in range(4):
                    pe.wait_ge(sq_ready, 4 * n + q + 1)
                    for c in (2 * q, 2 * q + 1):
                        mm = pe.matmul(ps[:, 4, 0:T], ones[:], sq[:, c, :], start=c == 0, stop=c == 7)
                mm.then_inc(ss_ready, 1)

            def col_T(U, x, bank, r=0, x_ready=None):
                take(U, r)
                w = slot8(U)
                for b in range(2):
                    for k in range(8):
                        if x_ready is not None and b == 0:
                            pe.wait_ge(xn_ready, x_ready + k + 1)
                        mm = pe.matmul(ps[:, bank, b * T:b * T + T], w[:, k, b * P:b * P + P], x[:, k, :],
                                       start=k == 0, stop=k == 7)
                mm.then_inc(used, 1)

            def col_tok(U, x, bank, x_ready=None):
                take(U)
                w = slot8(U)
                for t in range(2):
                    for k in range(8):
                        if x_ready is not None and t == 0:
                            pe.wait_ge(xn_ready, x_ready + k + 1)
                        mm = pe.matmul(ps[:, bank, t * T:t * T + T], x[:, k, t * P:t * P + P], w[:, k, :],
                                       start=k == 0, stop=k == 7)
                mm.then_inc(used, 1)

            def row_T(U, x, bank0, first, last, r=0):
                take(U, r)
                w = slot2(U)
                for b in range(8):
                    for c in range(2):
                        mm = pe.matmul(ps[:, bank0 + b // 2, (b % 2) * T:(b % 2) * T + T],
                                       w[:, c, b * P:b * P + P], x[:, c, :],
                                       start=first and c == 0 and b % 2 == 0, stop=last and c == 1,
                                       skip_group_check=True)
                return mm

            pe.wait_ge(first_in, FIRST_IN)
            pe.wait_ge(rel_set, 1)
            pe.matmul(ps[0:HEADS, 5, 0:384], rel[:], bucket_rows[:], start=True, stop=True).then_inc(brow_mm, 1)
            for i in range(30):
                mm = pe.matmul(ps[:, 7, i * HEADS:(i + 1) * HEADS], bucket_cmp[0:33, i * P:(i + 1) * P], rel[:],
                               start=True, stop=True)
            mm.then_inc(brow_mm, 1)
            pe.wait_ge(ones_set, 1)
            norm(N_PRE0)
            pe.wait_ge(brow_ev, 1)
            pe.wait_ge(cbias_ev, 1)
            pe.wait_ge(cs_set, 2)

            def ada(u):
                U = U_RET + 2 * u + 1
                take(U)
                k = u % 8
                if u >= 8 and k == 0:
                    pe.wait_ge(ada_mod, u // 8)
                for j in range(4):
                    mm = pe.matmul(ps[32 * j:32 * j + 32, 6, :], cs[:, k, :], ring[:, U % RING, 512 * j:512 * j + 512],
                                   start=k == 0, stop=k == 7)
                mm.then_inc(used, 1)

            def ada_turn(r):
                pe.wait_ge(ada_ev, r + 1)
                for m in range(4):
                    mm = pe.transpose(ps[:, 6, m * P:m * P + P], ada_rows[:, m * P:m * P + P], ident)
                mm.then_inc(ada_tr, 1)

            for u in range(8):
                U = U_RET + 2 * u
                take(U)
                if u >= 2:
                    pe.wait_ge(qk_rot, u - 1)
                for b in range(2):
                    for k in range(8):
                        if u == 0 and b == 0:
                            pe.wait_ge(xn_ready, k + 1)
                        mm = pe.matmul(ps[:, 5 + 2 * (u % 2), b * T:b * T + T], slot8(U)[:, k, b::2], xn[:, k, :],
                                       start=k == 0, stop=k == 7)
                mm.then_inc(used, 1)
                ada(u)
            for u in range(8):
                pe.wait_ge(*((v_ev, u - 1) if u >= 2 else (qk_rot, 7 + u)))
                col_tok(U_RET + 16 + 2 * u, xn, 5 + 2 * (u % 2))
                if u == 0:
                    ada_turn(0)
                ada(8 + u)

            def g_unit(u):
                pe.wait_ge(*((g_ev, u - 1) if u >= 2 else (v_ev, 7 + u)))
                col_T(U_RET + 32 + 2 * u, xn, 5 + 2 * (u % 2))
                if u == 0:
                    ada_turn(1)
                ada(16 + u)

            def scores(hd):
                pe.wait_ge(qk_done, 2 * hd + 2)
                if hd >= 2:
                    pe.wait_ge(sc_ev, hd - 1)
                b = hd % 2
                for c in range(2):
                    pe.matmul(ps[:, b, 0:T], k_r[:, hd, c, 0:P], q_r[:, hd, c, :], start=c == 0, stop=c == 1)
                for c in range(2):
                    mm = pe.matmul(ps[:, b, T:T + P], k_r[:, hd, c, P:T], q_r[:, hd, c, P:T],
                                   start=c == 0, stop=c == 1)
                mm.then_inc(sc_mm, 1)

            scores(0)
            for hd in range(RET_HEADS):
                g_unit(2 * hd)
                pe.wait_ge(sc_ev, hd + 1)
                pe.wait_ge(v_ev, 8)
                if hd:
                    pe.wait_ge(on_ev, hd)
                for e in range(4):
                    o = ps[:, 2 + e // 2, (e % 2) * T:(e % 2) * T + T]
                    c0 = hd * RET_V + e * P
                    pe.matmul(o, v_r[:, 0, c0:c0 + P], sT[:, hd % 2, 0:T], start=e % 2 == 0, stop=False,
                              skip_group_check=True)
                    mm = pe.matmul(o[:, P:T], v_r[:, 1, c0:c0 + P], sT[:, hd % 2, T:T + P], start=False, stop=True,
                                   skip_group_check=True)
                mm.then_inc(o_mm, 1)
                g_unit(2 * hd + 1)
                if hd + 1 < RET_HEADS:
                    scores(hd + 1)
                pe.wait_ge(osq, hd + 1)
                for e in range(4):
                    mm = pe.matmul(ps[:, 4, 0:T], ones[:], sq[:, e, :], start=e == 0, stop=e == 3)
                mm.then_inc(oss, 1)
            ada_turn(2)

            pe.wait_ge(on_ev, 4)
            for u in range(8):
                pe.wait_ge(og_done, u + 1)
                mm = row_T(U_RO + u, o_r[:, 2 * u:2 * u + 2, :], 0, u == 0, u == 7)
                mm.then_inc(used, 1)
            norm(N_POST0)
            norm(N_PREF0)

            def ffn(f, U0, x0):
                base = f * PAIRS

                def gu(U, j, r=0, x_ready=None):
                    b = j % 2
                    if j >= 2:
                        pe.wait_ge(f_act, r * 2 + (base + j - 1))
                    col_T(U, xn, 4 + 2 * b, r, x_ready)
                    if j >= 2:
                        pe.wait_ge(f_hidden, r * 2 + (base + j - 1))
                    col_T(U + 1, xn, 5 + 2 * b, r)

                def o(U, j, r=0, first=False, last=False):
                    pe.wait_ge(f_hidden, r * 2 + (base + j + 1))
                    x = f_hid[:, j % 2, :].rearrange("p (c t) -> p c t", c=2)
                    row_T(U, x, 0, first, last, r).then_inc(used, 1)

                gu(U0, 0, 0, x0)
                gu(U0 + 2, 1)
                o(U0 + 4, 0, first=True)
                with pe.Fori(0, (PAIRS - 3) // 2) as i:
                    for c in range(2):
                        gu(U0 + 5 + 3 * c, 2 + c, i)
                        o(U0 + 7 + 3 * c, 1 + c, i)
                gu(U0 + 29, 10)
                o(U0 + 31, 9)
                o(U0 + 32, 10, last=True)

            ffn(0, U_F0, XN[N_PREF0])
            norm(N_POSTF0)
            norm(N_PRE1)

            for u in range(6):
                if u >= 2:
                    pe.wait_ge(kv_ev, u - 1)
                unit = col_T if u < 4 else col_tok
                unit(U_KV + u, xn, 5 + 2 * (u % 2), x_ready=XN[N_PRE1] if u == 0 else None)
            for u in range(4):
                pe.wait_ge(*((nq_ev, u - 1) if u >= 2 else (kv_ev, 5 + u)))
                if u == 0:
                    pe.wait_ge(xn_ready, XN[N_PRE1] + 16)
                if u == 0:
                    pe.wait_ge(blocks_set, 4)
                    for kind in range(2):
                        for w in range(2):
                            U = U_W1 + 2 * kind + w
                            take(U)
                            for c in range(8):
                                mm = pe.matmul(ps[0:60, kind, 0:T], blocks[:, kind, 8 * w + c, :], slot8(U)[:, c, :],
                                               start=w == 0 and c == 0, stop=w == 1 and c == 7)
                            mm.then_inc(used, 1)
                col_T(U_NQ + u, sq, 5 + 2 * (u % 2))
                if u == 1:
                    pe.wait_ge(c_act, 2)
                    for kind in range(2):
                        for c in range(2):
                            o = (2 * kind + c) * 60
                            mm = pe.transpose(ps[:, 2, o:o + 60],
                                              cmp_hid[0:60, kind * T + c * P:kind * T + c * P + P],
                                              ident[0:60, 0:60])
                    mm.then_inc(c_tr, 1)
                if u == 2:
                    pe.wait_ge(c_trev, 1)
                    pe.wait_ge(rest_in, REST_IN)
                    for c in range(2):
                        pe.matmul(ps[:, 3, 0:60], w2k[:, c, :, :], hidT[:, c * 60:c * 60 + 60],
                                  start=c == 0, stop=c == 1)
                    for g in range(GROUPS):
                        for c in range(2):
                            o = 120 + c * 60 + g * N_CMP
                            mm = pe.matmul(ps[0:N_CMP, 3, 64 + g * HD:64 + g * HD + HD], hidT[:, o:o + N_CMP],
                                           w2v[:, c, :], start=c == 0, stop=c == 1)
                    mm.then_inc(c_kv, 1)
            pe.wait_ge(nq_ev, 3)
            pe.wait_ge(rest_in, REST_IN)
            for t in range(2):
                for k in range(8):
                    mm = pe.matmul(ps[:, 5, t * 48:t * 48 + 48], sq[:, k, t * P:t * P + P], w_gate[:, k, :],
                                   start=k == 0, stop=k == 7)
            mm.then_inc(nq_mm, 1)

            def n_scores(hd):
                pp, ch, g = head_parts(hd)
                b = 2 * (hd % 2)
                if hd >= 2:
                    pe.wait_ge(s_add, hd - 1)
                pe.matmul(ps[:, b, :], q_n[pp, ch, P:T], kd[pp, :, g, :], start=True, stop=True)
                pe.matmul(ps[:, b + 1, 272:272 + N_CMP], q_n[pp, ch, P:T], kc[pp, g, :], start=True, stop=True)
                pe.matmul(ps[:, b + 1, 0:T], q_n[pp, ch, 0:P], kd[pp, :, g, 0:P], start=True, stop=True)
                pe.matmul(ps[:, b + 1, T:T + N_CMP], q_n[pp, ch, 0:P], kc[pp, g, :],
                          start=True, stop=True).then_inc(s_mm, 1)

            def n_turn(hd):
                S = n_s[:, hd % 2, :]
                pe.wait_ge(s_p, hd + 1)
                if hd:
                    pe.wait_ge(s_trev, hd)
                    pe.wait_ge(s_trev2, hd)
                for br in range(2):
                    late = S[:, br * T:br * T + T]
                    early = S[:, 512 + br * P:512 + br * P + P]
                    pe.transpose(ps[:, 4 + br, 0:P], early, ident)
                    pe.transpose(ps[:, 4 + br, P:T], late[:, 0:P], ident)
                    pe.transpose(ps[:, 4 + br, T:T + P], late[:, P:T], ident)
                    mm = pe.transpose(ps[0:N_CMP, 4 + br, 384:512], S[:, 768 + 16 * br:768 + 16 * br + N_CMP], ident)
                mm.then_inc(s_tr, 1)

            def n_values(hd):
                pp, ch, g = head_parts(hd)
                pe.wait_ge(s_trev, hd + 1)
                pe.wait_ge(s_trev2, hd + 1)
                if hd % 2 == 0 and ch >= 2:
                    pe.wait_ge(s_ov, ch - 1)
                b = hd % 2
                o = ps[pp, 6 + ch % 2, 0:T]
                for br in range(2):
                    pe.matmul(o, v_n[:, br, 0, g * HD:g * HD + HD], n_pT[:, b, br, 0:T], start=br == 0, stop=False)
                    pe.matmul(o[:, P:T], v_n[:, br, 1, g * HD:g * HD + HD], n_pT[:, b, br, T:T + P],
                              start=False, stop=False)
                pe.matmul(o, vc[:, g, :], n_pc[0:N_CMP, b, :], start=False, stop=True).then_inc(s_pv, 1)

            pe.wait_ge(nq_ev, 5)
            pe.wait_ge(c_kvev, 2)
            pe.wait_ge(kd_in, 128)
            n_scores(0)
            n_scores(1)
            for hd in range(HEADS):
                n_turn(hd)
                if hd + 2 < HEADS:
                    n_scores(hd + 2)
                n_values(hd)
            pe.wait_ge(s_add, HEADS)
            for u in range(4):
                pe.wait_ge(s_ov, 2 * u + 2)
                row_T(U_NO + u, o_n[:, 2 * u:2 * u + 2, :], 0, u == 0, u == 3).then_inc(used, 1)
            norm(N_POST1)
            norm(N_PREF1)
            ffn(1, U_F1, XN[N_PREF1])
            norm(N_POSTF1)

            norm(N_CTX)
            norm(N_IN2)
            for u in range(4):
                if u >= 2:
                    pe.wait_ge(va_ev, u - 1)
                col_tok(U_IN2 + u, xn, 5 + 2 * (u % 2), x_ready=XN[N_IN2] if u == 0 else None)
            for u in range(4):
                pe.wait_ge(*((ua_ev, u - 1) if u >= 2 else (va_ev, 3 + u)))
                col_T(U_IN2 + 4 + u, xn, 5 + 2 * (u % 2))

            def turn_pairs(n, src):
                pe.wait_ge(qw_ev, n + 1)
                if n:
                    pe.wait_ge(q_sin, n)
                for c in range(2):
                    mm = pe.matmul(ps[:, 6, c * T:c * T + T], tab("perm"), src[:, c * T:c * T + T],
                                   start=True, stop=True)
                mm.then_inc(qp_mm, 1)

            for u in range(5):
                pe.wait_ge(*((qw_ev, u - 1) if u >= 2 else (ua_ev, 3 + u)))
                if u < 4:
                    col_T(U_IN2 + 8 + u, xn, 5 + 2 * (u % 2))
                else:
                    take(U_IN2 + 12)
                    for src, bank in ((xn, 5), (ctxn, 7)):
                        if bank == 7:
                            pe.wait_ge(qw_ev, 4)
                        for b in range(2):
                            for k in range(8):
                                mm = pe.matmul(ps[:, bank, b * T:b * T + T],
                                               slot8(U_IN2 + 12)[:, k, b * P:b * P + P], src[:, k, :],
                                               start=k == 0, stop=k == 7)
                        mm.then_inc(kw_mm if bank == 5 else used, 1)
                if u:
                    turn_pairs(u - 1, q_w[:, 2 * u - 2:2 * u, :].rearrange("p a t -> p (a t)"))
            turn_pairs(4, kw_raw[:, 0, :])
            pe.wait_ge(ln_seq, LN_END)
            pe.wait_ge(ln_in, 64)
            for g in range(A_GROUPS):
                for t in range(2):
                    mm = pe.matmul(ps[:, g // 2, (g % 2) * T + t * P:(g % 2) * T + t * P + P],
                                   va[:, t, g * P:g * P + P], ws[:, g, :], start=True, stop=True)
                if g % 2:
                    mm.then_inc(sp_mm, 1)
            for s in range(2):
                pe.wait_ge(qw_ev, 5 + s)
                src = xn if s == 0 else ctxn
                if s == 0:
                    take(U_IN2 + 13)
                for t in range(2):
                    for k in range(8):
                        mm = pe.matmul(ps[:, 5 + 2 * s, t * T:t * T + T], src[:, k, t * P:t * P + P],
                                       slot8(U_IN2 + 13)[:, k, :], start=k == 0, stop=k == 7)
                mm.then_inc(vw_mm if s == 0 else used, 1)
            for u in range(8):
                pe.wait_ge(*((gt_ev, u - 1) if u >= 2 else (vw_ev, 1 + u)))
                col_T(U_IN2 + 14 + u, xn, 5 + 2 * (u % 2))

            def w_scores(hd):
                pp, ch, g = head_parts(hd)
                b = 2 * (hd % 2)
                n = HEADS + hd
                pe.wait_ge(*((s_exp, n - 1) if hd >= 2 else (sp_add, 4)))
                for t in range(2):
                    mm = pe.matmul(ps[:, b + t, :], q_w[pp, ch, t * P:t * P + P], kd2[pp, g, :, :],
                                   start=True, stop=True)
                mm.then_inc(s_mm, 1)

            def w_turn(hd):
                n = HEADS + hd
                pe.wait_ge(s_p, n + 1)
                if hd:
                    pe.wait_ge(s_trev, n)
                    pe.wait_ge(s_trev2, n)
                for kb in range(4):
                    for t in range(2):
                        mm = pe.transpose(ps[:, 4 + kb // 2, (kb % 2) * T + t * P:(kb % 2) * T + t * P + P],
                                          w_s[:, hd % 2, t, kb * P:kb * P + P], ident)
                mm.then_inc(s_tr, 1)

            def w_values(hd):
                pp, ch, g = head_parts(hd)
                n = HEADS + hd
                pe.wait_ge(s_trev, n + 1)
                pe.wait_ge(s_trev2, n + 1)
                if hd % 2 == 0:
                    pe.wait_ge(*((s_ov, 8 + ch - 1) if ch >= 2 else (gt_ev, 8)))
                o = ps[pp, 6 + ch % 2, 0:T]
                for kb in range(4):
                    mm = pe.matmul(o, vw_tok[:, kb, g * HD:g * HD + HD], w_pT(hd)[:, kb, :],
                                   start=kb == 0, stop=kb == 3)
                mm.then_inc(s_pv, 1)

            pe.wait_ge(kd2_in, 128)
            pe.wait_ge(q_rot, 5)
            pe.wait_ge(gt_ev, 8)
            w_scores(0)
            w_scores(1)
            for hd in range(HEADS):
                w_turn(hd)
                if hd + 2 < HEADS:
                    w_scores(hd + 2)
                w_values(hd)
            pe.wait_ge(s_exp, 2 * HEADS)
            pe.wait_ge(ya_done, 4)
            for u in range(4):
                row_T(U_PA + u, ya[:, 2 * u:2 * u + 2, :], 0, u == 0, u == 3).then_inc(used, 1)
            for u in range(4):
                pe.wait_ge(s_ov, 8 + 2 * u + 2)
                if u == 0:
                    pe.wait_ge(s_ov, 16)
                row_T(U_PB + u, o_w[:, 2 * u:2 * u + 2, :], 4, u == 0, u == 3).then_inc(used, 1)
            for u in range(4):
                pe.wait_ge(merged, u + 1)
                row_T(U_WO + u, gb[:, 2 * u:2 * u + 2, :], 0, u == 0, u == 3).then_inc(used, 1)
            norm(N_MOE)

            pe.wait_ge(xn_ready, XN[N_MOE] + 8)
            for t in range(2):
                for k in range(8):
                    mm = pe.matmul(ps[:, 5, t * EXPERTS:(t + 1) * EXPERTS], xn[:, k, t * P:t * P + P],
                                   w_router[:, k, :], start=k == 0, stop=k == 7)
            mm.then_inc(lg_mm, 1)
            for b in range(4):
                t, half = b // 2, b % 2
                for k in range(4):
                    mm = pe.transpose(ps[:, b, k * P:k * P + P], xn[:, 4 * half + k, t * P:t * P + P], ident)
                mm.then_inc(tok_mm, 1)
            pe.wait_ge(r_seq, R_AFF)
            for t in range(2):
                mm = pe.transpose(ps[0:EXPERTS, 6, t * P:t * P + P], aff[:, t, :], ident)
            mm.then_inc(r_tr, 1)
            pe.wait_ge(r_seq, R_MASK)
            for t in range(2):
                mm = pe.transpose(ps[:, 7, t * EXPERTS:(t + 1) * EXPERTS], rank_work[0:EXPERTS, 1, t * P:t * P + P],
                                  ident[0:EXPERTS, 0:EXPERTS])
            mm.then_inc(r_tr, 1)
            pe.wait_ge(r_seq, R_MASKT)
            m = [e_small[:, 1, t * EXPERTS:(t + 1) * EXPERTS] for t in range(2)]
            pe.matmul(ps[:, 5, 0:EXPERTS], tab("tri"), m[0], start=True, stop=True)
            pe.matmul(ps[:, 5, EXPERTS:2 * EXPERTS], ones[:], m[0], start=True, stop=False)
            pe.matmul(ps[:, 5, EXPERTS:2 * EXPERTS], tab("tri"), m[1], start=False, stop=True).then_inc(r_pos, 1)
            pe.wait_ge(pick_set, 1)
            pe.wait_ge(tok_ev, 4)
            for k in range(8):
                for t in range(2):
                    mm = pe.matmul(ps[:, k, :], h2[:, t, k * P:k * P + P], pick[:, t, :],
                                   start=t == 0, stop=t == 1)
                mm.then_inc(xe_mm, 1)
            pe.wait_ge(xe_ev, 8)
            pe.wait_ge(r_seq, R_ZERO)
            for b in range(4):
                pe.matmul(ps[:, b, :], ones[:], zeros_row, start=True, stop=False, skip_group_check=True)

            def moe(n):
                pe.wait_ge(ed_ev, n)
                for b in range(4):
                    for half in range(2):
                        c = 4 * half + b
                        pp = slice(64 * half, 64 * half + 64)
                        mm = pe.matmul(ps[:, c // 2, (c % 2) * T:(c % 2) * T + T], e_y[pp, b * P:b * P + P],
                                       e_pT[pp, :], start=False, stop=False, skip_group_check=True)
                mm.then_inc(moe_mm, 1)

            def expert(e):
                first = isinstance(e, int)

                def etake(w):
                    pe.wait_ge(e_landed[w % ERING], e * 64 + 16 * (w // ERING + 1))

                pe.wait_ge(cur_set, e * 2 + 2)
                if not first:
                    pe.wait_ge(e_act, e)
                for part, bank in ((0, 4), (1, 5)):
                    if part and not first:
                        moe(e)
                        pe.wait_ge(e_hset, e)
                    for q in range(4):
                        w = 4 * part + q
                        etake(w)
                        sl = ering[:, w % ERING, :].rearrange("p (c n) -> p c n", c=2)
                        for c in range(2):
                            k = 2 * q + c
                            for j in range(4):
                                mm = pe.matmul(ps[32 * j:32 * j + 32, bank, :], xcur[:, k, :],
                                               sl[:, c, 512 * j:512 * j + 512], start=k == 0, stop=k == 7)
                        mm.then_inc(e_used, 1)
                if not first:
                    pe.wait_ge(eh_ev, e)
                for t in range(2):
                    mm = pe.transpose(ps[:, 7, t * P:t * P + P], pcur[:, t, :, :].rearrange("p r s -> p (r s)"),
                                      ident)
                mm.then_inc(ep_tr, 1)
                pe.wait_ge(e_hset, e + 1)
                pe.wait_ge(ep_ev, e + 1)
                for m in range(4):
                    mm = pe.transpose(ps[:, 7, m * P:m * P + P], e_hid[:, m * P:m * P + P], ident)
                mm.then_inc(eh_tr, 1)
                pe.wait_ge(eh_ev, e + 1)
                for w in range(8, 12):
                    etake(w)
                    sl = ering[:, w % ERING, :].rearrange("p (c n) -> p c n", c=4)
                    for m in range(4):
                        for half in range(2):
                            g = 2 * half + m % 2
                            mm = pe.matmul(ps[32 * g:32 * g + 32, 6, :],
                                           e_hidT[:, m * P + 32 * (w - 8):m * P + 32 * (w - 8) + 32],
                                           sl[:, m, 512 * half:512 * half + 512],
                                           start=w == 8 and m < 2, stop=w == 11 and m >= 2)
                    mm.then_inc(e_used, 1)

            expert(0)
            with pe.Fori(1, EXPERTS) as e:
                expert(e)
            moe(EXPERTS)
            norm(N_END)

        @block.scalar
        def _(act):
            act.dma_start(h[:], a["xT"].rearrange("(k p) t -> p k t", p=P)).then_inc(x_in, 16)
            firsts = [(tabs[:], a["tabs"]), (cols[:], a["cols"]), (rel[0:32, :], a["rel_bias"]),
                      (bucket_rows[:], a["bucket_rows"]), (bucket_cmp[0:33, :], a["bucket_cmp"])]
            assert len(firsts) * 16 == FIRST_IN
            for dst, src in firsts:
                act.dma_start(dst, src).then_inc(first_in, 16)
            act.dma_start(decay, a["decay"].rearrange("p (h j) -> p h j", h=RET_HEADS)).then_inc(decay_in, 16)
            rests = [(w_gate[:], a["nsa_w_in"].rearrange("(k p) n -> p k n", p=P)[:, :, HEADS * HD:]),
                     (w2k[:, :, 0, :], a["cmp_w2_k"].rearrange("(c p) n -> p c n", p=P)),
                     (w2k[:, :, 1, :], a["cmp_w2_k"].rearrange("(c p) n -> p c n", p=P)),
                     (w2v[:], a["cmp_w2_v"].rearrange("(c p) n -> p c n", p=P)),
                     (w_router[:], a["w_router_2"].rearrange("(k p) n -> p k n", p=P)),
                     (sink[:], a["attn_sink_2"].partition_broadcast(P))]
            assert len(rests) * 16 == REST_IN
            for dst, src in rests:
                act.dma_start(dst, src).then_inc(rest_in, 16)

            def squares(n, src, ready=None):
                for q in range(4):
                    if ready:
                        act.wait_ge(*ready(q))
                    act.activation(sq[:, 2 * q:2 * q + 2, :], src(q), ACT.Square).then_inc(sq_ready, 1)

            def roots(n):
                act.wait_ge(ss_ready, n + 1)
                if n:
                    act.wait_ge(rs_ready, n)
                act.activation(root[:], ps[:, 4, 0:T], ACT.Sqrt, scale=1.0 / D, bias=EPS).then_inc(root_ready, 1)

            def of_h(q):
                return h[:, 2 * q:2 * q + 2, :]

            def of_acc(q):
                return ps[:, q, :].rearrange("p (c t) -> p c t", c=2)

            act.wait_ge(x_in, 16)
            squares(N_PRE0, of_h)
            act.wait_ge(brow_mm, 2)
            act.activation(bias_rows[:], ps[0:HEADS, 5, 0:384], ACT.Copy).then_inc(brow_ev, 1)
            act.activation(cbias[:], ps[:, 7, 0:480].rearrange("p (t n h) -> p h t n", t=2, n=N_CMP),
                           ACT.Copy).then_inc(cbias_ev, 1)
            roots(N_PRE0)
            act.wait_ge(cs_set, 1)
            for r, name in enumerate(("c", "c_ctx")):
                ins = act.activation(cs[:, :, r], col(name), ACT.Silu)
            ins.then_inc(cs_set, 1)
            act.wait_ge(brow_ev, 1)
            act.dma_start(bias_dram, bias_rows[:].unsqueeze(1).to_broadcast([HEADS, P, 384])).then_inc(bias_out, 16)

            def ada_rows_out(r):
                taken(act, U_RET + 16 * r + 15)
                if r:
                    act.wait_ge(ada_tr, r)
                act.activation(ada_rows[:], ps[:, 6, :], ACT.Copy).then_inc(ada_ev, 1)

            ada_rows_out(0)
            for u in range(8):
                taken(act, U_RET + 16 + 2 * u)
                act.activation(v_r[:, :, u * T:u * T + T],
                               ps[:, 5 + 2 * (u % 2), :].rearrange("p (t n) -> p t n", t=2), ACT.Copy).then_inc(v_ev, 1)
            ada_rows_out(1)

            def g_out(u):
                taken(act, U_RET + 32 + 2 * u)
                if u >= 2:
                    act.wait_ge(og_done, u - 1)
                else:
                    act.wait_ge(qk_done, 8)
                act.activation(gs[:, u % 2, :], ps[:, 5 + 2 * (u % 2), :], ACT.Silu).then_inc(g_ev, 1)

            for hd in range(RET_HEADS):
                g_out(2 * hd)
                act.wait_ge(o_mm, hd + 1)
                if hd:
                    act.wait_ge(oss, hd)
                act.activation(sq[:, 0:4, :], ps[:, 2:4, :].rearrange("p b (c t) -> p (b c) t", c=2),
                               ACT.Square).then_inc(osq, 1)
                g_out(2 * hd + 1)
                act.wait_ge(oss, hd + 1)
                act.activation(root[:], ps[:, 4, 0:T], ACT.Sqrt, scale=1.0 / RET_V, bias=EPS).then_inc(oroot, 1)
            ada_rows_out(2)

            def post(n, before):
                taken(act, before)
                squares(n, of_acc)
                roots(n)

            def pre(n, posted):
                squares(n, of_h, lambda q: (h_ready, POST[posted] + 2 * q + 2))
                roots(n)

            post(N_POST0, U_F0 - 1)
            act.wait_ge(bias_out, 16)
            act.dma_start(bias, bass.AP(bias_dram.tensor, P - 1, [[383, P], [P * 384, HEADS], [1, T]])) \
               .then_inc(bias_in, 16)
            pre(N_PREF0, N_POST0)

            def ffn(f):
                base = f * PAIRS

                def silu(j, r=0):
                    taken(act, gate_unit(f, j), r)
                    if j >= 2:
                        act.wait_ge(f_hidden, r * 2 + (base + j - 1))
                    act.activation(f_silu[:, j % 2, :], ps[:, 4 + 2 * (j % 2), :], ACT.Silu).then_inc(f_act, 1)

                silu(0)
                silu(1)
                with act.Fori(0, (PAIRS - 3) // 2) as i:
                    silu(2, i)
                    silu(3, i)
                silu(10)

            ffn(0)
            post(N_POSTF0, U_KV - 1)
            pre(N_PRE1, N_POSTF0)
            for u in range(6):
                taken(act, U_KV + u)
                dst = kv_raw[:, u] if u < 4 else v_n[:, u - 4]
                act.activation(dst, ps[:, 5 + 2 * (u % 2), :].rearrange("p (t n) -> p t n", t=2),
                               ACT.Copy).then_inc(kv_ev, 1)
                if u in (1, 3):
                    act.wait_ge(kv_ev, u + 1)
                    for half in range(2):
                        for odd in range(2):
                            hp, op = slice(64 * half, 64 * half + 64), slice(64 * odd, 64 * odd + 64)
                            for kind in range(2):
                                if u == 1:
                                    act.dma_start(shifted[hp, kind, odd::2, 0:T - half],
                                                  kv_raw[op, kind, :, half:T]).then_inc(shift_in, 16)
                                else:
                                    act.dma_start(kd[hp, kind, odd::2, :],
                                                  kv_raw[op, 2 + kind, :, :]).then_inc(kd_in, 16)
            for kind in range(2):
                taken(act, U_W1 + 2 * kind + 1)
                act.activation(cmp_hid[0:60, kind * T:kind * T + T], ps[0:60, kind, 0:T],
                               ACT.Silu).then_inc(c_act, 1)
            for u in range(4):
                taken(act, U_NQ + u)
                act.activation(q_n[:, 2 * u:2 * u + 2, :],
                               ps[:, 5 + 2 * (u % 2), :].rearrange("p (c t) -> p c t", c=2), ACT.Copy,
                               scale=HD ** -0.5).then_inc(nq_ev, 1)
            act.wait_ge(nq_mm, 1)
            act.activation(gates[:], ps[:, 5, 0:96].rearrange("p (t n) -> p t n", t=2),
                           ACT.Sigmoid).then_inc(nq_ev, 1)

            def n_exp(hd):
                S, s = n_s[:, hd % 2, :], st[:, hd % 2, :]
                act.wait_ge(s_neg, hd + 1)
                for i, part in enumerate([S[:, 0:T], S[:, T:512], S[:, 512:640], S[:, 640:768],
                                          S[:, 768:768 + N_CMP], S[:, 784:784 + N_CMP]]):
                    ins = act.activation(part, part, ACT.Exp, bias=s[:, 6 + i:7 + i], accum_out=s[:, 12 + i:13 + i])
                ins.then_inc(s_exp, 1)

            def n_pout(hd):
                act.wait_ge(s_tr, hd + 1)
                if hd >= 2:
                    act.wait_ge(s_pv, hd - 1)
                act.activation(n_pT[:, hd % 2, :, :], ps[:, 4:6, 0:384], ACT.Copy).then_inc(s_trev, 1)
                act.activation(n_pc[0:N_CMP, hd % 2, :].rearrange("p (t j) -> p t j", t=2),
                               ps[0:N_CMP, 4:6, 384:512], ACT.Copy).then_inc(s_trev2, 1)

            n_exp(0)
            for hd in range(HEADS):
                if hd + 1 < HEADS:
                    n_exp(hd + 1)
                n_pout(hd)
            post(N_POST1, U_F1 - 1)
            pre(N_PREF1, N_POST1)
            ffn(1)
            post(N_POSTF1, U_IN2 - 1)
            act.dma_start(ctxn, a["ctxT"].rearrange("(k p) t -> p k t", p=P)).then_inc(ctx_in, 16)
            act.dma_start(ln_g, a["gmlp_ln_g_2"].partition_broadcast(P)).then_inc(ln_in, 16)
            act.dma_start(ln_b, a["gmlp_ln_b_2"].partition_broadcast(P)).then_inc(ln_in, 16)
            act.dma_start(bs, a["b_spatial_2"].partition_broadcast(P)).then_inc(ln_in, 16)
            act.dma_start(ws, a["w_spatialT"]).then_inc(ln_in, 16)
            act.wait_ge(ctx_in, 16)
            squares(N_CTX, lambda q: ctxn[:, 2 * q:2 * q + 2, :])
            roots(N_CTX)
            pre(N_IN2, N_POSTF1)
            for u in range(4):
                taken(act, U_IN2 + u)
                act.activation(va[:, :, u * T:u * T + T],
                               ps[:, 5 + 2 * (u % 2), :].rearrange("p (t n) -> p t n", t=2),
                               ACT.Gelu_apprx_tanh).then_inc(va_ev, 1)
            for u in range(4):
                taken(act, U_IN2 + 4 + u)
                act.activation(ya[:, 2 * u:2 * u + 2, :],
                               ps[:, 5 + 2 * (u % 2), :].rearrange("p (c t) -> p c t", c=2),
                               ACT.Gelu_apprx_tanh).then_inc(ua_ev, 1)
            act.wait_ge(ln_seq, 2)
            act.activation(st[:, 0, 28:30], st[:, 0, 24:28].rearrange("p (t c) -> p t c", c=2)[:, :, 1], ACT.Sqrt,
                           bias=EPS).then_inc(ln_root, 1)
            for n in range(6):
                if n == 4:
                    act.wait_ge(kw_mm, 1)
                else:
                    taken(act, U_IN2 + 8 + min(n, 4))
                dst = q_w[:, 2 * n:2 * n + 2, :].rearrange("p a t -> p (a t)") if n < 4 else kw_raw[:, n - 4, :]
                act.activation(dst, ps[:, 5 + 2 * (n % 2), :], ACT.Copy,
                               scale=HD ** -0.5 if n < 4 else 1.0).then_inc(qw_ev, 1)
            for s in range(2):
                if s == 0:
                    act.wait_ge(vw_mm, 1)
                else:
                    taken(act, U_IN2 + 13)
                act.activation(vw_tok[:, 2 * s:2 * s + 2, :],
                               ps[:, 5 + 2 * s, :].rearrange("p (t n) -> p t n", t=2), ACT.Copy).then_inc(vw_ev, 1)
            act.wait_ge(q_rot, 5)
            act.wait_ge(qw_ev, 6)
            for half in range(2):
                for odd in range(2):
                    hp, op = slice(64 * half, 64 * half + 64), slice(64 * odd, 64 * odd + 64)
                    for s in range(2):
                        act.dma_start(kd2[hp, odd::2, s, :],
                                      kw_raw[op, s, :].rearrange("p (g t) -> p g t", g=2)).then_inc(kd2_in, 16)
            for u in range(8):
                taken(act, U_IN2 + 14 + u)
                if u == 0:
                    act.wait_ge(sp_mm, 4)
                for c in range(2):
                    dst = (ga if u < 4 else gb)[:, (2 * u + c) % 8, :]
                    ins = act.activation(dst, ps[:, 5 + 2 * (u % 2), c * T:c * T + T], ACT.Sigmoid,
                                         bias=col("b_merge", 2 * u + c))
                ins.then_inc(gt_ev, 1)

            def w_exp(hd):
                S, s, b = w_s[:, hd % 2], st[:, hd % 2, :], 2 * (hd % 2)
                act.wait_ge(s_neg, HEADS + hd + 1)
                for t in range(2):
                    act.activation(S[:, t, 0:T], S[:, t, 0:T], ACT.Exp, bias=s[:, 6 + t:7 + t],
                                   accum_out=s[:, 12 + t:13 + t])
                    act.activation(S[:, t, T:512], ps[:, b + t, T:512], ACT.Exp, bias=s[:, 6 + t:7 + t],
                                   accum_out=s[:, 14 + t:15 + t])
                act.activation(s[:, 16:18], s[:, 6:8], ACT.Exp, bias=sink[:, hd:hd + 1]).then_inc(s_exp, 1)

            def w_pout(hd):
                n = HEADS + hd
                act.wait_ge(s_tr, n + 1)
                if hd >= 2:
                    act.wait_ge(s_pv, n - 1)
                act.activation(w_pT(hd)[:, 0:2, :], ps[:, 4, :].rearrange("p (k t) -> p k t", k=2),
                               ACT.Copy).then_inc(s_trev, 1)

            act.wait_ge(rest_in, REST_IN)
            w_exp(0)
            for hd in range(HEADS):
                if hd + 1 < HEADS:
                    w_exp(hd + 1)
                w_pout(hd)
            squares(N_MOE, of_h, lambda q: (x2_done, q + 1))
            roots(N_MOE)
            for b in range(4):
                act.wait_ge(tok_mm, b + 1)
                act.activation(h2[:, b // 2, (b % 2) * 512:(b % 2) * 512 + 512], ps[:, b, :],
                               ACT.Copy).then_inc(tok_ev, 1)
            act.wait_ge(r_seq, 2)
            for t in range(2):
                ins = act.activation(aff[:, t, :], ps[:, 5, t * EXPERTS:(t + 1) * EXPERTS], ACT.Exp,
                                     bias=st[:, 0, 2 + t:3 + t], accum_out=st[:, 0, 4 + t:5 + t])
            ins.then_inc(r_exp, 1)
            for k in range(8):
                act.wait_ge(xe_mm, k + 1)
                act.activation(xe[:, k, :], ps[:, k, :], ACT.Copy).then_inc(xe_ev, 1)

            def expert(e):
                first = isinstance(e, int)
                act.wait_ge(e_used, e * E_UNITS + 4)
                if not first:
                    act.wait_ge(e_hset, e)
                act.activation(e_silu, ps[:, 4, :], ACT.Silu).then_inc(e_act, 1)
                act.wait_ge(ep_tr, e + 1)
                if not first:
                    act.wait_ge(moe_mm, e)
                act.activation(e_pT, ps[:, 7, 0:T], ACT.Copy).then_inc(ep_ev, 1)
                act.wait_ge(e_used, e * E_UNITS + 12)
                act.activation(e_y, ps[:, 6, :], ACT.Copy).then_inc(ed_ev, 1)

            expert(0)
            with act.Fori(1, EXPERTS) as e:
                expert(e)
            squares(N_END, of_h, lambda q: (moe_done, 2 * q + 2))
            roots(N_END)

        @block.vector
        def _(dve):
            dve.memset(ones[:], 1.0).then_inc(ones_set, 1)
            dve.memset(cs[:], 0.0).then_inc(cs_set, 1)

            def inverse(n):
                dve.wait_ge(root_ready, n + 1)
                dve.reciprocal(rs[:], root[:]).then_inc(rs_ready, 1)
                dve.wait_ge(rs_ready, n + 1)

            def pre(n, gains, dst=None, src=None):
                dst, src = dst or xn, src or h
                for k in range(8):
                    dve.scalar_tensor_tensor(out=dst[:, k, :], in0=src[:, k, :], scalar=gains(k), in1=rs[:],
                                             op0=ALU.mult, op1=ALU.mult).then_inc(xn_ready, 1)

            def gain_of(name):
                return lambda k: col(name, k)

            dve.wait_ge(first_in, FIRST_IN)
            inverse(N_PRE0)
            pre(N_PRE0, gain_of("mix_pre0"))

            def ada_out(r):
                dve.wait_ge(ada_tr, r + 1)
                for row in range(2):
                    o = COLS["b_ada"][0] + 16 * r
                    ins = dve.tensor_tensor(
                        mod[:, row, 16 * r:16 * r + 16].rearrange("p (j m) -> p j m", j=4),
                        ps[:, 6, :].rearrange("p (m j s) -> p j m s", m=4, j=4)[:, :, :, row],
                        cols[:, o:o + 16].rearrange("p (j m) -> p j m", j=4), ALU.add)
                ins.then_inc(ada_mod, 1)

            for u in range(8):
                taken(dve, U_RET + 2 * u)
                if u >= 2:
                    dve.wait_ge(qk_done, u - 1)
                src = ps[:, 5 + 2 * (u % 2), :]
                dve.tensor_tensor(rot[:, u % 2, 0, :].rearrange("p (c t) -> p c t", c=2),
                                  src.rearrange("p (c t) -> p c t", c=2),
                                  tab("ret_cos").unsqueeze(1).to_broadcast([P, 2, T]), ALU.mult)
                dve.tensor_tensor(rot[:, u % 2, 1, 0:T], src[:, T:512], tab("ret_nsin"), ALU.mult)
                dve.tensor_tensor(rot[:, u % 2, 1, T:512], src[:, 0:T], tab("ret_sin"), ALU.mult).then_inc(qk_rot, 1)
            ada_out(0)

            def ret_norm(hd):
                dve.wait_ge(oroot, hd + 1)
                dve.reciprocal(rs[:], root[:]).then_inc(ors, 1)
                dve.wait_ge(ors, hd + 1)
                dve.tensor_tensor(o_r[:, 4 * hd:4 * hd + 4, :],
                                  ps[:, 2:4, :].rearrange("p b (c t) -> p (b c) t", c=2),
                                  rs[:].unsqueeze(1).to_broadcast([P, 4, T]), ALU.mult).then_inc(on_ev, 1)

            dve.wait_ge(decay_in, 16)
            dve.wait_ge(qk_done, 8)
            for hd in range(RET_HEADS):
                dve.wait_ge(sc_mm, hd + 1)
                if hd >= 2:
                    dve.wait_ge(o_mm, hd - 1)
                dve.tensor_tensor(sT[:, hd % 2, :], ps[:, hd % 2, 0:384], decay[:, hd, :], ALU.mult).then_inc(sc_ev, 1)
                if hd == 0:
                    ada_out(1)
                if hd:
                    ret_norm(hd - 1)
            ret_norm(RET_HEADS - 1)
            ada_out(2)
            dve.wait_ge(ada_mod, 3)
            for i, (row, o, name) in enumerate(((0, 8, "norm1"), (1, 8, "norm1"), (0, 32, "norm2"))):
                ins = dve.scalar_tensor_tensor(out=gain[:, i, :], in0=mod[:, row, o:o + 8], scalar=1.0,
                                               in1=col(name), op0=ALU.add, op1=ALU.mult)
            ins.then_inc(gains_set, 1)

            def post(n, name):
                inverse(n)
                for k in range(8):
                    dve.scalar_tensor_tensor(out=xn[:, k, :], in0=ps[:, k // 2, (k % 2) * T:(k % 2) * T + T],
                                             scalar=col(name, k), in1=rs[:], op0=ALU.mult,
                                             op1=ALU.mult).then_inc(scaled, 1)

            post(N_POST0, "mix_post0")
            inverse(N_PREF0)
            pre(N_PREF0, gain_of("ffn_pre0"))

            def ffn(f):
                base = f * PAIRS

                def hidden(j, r=0):
                    dve.wait_ge(f_act, r * 2 + (base + j + 1))
                    taken(dve, gate_unit(f, j) + 1, r)
                    if j >= 2:
                        taken(dve, out_unit(f, j - 2), r)
                    dve.tensor_tensor(f_hid[:, j % 2, :], f_silu[:, j % 2, :], ps[:, 5 + 2 * (j % 2), :],
                                      ALU.mult).then_inc(f_hidden, 1)

                hidden(0)
                hidden(1)
                with dve.Fori(0, (PAIRS - 3) // 2) as i:
                    hidden(2, i)
                    hidden(3, i)
                hidden(10)

            ffn(0)
            post(N_POSTF0, "ffn_post0")
            inverse(N_PRE1)
            pre(N_PRE1, gain_of("kv_norm"))
            pre(N_PRE1, gain_of("mix_pre1"), dst=sq)
            dve.wait_ge(shift_in, 128)
            for kind, name in enumerate(("pe_k", "pe_v")):
                win = shifted[:, kind].rearrange("p g (n s) -> p s g n", s=16)
                for w in range(2):
                    dve.tensor_tensor(blocks[:, kind, 8 * w:8 * w + 8, :].rearrange("p c (g n) -> p c g n", g=GROUPS),
                                      win[:, 0:16:2, :, w:w + N_CMP],
                                      col(name)[:, 8 * w:8 * w + 8].unsqueeze(2).unsqueeze(3)
                                      .to_broadcast([P, 8, GROUPS, N_CMP]), ALU.add).then_inc(blocks_set, 1)
            dve.wait_ge(c_tr, 1)
            dve.tensor_copy(hidT[:, 0:240], ps[:, 2, 0:240]).then_inc(c_trev, 1)
            dve.wait_ge(c_kv, 1)
            dve.tensor_copy(kc[:].rearrange("p g n -> p (g n)"), ps[:, 3, 0:60]).then_inc(c_kvev, 1)
            dve.tensor_copy(vc[:].rearrange("p g n -> p (g n)"), ps[0:N_CMP, 3, 64:320]).then_inc(c_kvev, 1)
            dve.wait_ge(bias_in, 16)
            dve.wait_ge(nq_ev, 5)

            def two(v):
                return v.unsqueeze(1).to_broadcast([P, 2, v.shape[1]])

            def parts(S):
                return (S[:, 0:512].rearrange("p (r j) -> p r j", r=2),
                        S[:, 512:768].rearrange("p (r j) -> p r j", r=2),
                        S[:, 768:800].rearrange("p (r j) -> p r j", r=2)[:, :, 0:N_CMP])

            def n_max(hd):
                S, s, b = n_s[:, hd % 2, :], st[:, hd % 2, :], 2 * (hd % 2)
                late, early, comp = parts(S)
                dve.wait_ge(s_mm, hd + 1)
                if hd >= 2:
                    dve.wait_ge(s_tr, hd - 1)
                dve.tensor_tensor(late, ps[:, b, :].rearrange("p (r j) -> p r j", r=2), two(bias[:, hd, :]), ALU.add)
                dve.tensor_tensor(early, ps[:, b + 1, 0:T].rearrange("p (r j) -> p r j", r=2),
                                  two(bias[:, hd, P:T]), ALU.add)
                dve.tensor_tensor(comp, ps[:, b + 1, T:T + 32].rearrange("p (r j) -> p r j", r=2)[:, :, 0:N_CMP],
                                  cbias[:, hd, :, :], ALU.add).then_inc(s_add, 1)
                dve.wait_ge(s_add, hd + 1)
                dve.tensor_reduce(s[:, 0:2], late, AX_X, ALU.max)
                dve.tensor_reduce(s[:, 2:4], early, AX_X, ALU.max)
                dve.tensor_reduce(s[:, 4:6], comp, AX_X, ALU.max).then_inc(s_max, 1)
                dve.wait_ge(s_max, hd + 1)
                dve.tensor_scalar(s[:, 6:12], s[:, 0:6], -1.0, LEAST, ALU.mult, ALU.min).then_inc(s_neg, 1)

            def n_scale(hd):
                S, s = n_s[:, hd % 2, :], st[:, hd % 2, :]
                dve.wait_ge(s_exp, hd + 1)
                dve.tensor_scalar(s[:, 18:24], s[:, 12:18], TINY, None, ALU.max).then_inc(s_sum, 1)
                dve.wait_ge(s_sum, hd + 1)
                dve.reciprocal(s[:, 24:30], s[:, 18:24]).then_inc(s_inv, 1)
                dve.wait_ge(s_inv, hd + 1)
                dve.tensor_tensor(s[:, 18:20], s[:, 24:26], gates[:, 1, 3 * hd + 1:3 * hd + 3], ALU.mult)
                dve.tensor_tensor(s[:, 20:22], s[:, 26:28], gates[:, 0, 3 * hd + 1:3 * hd + 3], ALU.mult)
                dve.tensor_tensor(s[:, 22:24], s[:, 28:30], gates[:, :, 3 * hd], ALU.mult).then_inc(s_fac, 1)
                dve.wait_ge(s_fac, hd + 1)
                for i, part in enumerate(parts(S)):
                    ins = dve.tensor_tensor(part, part, s[:, 18 + 2 * i:20 + 2 * i].unsqueeze(2)
                                            .to_broadcast([P, 2, part.shape[2]]), ALU.mult)
                ins.then_inc(s_p, 1)

            def o_out(dst, ch, n0):
                dve.wait_ge(s_pv, n0 + 2 * ch + 2)
                dve.tensor_copy(dst[:, ch, :], ps[:, 6 + ch % 2, 0:T]).then_inc(s_ov, 1)

            n_max(0)
            n_max(1)
            for hd in range(HEADS):
                n_scale(hd)
                if hd + 2 < HEADS:
                    n_max(hd + 2)
                if hd % 2 == 1 and hd >= 3:
                    o_out(o_n, (hd - 3) // 2, 0)
            o_out(o_n, 7, 0)
            post(N_POST1, "mix_post1")
            inverse(N_PREF1)
            pre(N_PREF1, gain_of("ffn_pre1"))
            ffn(1)
            post(N_POSTF1, "ffn_post1")

            def shift(n, dst, row, o):
                for k in range(8):
                    dve.wait_ge(mod_scaled, MODP[n] + k + 1)
                    dve.tensor_scalar(dst[:, k, :], dst[:, k, :], mod[:, row, o + k:o + k + 1], None,
                                      ALU.add).then_inc(xn_ready, 1)

            def mod_norm(n, src, dst, i, row, o):
                if n == N_CTX:
                    dve.wait_ge(scaled, POST[N_POSTF1] + 8)
                else:
                    dve.wait_ge(mod_scaled, MODP[n])
                inverse(n)
                for k in range(8):
                    dve.scalar_tensor_tensor(out=dst[:, k, :], in0=src[:, k, :], scalar=gain[:, i, k:k + 1],
                                             in1=rs[:], op0=ALU.mult, op1=ALU.mult).then_inc(mod_scaled, 1)
                shift(n, dst, row, o)

            mod_norm(N_CTX, ctxn, ctxn, 1, 1, 0)
            mod_norm(N_IN2, h, xn, 0, 0, 0)
            dve.wait_ge(va_ev, 4)
            for t in range(2):
                for c in range(2):
                    ins = dve.bn_stats(st[:, 0, 6 * (2 * t + c):6 * (2 * t + c) + 6], va[:, t, 512 * c:512 * c + 512])
            ins.then_inc(ln_seq, 1)
            dve.wait_ge(ln_seq, 1)
            for t in range(2):
                ins = dve.bn_aggr(st[:, 0, 24 + 2 * t:26 + 2 * t], st[:, 0, 12 * t:12 * t + 12])
            ins.then_inc(ln_seq, 1)
            dve.wait_ge(ln_root, 1)
            dve.reciprocal(st[:, 0, 30:32], st[:, 0, 28:30]).then_inc(ln_seq, 1)
            dve.wait_ge(ln_seq, 3)
            dve.wait_ge(ln_in, 64)
            for t in range(2):
                ins = dve.tensor_scalar(va[:, t, :], va[:, t, :], st[:, 0, 24 + 2 * t:25 + 2 * t],
                                        st[:, 0, 30 + t:31 + t], ALU.subtract, ALU.mult)
            ins.then_inc(ln_seq, 1)
            dve.wait_ge(ln_seq, 4)
            for t in range(2):
                ins = dve.tensor_tensor(va[:, t, :], va[:, t, :], ln_g, ALU.mult)
            ins.then_inc(ln_seq, 1)
            dve.wait_ge(ln_seq, 5)
            for t in range(2):
                ins = dve.tensor_tensor(va[:, t, :], va[:, t, :], ln_b, ALU.add)
            ins.then_inc(ln_seq, 1)

            def rotate(n, src):
                v = src.rearrange("p (c t) -> p c t", c=2)
                dve.wait_ge(qp_mm, n + 1)
                if n:
                    dve.wait_ge(q_rot, n)
                dve.tensor_tensor(rot2.rearrange("p (c t) -> p c t", c=2),
                                  ps[:, 6, :].rearrange("p (c t) -> p c t", c=2), two(tab("rope_sin")),
                                  ALU.mult).then_inc(q_sin, 1)
                dve.tensor_tensor(v, v, two(tab("rope_cos")), ALU.mult).then_inc(q_cos, 1)
                dve.wait_ge(q_cos, n + 1)
                dve.wait_ge(q_sin, n + 1)
                dve.tensor_tensor(src, src, rot2, ALU.add).then_inc(q_rot, 1)

            for n in range(5):
                rotate(n, q_w[:, 2 * n:2 * n + 2, :].rearrange("p a t -> p (a t)") if n < 4 else kw_raw[:, 0, :])
            for b in range(4):
                dve.wait_ge(sp_mm, b + 1)
                src = ps[:, b, :].rearrange("p (g t q) -> p g t q", g=2, t=2)
                spatial = sq[:, 2 * b:2 * b + 2, :].rearrange("p g (t q) -> p g t q", t=2)
                dve.tensor_tensor(spatial, src,
                                  bs[:, 2 * b:2 * b + 2, :].unsqueeze(2).to_broadcast([P, 2, 2, P]),
                                  ALU.add).then_inc(sp_add, 1)
                dve.wait_ge(sp_add, b + 1)
                y = ya[:, 2 * b:2 * b + 2, :].rearrange("p g (t q) -> p g t q", t=2)
                dve.tensor_tensor(y, y, spatial, ALU.mult).then_inc(ya_done, 1)

            def w_max(hd):
                n = HEADS + hd
                S, s, b = w_s[:, hd % 2], st[:, hd % 2, :], 2 * (hd % 2)
                dve.wait_ge(s_mm, n + 1)
                if hd >= 2:
                    dve.wait_ge(s_tr, n - 1)
                dve.tensor_tensor(S[:, :, 0:T], ps[:, b:b + 2, 0:T], tab("band").rearrange("p (t j) -> p t j", t=2),
                                  ALU.add).then_inc(s_add, 1)
                dve.tensor_reduce(s[:, 2:4], ps[:, b:b + 2, T:512], AX_X, ALU.max)
                dve.wait_ge(s_add, n + 1)
                dve.tensor_reduce(s[:, 0:2], S[:, :, 0:T], AX_X, ALU.max).then_inc(s_max, 1)
                dve.wait_ge(s_max, n + 1)
                dve.scalar_tensor_tensor(out=s[:, 4:6], in0=s[:, 0:2], scalar=sink[:, hd:hd + 1], in1=s[:, 2:4],
                                         op0=ALU.max, op1=ALU.max).then_inc(s_fac, 1)
                dve.wait_ge(s_fac, n + 1)
                dve.tensor_scalar(s[:, 6:8], s[:, 4:6], -1.0, None, ALU.mult).then_inc(s_neg, 1)

            def w_scale(hd):
                n = HEADS + hd
                S, s = w_s[:, hd % 2], st[:, hd % 2, :]
                dve.wait_ge(s_exp, n + 1)
                dve.tensor_tensor(s[:, 18:20], s[:, 12:14], s[:, 14:16], ALU.add).then_inc(w_sum, 1)
                dve.wait_ge(w_sum, hd + 1)
                dve.tensor_tensor(s[:, 20:22], s[:, 18:20], s[:, 16:18], ALU.add).then_inc(s_sum, 1)
                dve.wait_ge(s_sum, n + 1)
                dve.reciprocal(s[:, 24:26], s[:, 20:22]).then_inc(s_inv, 1)
                dve.wait_ge(s_inv, n + 1)
                dve.tensor_tensor(S, S, s[:, 24:26].unsqueeze(2).to_broadcast([P, 2, 512]),
                                  ALU.mult).then_inc(s_p, 1)

            def w_out(hd):
                n = HEADS + hd
                dve.wait_ge(s_tr, n + 1)
                if hd >= 2:
                    dve.wait_ge(s_pv, n - 1)
                dve.tensor_copy(w_pT(hd)[:, 2:4, :],
                                ps[:, 5, :].rearrange("p (k t) -> p k t", k=2)).then_inc(s_trev2, 1)

            dve.wait_ge(rest_in, REST_IN)
            w_max(0)
            w_max(1)
            for hd in range(HEADS):
                w_scale(hd)
                w_out(hd)
                if hd + 2 < HEADS:
                    w_max(hd + 2)
                if hd % 2 == 1 and hd >= 3:
                    o_out(o_w, (hd - 3) // 2, HEADS)
            o_out(o_w, 7, HEADS)
            for i, (bank, g) in enumerate(((0, ga), (4, gb))):
                taken(dve, (U_PA, U_PB)[i] + 3)
                for b in range(4):
                    v = g[:, 2 * b:2 * b + 2, :]
                    dve.tensor_tensor(v, v, ps[:, bank + b, :].rearrange("p (c t) -> p c t", c=2),
                                      ALU.mult).then_inc(pab_ev, 1)
            taken(dve, U_WO + 3)
            for k in range(8):
                ins = dve.scalar_tensor_tensor(out=h[:, k, :], in0=ps[:, k // 2, (k % 2) * T:(k % 2) * T + T],
                                               scalar=mod[:, 0, 16 + k:17 + k], in1=h[:, k, :], op0=ALU.mult,
                                               op1=ALU.add)
                if k % 2:
                    ins.then_inc(x2_done, 1)
            mod_norm(N_MOE, h, xn, 2, 0, 24)

            seq = [0]

            def step(ins):
                seq[0] += 1
                ins.then_inc(r_seq, 1)
                dve.wait_ge(r_seq, seq[0])

            s = st[:, 0, :]
            dve.wait_ge(lg_mm, 1)
            step(dve.tensor_reduce(s[:, 0:2], ps[:, 5, 0:32].rearrange("p (t e) -> p t e", t=2), AX_X, ALU.max))
            step(dve.tensor_scalar(s[:, 2:4], s[:, 0:2], -1.0, None, ALU.mult))
            dve.wait_ge(r_exp, 1)
            step(dve.reciprocal(s[:, 6:8], s[:, 4:6]))
            step(dve.tensor_tensor(aff, aff, s[:, 6:8].unsqueeze(2).to_broadcast([P, 2, EXPERTS]), ALU.mult))
            assert seq[0] == R_AFF
            dve.wait_ge(r_tr, 1)
            work = rank_work[0:EXPERTS, 0, :]
            step(dve.tensor_copy(work, ps[0:EXPERTS, 6, 0:T]))
            top = e_small[0:EXPERTS, 0, 32:40]
            for _r in range(CAP // 8):
                step(dve.max(top, work))
                step(dve.match_replace(work, top, work, -1.0))
            step(dve.tensor_scalar(rank_work[0:EXPERTS, 1, :], work, 0.0, None, ALU.is_lt))
            assert seq[0] == R_MASK
            dve.wait_ge(r_tr, 2)
            step(dve.tensor_copy(e_small[:, 1, 0:32], ps[:, 7, 0:32]))
            assert seq[0] == R_MASKT
            dve.wait_ge(r_pos, 1)
            step(dve.tensor_scalar(e_small[:, 0, 0:32], e_small[:, 1, 0:32], -1.0, 1000.0, ALU.add, ALU.mult))
            step(dve.tensor_tensor(e_small[:, 1, 32:64], e_small[:, 0, 0:32], ps[:, 5, 0:32], ALU.add))
            p4 = pick.rearrange("p t (e s) -> p (t e) s", e=EXPERTS)
            dve.tensor_tensor(p4, e_small[:, 1, 32:64].unsqueeze(2).to_broadcast([P, 32, CAP]),
                              tab("slot").unsqueeze(1).to_broadcast([P, 32, CAP]), ALU.is_equal).then_inc(pick_set, 1)
            dve.wait_ge(pick_set, 1)
            dve.tensor_tensor(wpick.rearrange("p t (e s) -> p (t e) s", e=EXPERTS), p4,
                              aff.rearrange("p t e -> p (t e)").unsqueeze(2).to_broadcast([P, 32, CAP]),
                              ALU.mult).then_inc(pick_set, 1)
            step(dve.memset(zeros_row, 0.0))
            assert seq[0] == R_ZERO

            def expert(e):
                first = isinstance(e, int)
                dve.wait_ge(e_act, e + 1)
                dve.wait_ge(e_used, e * E_UNITS + 8)
                if not first:
                    dve.wait_ge(eh_tr, e)
                dve.tensor_tensor(e_hid, e_silu, ps[:, 5, :], ALU.mult).then_inc(e_hset, 1)
                dve.wait_ge(eh_tr, e + 1)
                if not first:
                    dve.wait_ge(e_used, e * E_UNITS)
                dve.tensor_copy(e_hidT, ps[:, 7, :]).then_inc(eh_ev, 1)

            expert(0)
            with dve.Fori(1, EXPERTS) as e:
                expert(e)
            dve.wait_ge(moe_mm, EXPERTS)
            for k in range(8):
                dve.scalar_tensor_tensor(out=h[:, k, :], in0=ps[:, k // 2, (k % 2) * T:(k % 2) * T + T],
                                         scalar=mod[:, 0, 40 + k:41 + k], in1=h[:, k, :], op0=ALU.mult,
                                         op1=ALU.add).then_inc(moe_done, 1)
            inverse(N_END)
            pre(N_END, gain_of("final"))

        @block.gpsimd
        def _(pool):
            pool.memset(rel[32:33, :], NEG).then_inc(rel_set, 1)
            for u in range(8):
                pool.wait_ge(qk_rot, u + 1)
                dst = (q_r if u % 2 == 0 else k_r)[:, u // 2, :, :].rearrange("p c t -> p (c t)")
                pool.tensor_tensor(dst, rot[:, u % 2, 0, :], rot[:, u % 2, 1, :], ALU.add).then_inc(qk_done, 1)
            for u in range(8):
                pool.wait_ge(g_ev, u + 1)
                pool.wait_ge(on_ev, u // 2 + 1)
                v = o_r[:, 2 * u:2 * u + 2, :].rearrange("p c t -> p (c t)")
                pool.tensor_tensor(v, v, gs[:, u % 2, :], ALU.mult).then_inc(og_done, 1)

            def residual(n):
                for k in range(8):
                    pool.wait_ge(scaled, POST[n] + k + 1)
                    pool.tensor_tensor(h[:, k, :], h[:, k, :], xn[:, k, :], ALU.add).then_inc(h_ready, 1)

            for n in (N_POST0, N_POSTF0, N_POST1, N_POSTF1):
                residual(n)
            for b in range(4):
                pool.wait_ge(pab_ev, 4 + b + 1)
                pool.tensor_tensor(gb[:, 2 * b:2 * b + 2, :], gb[:, 2 * b:2 * b + 2, :], ga[:, 2 * b:2 * b + 2, :],
                                   ALU.add).then_inc(merged, 1)
            pool.wait_ge(pick_set, 2)
            pool.wait_ge(xe_ev, 8)

            def expert(e):
                if isinstance(e, int):
                    x, p = xe[:, :, 0:CAP], wpick[:, :, 0:CAP]
                else:
                    pool.wait_ge(ep_tr, e)
                    x, p = xe[:, :, bass.ds(e * CAP, CAP)], wpick[:, :, bass.ds(e * CAP, CAP)]
                pool.tensor_copy(xcur, x).then_inc(cur_set, 1)
                pool.tensor_copy(pcur, p.unsqueeze(2).to_broadcast([P, 2, 4, CAP])).then_inc(cur_set, 1)

            expert(0)
            with pool.Fori(1, EXPERTS) as e:
                expert(e)


def rotary_tables():
    f = np.float32
    pos = np.arange(T, dtype=f)
    theta = (f(1.0) / f(10000.0) ** np.linspace(0.0, 1.0, RET_QK // 2, dtype=f)).astype(f)
    ret = (theta[:, None] * pos[None, :]).astype(f)
    freq = (f(10000.0) ** (-np.arange(0, HD // 2, 2, dtype=f) / f(HD // 2))).astype(f)
    tok = np.arange(T)
    rows = freq[:, None] * (tok // GRID_W).astype(f)[None, :]
    cols_ = freq[:, None] * (tok % GRID_W).astype(f)[None, :]
    rope = np.tile(np.concatenate([rows, rows, cols_, cols_], axis=0), (2, 1)).astype(f)
    return ret, rope


def shape_tables():
    f = np.float32
    ret, rope = rotary_tables()
    perm = np.zeros((P, P), f)
    for m in range(P):
        perm[m + 16 if m % 32 < 16 else m - 16, m] = -1.0 if m % 32 < 16 else 1.0
    p = np.arange(P)
    tok, key = np.arange(T).reshape(2, P).T, np.arange(T)
    band = np.where(np.abs(key[None, None, :] - tok[:, :, None]) <= WINDOW, f(0.0), f(NEG)).reshape(P, 2 * T)
    parts = {"ident": np.eye(P), "perm": perm, "tri": p[:, None] < p[None, :],
             "slot": np.tile(np.arange(CAP), (P, 1)), "ret_cos": np.cos(ret), "ret_sin": np.sin(ret),
             "ret_nsin": -np.sin(ret), "rope_cos": np.cos(rope), "rope_sin": np.sin(rope), "band": band}
    return np.concatenate([parts[n].astype(f) for n in TABS], axis=1)


def decay_table():
    log_gamma = np.log(1.0 - 2.0 ** (-5.0 - np.arange(RET_HEADS)))
    rel = np.arange(T)[None, :] - np.arange(P)[:, None]
    one = [np.where(rel >= 0, np.exp(np.maximum(rel, 0) * g), 0.0) * RET_QK ** -0.5 for g in log_gamma]
    return np.concatenate([np.concatenate([m, m[:, :P]], axis=1) for m in one], axis=1).astype(np.float32)


def bucket_table(dist):
    f = np.float32
    half = BUCKETS // 2
    n = np.maximum(dist, 0)
    nf = np.maximum(n, 1).astype(f)
    large = half + (np.log(nf / f(half)) / f(np.log(MAX_DIST / half)) * f(BUCKETS - half)).astype(np.int32)
    bucket = np.where(n < half, n, np.minimum(large, BUCKETS - 1))
    bucket = np.where(dist >= 0, bucket, BUCKETS)
    return (np.arange(BUCKETS + 1)[:, None] == bucket.reshape(1, -1)).astype(f)


def kernel(**inputs):
    import concourse.bacc as bacc
    from concourse.bass_utils import run_bass_kernel_spmd

    x = {n: np.asarray(v) for n, v in inputs.items()}

    def by_chunk(v):
        return v.reshape(-1, P).T

    def pairs(pe):
        return pe.reshape(CMP_LEN // 2, 2 * HD).T

    small = {"mix_pre0": x["mix_norm_pre"][0], "mix_pre1": x["mix_norm_pre"][1], "mix_post0": x["mix_norm_post"][0],
             "mix_post1": x["mix_norm_post"][1], "ffn_pre0": x["ffn_norm_pre"][0], "ffn_pre1": x["ffn_norm_pre"][1],
             "ffn_post0": x["ffn_norm_post"][0], "ffn_post1": x["ffn_norm_post"][1], "kv_norm": x["kv_norm"],
             "norm1": x["norm1_g_2"], "norm2": x["norm2_g_2"], "final": x["final_g_2"], "b_ada": x["b_ada_2"],
             "b_merge": x["b_merge_gate_2"], "c": x["c_2"], "c_ctx": x["c_ctx_2"]}
    columns = [by_chunk(small[n]) if n in small else pairs(x["cmp_" + n]) for n in COLS]
    tok = np.arange(P)[None, :]
    cmp_dist = np.concatenate([(P * t + tok - (CMP_STRIDE * n + CMP_LEN - 1)) for t in range(2) for n in range(N_CMP)])
    arrays = {
        "xT": x["x"][0].T, "ctxT": x["ctx_2"][0].T, "cols": np.concatenate(columns, axis=1),
        "tabs": shape_tables(), "decay": decay_table(), "bucket_rows": bucket_table(T - 1 - np.arange(384)),
        "bucket_cmp": bucket_table(cmp_dist), "rel_bias": x["rel_bias"],
        "ret_w_in": x["ret_w_in"][0], "ret_w_out": x["ret_w_out"][0],
        "ffn_w_in0": x["ffn_w_in"][0], "ffn_w_in1": x["ffn_w_in"][1],
        "ffn_w_out0": x["ffn_w_out"][0], "ffn_w_out1": x["ffn_w_out"][1], "kv_w": x["kv_w"],
        "cmp_w1_k": x["cmp_w1_k"], "cmp_w1_v": x["cmp_w1_v"], "cmp_w2_k": x["cmp_w2_k"], "cmp_w2_v": x["cmp_w2_v"],
        "nsa_w_in": x["nsa_w_in"][0], "nsa_w_out": x["nsa_w_out"][0], "w_ada_2": x["w_ada_2"][0],
        "w_in_2": x["w_in_2"][0], "gmlp_ln_g_2": x["gmlp_ln_g_2"][0], "gmlp_ln_b_2": x["gmlp_ln_b_2"][0],
        "w_spatialT": x["w_spatial_2"][0].transpose(2, 0, 1), "b_spatial_2": x["b_spatial_2"][0],
        "attn_sink_2": x["attn_sink_2"][0], "w_proj_a_2": x["w_proj_a_2"][0], "w_proj_b_2": x["w_proj_b_2"][0],
        "w_out_2": x["w_out_2"][0], "w_router_2": x["w_router_2"][0], "w_exp_gate_2": x["w_exp_gate_2"][0],
        "w_exp_up_2": x["w_exp_up_2"][0], "w_exp_down_2": x["w_exp_down_2"][0],
    }
    arrays = {n: np.ascontiguousarray(v) for n, v in arrays.items()}
    nc = bacc.Bacc("TRN2", target_bir_lowering=False, num_devices=1, dynamic_dma_scratch_size=4096)
    aps = {n: nc.dram_tensor("in_" + n, v.shape, mybir.dt.from_np(v.dtype), kind="ExternalInput").ap()
           for n, v in arrays.items()}
    out = nc.dram_tensor("outT", (D, T), F32, kind="ExternalOutput").ap()
    program(nc, aps, out)
    r = run_bass_kernel_spmd(nc, [{"in_" + n: v for n, v in arrays.items()}], core_ids=[0])
    return np.ascontiguousarray(r.results[0]["outT"].T).reshape(1, T, D)
```

```python
from contextlib import ExitStack

import numpy as np

import concourse.bass as bass
from concourse import mybir

F32 = mybir.dt.float32
F32R = mybir.dt.float32r
ALU = mybir.AluOpType
ACT = mybir.ActivationFunctionType
AX_X = mybir.AxisListType.X

P = 128
D = 1024
T = 256
DC = D // P
EPS = 1e-6

RET_HEADS = 4
RET_QK = D // RET_HEADS
RET_V = 2 * D // RET_HEADS
HID = ((8 * D + 3 * 256 - 1) // (3 * 256)) * 256
PAIRS = HID // 256

HEADS = 16
GROUPS = 4
HD = 64
CMP_LEN, CMP_STRIDE = 32, 16
N_CMP = (T - CMP_LEN) // CMP_STRIDE + 1
BUCKETS, MAX_DIST = 32, 128
NEG = -1e30
LEAST = 1e20
TINY = float(np.finfo(np.float32).tiny)

A_GROUPS = 8
EXPERTS = 16
CAP = 2 * T // EXPERTS
DE = 2048
WINDOW = 128
GRID_W = 64
IN2 = 5632

UNIT = 2048
RING = 3
EUNIT = 4096
ERING = 3
E_UNITS = 12

U_RET = 0
U_RO = U_RET + 48
U_F0 = U_RO + 8
U_KV = U_F0 + 3 * PAIRS
U_W1 = U_KV + 6
U_NQ = U_W1 + 4
U_NO = U_NQ + 4
U_F1 = U_NO + 4
U_IN2 = U_F1 + 3 * PAIRS
U_PA = U_IN2 + IN2 // 256
U_PB = U_PA + 4
U_WO = U_PB + 4
U_END = U_WO + 4

WHOLE = set(range(U_RET + 1, U_RO, 2)) | set(range(U_W1, U_NQ)) | {U_IN2 + 12, U_IN2 + 13}
SPLIT_UNITS = [U for U in range(U_END) if U not in WHOLE]
SPLIT_NO = {U: i for i, U in enumerate(SPLIT_UNITS)}

COLS = {}
_at = 0
for _name, _n in [("mix_pre0", 8), ("mix_pre1", 8), ("mix_post0", 8), ("mix_post1", 8), ("ffn_pre0", 8),
                  ("ffn_pre1", 8), ("ffn_post0", 8), ("ffn_post1", 8), ("kv_norm", 8), ("norm1", 8),
                  ("norm2", 8), ("final", 8), ("b_ada", 48), ("b_merge", 16), ("c", 8), ("c_ctx", 8),
                  ("pe_k", 16), ("pe_v", 16)]:
    COLS[_name] = (_at, _n)
    _at += _n
N_COLS = _at

TABS = {}
_at = 0
for _name, _n in [("ident", 128), ("perm", 128), ("tri", 128), ("slot", 32), ("ret_cos", T), ("ret_sin", T),
                  ("ret_nsin", T), ("rope_cos", T), ("rope_sin", T), ("band", 2 * T)]:
    TABS[_name] = (_at, _n)
    _at += _n
N_TABS = _at
N_DECAY = RET_HEADS * 384

(N_PRE0, N_POST0, N_PREF0, N_POSTF0, N_PRE1, N_POST1, N_CTX, N_PREF1, N_POSTF1, N_IN2, N_MOE, N_END) = range(12)
XN = {N_PRE0: 0, N_PREF0: 8, N_PRE1: 16, N_CTX: 32, N_PREF1: 40, N_IN2: 48, N_MOE: 56, N_END: 64}
XN_END = 72
X_RET, X_RO, X_F0, X_KV, X_NQ, X_NO, X_F1, X_IN2 = 0, 8, 16, 24, 32, 40, 44, 52
X_PA, X_PB, X_WO = 60, 64, 68
POST = {N_POST0: 0, N_POSTF0: 8, N_POST1: 16, N_POSTF1: 24}
MODP = {N_CTX: 0, N_IN2: 8, N_MOE: 16}

FIRST_IN, REST_IN = 4 * 16, 6 * 16
LN_END = 6
R_AFF, R_MASK, R_MASKT, R_ZERO = 4, 6 + 2 * (CAP // 8), 7 + 2 * (CAP // 8), 10 + 2 * (CAP // 8)
IN2_ORDER = [4, 5, 6, 7, 0, 1, 2, 3] + list(range(8, 22))


def program(nc, a, out):
    ctx = ExitStack()
    with ctx:
        def sb(name, shape, dtype=F32):
            return ctx.enter_context(nc.sbuf_tensor(name, shape, dtype))

        def sem(name):
            return ctx.enter_context(nc.semaphore(name))

        ring = sb("dense_ring", [P, RING, UNIT])
        ering = sb("expert_ring", [P, ERING - 1, EUNIT])
        w_hi = sb("weights_hi", [P, 2, UNIT], F32R)
        w_lo = sb("weights_lo", [P, 2, UNIT], F32R)
        x_hi = sb("tokens_hi", [P, DC, T], F32R)
        x_lo = sb("tokens_lo", [P, DC, T], F32R)
        f_hi = sb("hidden_hi", [P, 2, T], F32R)
        f_lo = sb("hidden_lo", [P, 2, T], F32R)
        h = sb("residual", [P, DC, T])
        xn = sb("normed", [P, DC, T])
        sq = sb("squares", [P, DC, T])
        cols = sb("cols", [P, N_COLS])
        tabs = sb("tabs", [P, N_TABS])
        ones = sb("ones", [P, P])
        cs = sb("cond_silu", [P, DC, 32])
        root = sb("root", [P, T])
        rs = sb("inv_root", [P, T])
        ada_rows = sb("ada_rows", [P, 512])
        mod = sb("mod", [P, 2, 48])
        gain = sb("mod_gain", [P, 3, DC])
        vw_tok = sb("window_values", [P, 4, T])
        early = vw_tok[:].rearrange("p k t -> p (k t)")
        w_gate = early[:, 0:384].rearrange("p (k n) -> p k n", k=DC)
        w2k = early[:, 384:640].rearrange("p (c r d) -> p c r d", c=2, r=2)
        vc = early[0:N_CMP, 640:896].rearrange("p (g d) -> p g d", g=GROUPS)
        kc = early[:, 896:896 + GROUPS * N_CMP].rearrange("p (g n) -> p g n", g=GROUPS)
        w2v = sb("cmp_w2_v", [P, 2, HD])
        w_router = sb("router_w", [P, DC, EXPERTS])
        rel = sb("rel_ext", [33, HEADS])
        cbias = sb("cmp_bias", [P, HEADS, 2, N_CMP])
        gates = sb("nsa_gates", [P, 2, 48])
        sink = sb("sink", [P, HEADS])
        st = sb("softmax_stats", [P, 3, 32])
        ARENA = 62 * 256
        arena = sb("arena", [P, ARENA])
        ps = ctx.enter_context(nc.psum_tensor("ps", [P, 8, 512], F32))
        bias_dram = nc.dram_tensor("bias_skew", (HEADS, P, 384), F32).ap()

        def at(kb, *dims):
            n = int(np.prod(dims))
            o = int(kb * 256)
            assert o + n <= ARENA, (kb, dims)
            v = arena[:, o:o + n]
            if len(dims) == 1:
                return v
            names = "abcd"[:len(dims)]
            return v.rearrange(f"p ({' '.join(names)}) -> p {' '.join(names)}", **dict(zip(names, dims)))

        def col(name, k=None):
            o, n = COLS[name]
            return cols[:, o:o + n] if k is None else cols[:, o + k:o + k + 1]

        def tab(name):
            o, n = TABS[name]
            return tabs[:, o:o + n]

        ident = tab("ident")

        spare = xn[:].rearrange("p k t -> p (k t)")

        q_r = at(0, RET_HEADS, 2, T)
        k_r = at(8, RET_HEADS, 2, T)
        v_r = at(16, 2, RET_HEADS * RET_V)
        o_r = at(32, 16, T)
        bucket_cmp = at(32, 30 * P)
        bucket_rows = at(16, 384)[0:33, :]
        bias_rows = at(18, 384)[0:HEADS, :]
        rot = at(48, 2, 2, 512)
        sT = at(48, 2, 384)
        gs = at(52, 2, 512)
        decay = at(56, RET_HEADS, 384)
        f_silu = at(0, 2, 512)
        f_hid = at(4, 2, 512)
        bias = at(8, HEADS, T)
        kv_raw = at(24, 4, 2, T)
        o_n = at(24, DC, T)
        shifted = at(32, 2, GROUPS, T)
        blocks = at(40, 2, 16, GROUPS * N_CMP)
        kd = at(48, 2, GROUPS, T)
        v_n = at(56, 2, 2, T)
        q_n = at(0, DC, T)
        cmp_hid = at(60, 512)
        n_s = [at(32, 800), at(35.25, 800), spare[:, 0:800]]
        n_pT = at(38.5, 2, 2, 384)
        n_pc = at(44.5, 2, T)
        hidT = ada_rows
        ctxn = at(48, DC, T)
        o_w = at(0, DC, T)
        va = at(8, 2, D)
        ln_g = at(16, D)
        ln_b = at(20, D)
        ga = at(8, DC, T)
        gb = at(16, DC, T)
        ws = at(24, A_GROUPS, P)
        bs = at(28, A_GROUPS, P)
        w_s = [at(24, 2, 512), at(28, 2, 512), spare[:, 0:1024].rearrange("p (t j) -> p t j", t=2)]
        ya = at(32, DC, T)
        q_w = at(40, DC, T)
        kd2 = at(48, GROUPS, 2, T)
        kw_raw = at(56, 2, 512)
        rot2 = at(60, 512)
        h2 = at(0, 2, D)
        pick = at(8, 2, EXPERTS * CAP)
        wpick = at(12, 2, EXPERTS * CAP)
        xe = at(16, DC, EXPERTS * CAP)
        xcur = at(32, DC, CAP)
        pcur = at(33, 2, 4, CAP)
        e_silu = at(34, 512)
        e_hid = at(36, 512)
        e_hidT = at(38, 512)
        e_y = at(40, 512)
        e_pT = at(42, T)
        aff = at(43, 2, EXPERTS)
        e_small = at(44, 2, 64)
        rank_work = at(45, 2, T)

        landed = [sem(f"dense_landed{i}") for i in range(RING)]
        used = sem("dense_used")
        hi_ready = sem("weights_hi_ready")
        lo_ready = sem("weights_lo_ready")
        xhi_ready = sem("tokens_hi_ready")
        xlo_ready = sem("tokens_lo_ready")
        fhi_ready = sem("hidden_hi_ready")
        flo_ready = sem("hidden_lo_ready")
        e_landed = [sem(f"expert_landed{i}") for i in range(ERING)]
        e_used = sem("expert_used")
        x_in = sem("x_in")
        cols_in = sem("cols_in")
        first_in = sem("first_in")
        rest_in = sem("rest_in")
        decay_in = sem("decay_in")
        bias_out = sem("bias_out")
        bias_in = sem("bias_in")
        ones_set = sem("ones_set")
        cs_set = sem("cs_set")
        rel_set = sem("rel_set")
        brow_mm = sem("brow_mm")
        brow_ev = sem("brow_ev")
        cbias_ev = sem("cbias_ev")
        sq_ready = sem("sq_ready")
        ss_ready = sem("ss_ready")
        root_ready = sem("root_ready")
        rs_ready = sem("rs_ready")
        xn_ready = sem("xn_ready")
        scaled = sem("post_scaled")
        h_ready = sem("h_ready")
        ada_ev = sem("ada_ev")
        ada_tr = sem("ada_tr")
        ada_mod = sem("ada_mod")
        gains_set = sem("gains_set")
        qk_rot = sem("qk_rot")
        qk_done = sem("qk_done")
        v_mm = sem("v_mm")
        v_ev = sem("v_ev")
        g_mm = sem("g_mm")
        g_ev = sem("g_ev")
        og_done = sem("og_done")
        sc_mm = sem("sc_mm")
        sc_ev = sem("sc_ev")
        o_mm = sem("o_mm")
        osq = sem("osq")
        oss = sem("oss")
        oroot = sem("oroot")
        ors = sem("ors")
        on_ev = sem("on_ev")
        f_act = sem("f_act")
        f_hidden = sem("f_hidden")
        kv_ev = sem("kv_ev")
        shift_in = sem("shift_in")
        kd_in = sem("kd_in")
        blocks_set = sem("blocks_set")
        c_mm = sem("c_mm")
        c_act = sem("c_act")
        c_tr = sem("c_tr")
        c_trev = sem("c_trev")
        c_kv = sem("c_kv")
        c_kvev = sem("c_kvev")
        nq_mm = sem("nq_mm")
        nq_ev = sem("nq_ev")
        s_mm = sem("s_mm")
        s_add = sem("s_add")
        s_max = sem("s_max")
        s_neg = sem("s_neg")
        s_exp = sem("s_exp")
        s_sum = sem("s_sum")
        s_inv = sem("s_inv")
        s_fac = sem("s_fac")
        s_p = sem("s_p")
        s_tr = sem("s_tr")
        s_trev = sem("s_trev")
        s_trev2 = sem("s_trev2")
        s_pv = sem("s_pv")
        s_ov = sem("s_ov")
        ctx_in = sem("ctx_in")
        mod_scaled = sem("mod_scaled")
        w_sum = sem("w_sum")
        ln_root = sem("ln_root")
        ln_in = sem("ln_in")
        va_ev = sem("va_ev")
        ln_seq = sem("ln_seq")
        ua_ev = sem("ua_ev")
        sp_mm = sem("sp_mm")
        sp_add = sem("sp_add")
        ya_done = sem("ya_done")
        qw_ev = sem("qw_ev")
        kw_mm = sem("kw_mm")
        qp_mm = sem("qp_mm")
        q_cos = sem("q_cos")
        q_sin = sem("q_sin")
        q_rot = sem("q_rot")
        vw_mm = sem("vw_mm")
        vw_ev = sem("vw_ev")
        kd2_in = sem("kd2_in")
        gt_ev = sem("gt_ev")
        pab_ev = sem("pab_ev")
        merged = sem("merged")
        x2_done = sem("x2_done")
        tok_mm = sem("tok_mm")
        tok_ev = sem("tok_ev")
        lg_mm = sem("lg_mm")
        r_seq = sem("router_seq")
        r_exp = sem("router_exp")
        r_tr = sem("router_tr")
        r_pos = sem("router_pos")
        pick_set = sem("pick_set")
        xe_mm = sem("xe_mm")
        xe_ev = sem("xe_ev")
        cur_set = sem("cur_set")
        e_act = sem("e_act")
        e_hset = sem("e_hset")
        ep_tr = sem("ep_tr")
        ep_ev = sem("ep_ev")
        eh_tr = sem("eh_tr")
        eh_ev = sem("eh_ev")
        ed_ev = sem("ed_ev")
        moe_mm = sem("moe_mm")
        moe_done = sem("moe_done")
        out_done = sem("out_done")

        block = ctx.enter_context(nc.Block())

        def col_src(w, n0):
            return w.rearrange("(k p) n -> p k n", p=P)[:, :, n0:n0 + 256] if isinstance(n0, int) else \
                w.rearrange("(k p) n -> p k n", p=P)[:, :, bass.ds(n0, 256)]

        def row_src(w, u):
            v = w.rearrange("(c p) n -> p c n", p=P)
            return v[:, 2 * u:2 * u + 2, :] if isinstance(u, int) else v[:, bass.ds(u * 2, 2), :]

        def slot8(U):
            return ring[:, U % RING, :].rearrange("p (k n) -> p k n", k=8)

        def slot2(U):
            return ring[:, U % RING, :].rearrange("p (c n) -> p c n", c=2)

        def eslot(w, c):
            v = ering[:, w % ERING, :] if w % ERING < ERING - 1 else ring[:, 0:2, :].rearrange("p u n -> p (u n)")
            return v.rearrange("p (c n) -> p c n", c=c)

        def parts_of(U):
            b = SPLIT_NO[U] % 2
            return [w[:, b, :].rearrange("p (k n) -> p k n", k=8) for w in (w_hi, w_lo)]

        @block.sync
        def _(sp):
            def load(U, src, k, round_=0):
                dst = slot8(U) if k == 8 else slot2(U) if k == 2 else ring[:, U % RING, :]
                V = U - RING
                if V in WHOLE:
                    sp.wait_ge(used, V + 1 + round_ * 6)
                elif V >= 0:
                    sp.wait_ge(lo_ready, 2 * SPLIT_NO[V] + 2 + round_ * 12)
                sp.dma_start(dst, src).then_inc(landed[U % RING], 16)

            w_in = a["ret_w_in"]
            order = [c for hd in range(4) for c in (hd, 4 + hd)] + list(range(8, 24))
            ada_v = a["w_ada_2"].rearrange("(k p) n -> p k n", p=P)

            def load_expert(e, w):
                u = w % 4
                if w < 8:
                    src = a["w_exp_gate_2" if w < 4 else "w_exp_up_2"][e].rearrange("(c p) n -> p c n", p=P)
                    src = src[:, 2 * u:2 * u + 2, :]
                    dst = eslot(w, 2)
                else:
                    src = a["w_exp_down_2"][e].rearrange("(c p) n -> p c n", p=P)[:, 4 * u:4 * u + 4, :]
                    dst = eslot(w, 4)
                sp.dma_start(dst, src).then_inc(e_landed[w % ERING], 16)

            for u in range(24):
                load(2 * u, col_src(w_in, 256 * order[u]), 8)
                load(2 * u + 1, ada_v[:, u % 8, 2048 * (u // 8):2048 * (u // 8) + 2048], 0)
            for u in range(8):
                load(U_RO + u, row_src(a["ret_w_out"], u), 2)
                if u in (3, 6):
                    load_expert(0, u // 4)

            def ffn(f, U0):
                w1, w2 = a[f"ffn_w_in{f}"], a[f"ffn_w_out{f}"]

                def gu(U, j, r=0):
                    load(U, col_src(w1, j * 256), 8, r)
                    load(U + 1, col_src(w1, j * 256 + HID), 8, r)

                gu(U0, 0)
                gu(U0 + 2, 1)
                load(U0 + 4, row_src(w2, 0), 2)
                with sp.Fori(0, (PAIRS - 3) // 2) as i:
                    for c in range(2):
                        gu(U0 + 5 + 3 * c, i * 2 + (2 + c), i)
                        load(U0 + 7 + 3 * c, row_src(w2, i * 2 + (1 + c)), 2, i)
                gu(U0 + 29, 10)
                load(U0 + 31, row_src(w2, 9), 2)
                load(U0 + 32, row_src(w2, 10), 2)

            ffn(0, U_F0)
            for u, c in enumerate((0, 1, 2, 4, 3, 5)):
                load(U_KV + u, col_src(a["kv_w"], 256 * c), 8)
            for kind, w in enumerate(("cmp_w1_k", "cmp_w1_v")):
                v = a[w].rearrange("(c p) n -> p c n", p=P)
                for u in range(2):
                    load(U_W1 + 2 * kind + u, v[:, 8 * u:8 * u + 8, :], 8)
            for u in range(4):
                load(U_NQ + u, col_src(a["nsa_w_in"], 256 * u), 8)
            for u in range(4):
                load(U_NO + u, row_src(a["nsa_w_out"], u), 2)
            ffn(1, U_F1)
            for u, c in enumerate(IN2_ORDER):
                load(U_IN2 + u, col_src(a["w_in_2"], 256 * c), 8)
            for U0, w in ((U_PA, "w_proj_a_2"), (U_PB, "w_proj_b_2"), (U_WO, "w_out_2")):
                for u in range(4):
                    load(U0 + u, row_src(a[w], u), 2)
            for w in range(ERING - 1, E_UNITS):
                if w < ERING:
                    sp.wait_ge(lo_ready, 2 * len(SPLIT_UNITS))
                else:
                    sp.wait_ge(e_used, w - ERING + 1)
                load_expert(0, w)
            with sp.Fori(1, EXPERTS) as e:
                for w in range(E_UNITS):
                    sp.wait_ge(e_used, e * E_UNITS + (w - ERING + 1))
                    load_expert(e, w)
            sp.wait_ge(xn_ready, XN_END)
            sp.dma_start(out.rearrange("(k p) t -> p k t", p=P), xn[:]).then_inc(out_done, 16)
            sp.wait_ge(out_done, 16)

        def taken(eng, U, r=0):
            eng.wait_ge(used, r * 6 + (U + 1) if not isinstance(r, int) else U + 1)

        def split_hi(act, U, r=0):
            n = SPLIT_NO[U]
            act.wait_ge(landed[U % RING], r * (96 // RING) + 16 * (U // RING + 1))
            if n >= 2:
                taken(act, SPLIT_UNITS[n - 2], r)
            for q in range(2):
                c = slice(q * UNIT // 2, (q + 1) * UNIT // 2)
                act.activation(w_hi[:, n % 2, c], ring[:, U % RING, c], ACT.Copy).then_inc(hi_ready, 1)

        def split_lo(dve, U, r=0):
            n = SPLIT_NO[U]
            for q in range(2):
                c = slice(q * UNIT // 2, (q + 1) * UNIT // 2)
                dve.wait_ge(hi_ready, r * 12 + (2 * n + q + 1))
                dve.tensor_tensor(w_lo[:, n % 2, c], ring[:, U % RING, c], w_hi[:, n % 2, c],
                                  ALU.subtract).then_inc(lo_ready, 1)

        def pair_hi(act, u, src):
            act.activation(x_hi[:, 2 * (u % 4):2 * (u % 4) + 2, :], src, ACT.Copy).then_inc(xhi_ready, 1)

        def pair_lo(dve, x0, u, src):
            dve.wait_ge(xhi_ready, x0 + u + 1)
            c = slice(2 * (u % 4), 2 * (u % 4) + 2)
            dve.tensor_tensor(x_lo[:, c, :], src, x_hi[:, c, :], ALU.subtract).then_inc(xlo_ready, 1)

        def two_chunks(v, u):
            return v[:, 2 * u:2 * u + 2, :]

        def split_tokens_hi(act, src, ready):
            for k in range(DC):
                act.wait_ge(xn_ready, ready + k + 1)
                act.activation(x_hi[:, k, :], src[:, k, :], ACT.Copy).then_inc(xhi_ready, 1)

        def token_lo(dve, x0, src, k):
            dve.wait_ge(xhi_ready, x0 + k + 1)
            dve.tensor_tensor(x_lo[:, k, :], src[:, k, :], x_hi[:, k, :], ALU.subtract).then_inc(xlo_ready, 1)

        def w_pT(hd):
            return sq[:, 4 * (hd % 2):4 * (hd % 2) + 4, :]

        zeros_row = e_y

        def gate_unit(f, j):
            U0 = (U_F0, U_F1)[f]
            return U0 + (2 * j if j < 2 else 3 * j - 1)

        def out_unit(f, j):
            U0 = (U_F0, U_F1)[f]
            return U0 + (3 * j + 4 if j < PAIRS - 1 else 3 * PAIRS - 1)

        def hidden_of(j):
            return f_hid[:, j % 2, :].rearrange("p (c t) -> p c t", c=2)

        def head_parts(hd):
            return slice(64 * (hd % 2), 64 * (hd % 2) + 64), hd // 2, hd // (HEADS // GROUPS)

        @block.tensor
        def _(pe):
            def take(U, r=0):
                pe.wait_ge(landed[U % RING], r * (96 // RING) + 16 * (U // RING + 1))

            def norm(n):
                for q in range(4):
                    pe.wait_ge(sq_ready, 4 * n + q + 1)
                    for c in (2 * q, 2 * q + 1):
                        mm = pe.matmul(ps[:, 4, 0:T], ones[:], sq[:, c, :], start=c == 0, stop=c == 7)
                mm.then_inc(ss_ready, 1)

            def col_products(U, bank, place, r=0, x0=None):
                n = SPLIT_NO[U]
                hi, lo = parts_of(U)
                for b in range(2):
                    for k in range(8):
                        if b == 0 and k % 4 == 0:
                            pe.wait_ge(lo_ready, r * 12 + (2 * n + k // 4 + 1))
                        if b == 0 and x0 is not None:
                            pe.wait_ge(xlo_ready, x0 + k + 1)
                        for i, (w, x) in enumerate(((hi, x_hi), (hi, x_lo), (lo, x_hi))):
                            left, right = place(b, w[:, k, :], x[:, k, :])
                            mm = pe.matmul(ps[:, bank, b * T:b * T + T], left, right,
                                           start=k == 0 and i == 0, stop=k == 7 and i == 2)
                mm.then_inc(used, 1)

            def col_T(U, bank, r=0, x0=None):
                col_products(U, bank, lambda b, w, x: (w[:, b * P:b * P + P], x), r, x0)

            def col_tok(U, bank, x0=None):
                col_products(U, bank, lambda b, w, x: (x[:, b * P:b * P + P], w), 0, x0)

            def row_T(U, x, bank0, first, last, r=0):
                n = SPLIT_NO[U]
                hi, lo = [w.rearrange("p k n -> p (k n)").rearrange("p (c n) -> p c n", c=2) for w in parts_of(U)]
                pe.wait_ge(lo_ready, r * 12 + (2 * n + 2))
                for b in range(8):
                    for c in range(2):
                        for i, (w, v) in enumerate(((hi, x[0]), (hi, x[1]), (lo, x[0]))):
                            mm = pe.matmul(ps[:, bank0 + b // 2, (b % 2) * T:(b % 2) * T + T],
                                           w[:, c, b * P:b * P + P], v[:, c, :],
                                           start=first and c == 0 and i == 0 and b % 2 == 0,
                                           stop=last and c == 1 and i == 2, skip_group_check=True)
                mm.then_inc(used, 1)

            def row_pair(U0, u, n, x0, bank0):
                pe.wait_ge(xlo_ready, x0 + u + 1)
                row_T(U0 + u, [two_chunks(v, u % 4) for v in (x_hi, x_lo)], bank0, u == 0, u == n - 1)

            pe.wait_ge(ones_set, 1)
            norm(N_PRE0)
            pe.wait_ge(first_in, FIRST_IN)
            pe.wait_ge(rel_set, 1)
            pe.matmul(ps[0:HEADS, 0, 0:384], rel[:], bucket_rows, start=True, stop=True).then_inc(brow_mm, 1)
            for i in range(30):
                mm = pe.matmul(ps[:, 1, i * HEADS:(i + 1) * HEADS], bucket_cmp[0:33, i * P:(i + 1) * P], rel[:],
                               start=True, stop=True)
            mm.then_inc(brow_mm, 1)
            pe.wait_ge(cs_set, 2)

            def ada(u):
                U = U_RET + 2 * u + 1
                take(U)
                k = u % 8
                if u >= 8 and k == 0:
                    pe.wait_ge(ada_mod, u // 8)
                for j in range(4):
                    mm = pe.matmul(ps[32 * j:32 * j + 32, 6, :], cs[:, k, :], ring[:, U % RING, 512 * j:512 * j + 512],
                                   start=k == 0, stop=k == 7)
                mm.then_inc(used, 1)

            def ada_turn(r):
                pe.wait_ge(ada_ev, r + 1)
                for m in range(4):
                    mm = pe.transpose(ps[:, 6, m * P:m * P + P], ada_rows[:, m * P:m * P + P], ident)
                mm.then_inc(ada_tr, 1)

            for u in range(8):
                if u >= 2:
                    pe.wait_ge(qk_rot, u - 1)
                col_products(U_RET + 2 * u, 5 + 2 * (u % 2), lambda b, w, x: (w[:, b::2], x),
                             x0=X_RET if u == 0 else None)
                ada(u)
            for u in range(8):
                pe.wait_ge(*((v_ev, u - 1) if u >= 2 else (qk_rot, 7 + u)))
                col_tok(U_RET + 16 + 2 * u, 5 + 2 * (u % 2))
                if u == 0:
                    ada_turn(0)
                ada(8 + u)

            def g_unit(u):
                pe.wait_ge(*((g_ev, u - 1) if u >= 2 else (v_ev, 7 + u)))
                col_T(U_RET + 32 + 2 * u, 5 + 2 * (u % 2))
                if u == 0:
                    ada_turn(1)
                ada(16 + u)

            def scores(hd):
                pe.wait_ge(qk_done, 2 * hd + 2)
                if hd >= 2:
                    pe.wait_ge(sc_ev, hd - 1)
                b = hd % 2
                for c in range(2):
                    pe.matmul(ps[:, b, 0:T], k_r[:, hd, c, 0:P], q_r[:, hd, c, :], start=c == 0, stop=c == 1)
                for c in range(2):
                    mm = pe.matmul(ps[:, b, T:T + P], k_r[:, hd, c, P:T], q_r[:, hd, c, P:T],
                                   start=c == 0, stop=c == 1)
                mm.then_inc(sc_mm, 1)

            pe.wait_ge(brow_ev, 1)
            pe.wait_ge(cbias_ev, 1)
            scores(0)
            for hd in range(RET_HEADS):
                g_unit(2 * hd)
                pe.wait_ge(sc_ev, hd + 1)
                pe.wait_ge(v_ev, 8)
                if hd:
                    pe.wait_ge(on_ev, hd)
                for e in range(4):
                    o = ps[:, 2 + e // 2, (e % 2) * T:(e % 2) * T + T]
                    c0 = hd * RET_V + e * P
                    pe.matmul(o, v_r[:, 0, c0:c0 + P], sT[:, hd % 2, 0:T], start=e % 2 == 0, stop=False,
                              skip_group_check=True)
                    mm = pe.matmul(o[:, P:T], v_r[:, 1, c0:c0 + P], sT[:, hd % 2, T:T + P], start=False, stop=True,
                                   skip_group_check=True)
                mm.then_inc(o_mm, 1)
                g_unit(2 * hd + 1)
                if hd + 1 < RET_HEADS:
                    scores(hd + 1)
                pe.wait_ge(osq, hd + 1)
                for e in range(4):
                    mm = pe.matmul(ps[:, 4, 0:T], ones[:], sq[:, e, :], start=e == 0, stop=e == 3)
                mm.then_inc(oss, 1)
            ada_turn(2)

            pe.wait_ge(on_ev, 4)
            for u in range(8):
                row_pair(U_RO, u, 8, X_RO, 0)
            norm(N_POST0)
            norm(N_PREF0)

            def ffn(f, U0, x0):
                base = f * PAIRS

                def gu(U, j, r=0, x0=None):
                    b = j % 2
                    if j >= 2:
                        pe.wait_ge(f_act, r * 2 + (base + j - 1))
                    col_T(U, 4 + 2 * b, r, x0)
                    if j >= 2:
                        pe.wait_ge(f_hidden, r * 2 + (base + j - 1))
                    col_T(U + 1, 5 + 2 * b, r)

                def o(U, j, r=0, first=False, last=False):
                    pe.wait_ge(flo_ready, r * 2 + (base + j + 1))
                    row_T(U, (f_hi, f_lo), 0, first, last, r)

                gu(U0, 0, 0, x0)
                gu(U0 + 2, 1)
                o(U0 + 4, 0, first=True)
                with pe.Fori(0, (PAIRS - 3) // 2) as i:
                    for c in range(2):
                        gu(U0 + 5 + 3 * c, 2 + c, i)
                        o(U0 + 7 + 3 * c, 1 + c, i)
                gu(U0 + 29, 10)
                o(U0 + 31, 9)
                o(U0 + 32, 10, last=True)

            ffn(0, U_F0, X_F0)
            norm(N_POSTF0)
            norm(N_PRE1)

            for u in range(6):
                if u >= 2:
                    pe.wait_ge(kv_ev, u - 1)
                unit = col_T if u < 4 else col_tok
                unit(U_KV + u, 5 + 2 * (u % 2), x0=X_KV if u == 0 else None)
            for u in range(4):
                pe.wait_ge(*((nq_ev, u - 1) if u >= 2 else (kv_ev, 5 + u)))
                if u == 0:
                    pe.wait_ge(blocks_set, 4)
                    for kind in range(2):
                        for w in range(2):
                            U = U_W1 + 2 * kind + w
                            take(U)
                            for c in range(8):
                                mm = pe.matmul(ps[0:60, kind, 0:T], blocks[:, kind, 8 * w + c, :], slot8(U)[:, c, :],
                                               start=w == 0 and c == 0, stop=w == 1 and c == 7)
                            mm.then_inc(used, 1)
                col_T(U_NQ + u, 5 + 2 * (u % 2), x0=X_NQ if u == 0 else None)
                if u == 1:
                    pe.wait_ge(c_act, 2)
                    for kind in range(2):
                        for c in range(2):
                            o = (2 * kind + c) * 60
                            mm = pe.transpose(ps[:, 2, o:o + 60],
                                              cmp_hid[0:60, kind * T + c * P:kind * T + c * P + P],
                                              ident[0:60, 0:60])
                    mm.then_inc(c_tr, 1)
                if u == 2:
                    pe.wait_ge(c_trev, 1)
                    pe.wait_ge(rest_in, REST_IN)
                    for c in range(2):
                        pe.matmul(ps[:, 3, 0:60], w2k[:, c, :, :], hidT[:, c * 60:c * 60 + 60],
                                  start=c == 0, stop=c == 1)
                    for g in range(GROUPS):
                        for c in range(2):
                            o = 120 + c * 60 + g * N_CMP
                            mm = pe.matmul(ps[0:N_CMP, 3, 64 + g * HD:64 + g * HD + HD], hidT[:, o:o + N_CMP],
                                           w2v[:, c, :], start=c == 0, stop=c == 1)
                    mm.then_inc(c_kv, 1)
            pe.wait_ge(nq_ev, 3)
            pe.wait_ge(rest_in, REST_IN)
            for t in range(2):
                for k in range(8):
                    mm = pe.matmul(ps[:, 5, t * 48:t * 48 + 48], sq[:, k, t * P:t * P + P], w_gate[:, k, :],
                                   start=k == 0, stop=k == 7)
            mm.then_inc(nq_mm, 1)

            def n_scores(hd):
                pp, ch, g = head_parts(hd)
                b = 2 * (hd % 2)
                if hd >= 2:
                    pe.wait_ge(s_add, hd - 1)
                pe.matmul(ps[:, b, :], q_n[pp, ch, P:T], kd[pp, :, g, :], start=True, stop=True)
                pe.matmul(ps[:, b + 1, 272:272 + N_CMP], q_n[pp, ch, P:T], kc[pp, g, :], start=True, stop=True)
                pe.matmul(ps[:, b + 1, 0:T], q_n[pp, ch, 0:P], kd[pp, :, g, 0:P], start=True, stop=True)
                pe.matmul(ps[:, b + 1, T:T + N_CMP], q_n[pp, ch, 0:P], kc[pp, g, :],
                          start=True, stop=True).then_inc(s_mm, 1)

            def n_turn(hd):
                S = n_s[hd % 3]
                pe.wait_ge(s_p, hd + 1)
                if hd:
                    pe.wait_ge(s_trev, hd)
                    pe.wait_ge(s_trev2, hd)
                for br in range(2):
                    late = S[:, br * T:br * T + T]
                    early = S[:, 512 + br * P:512 + br * P + P]
                    pe.transpose(ps[:, 4 + br, 0:P], early, ident)
                    pe.transpose(ps[:, 4 + br, P:T], late[:, 0:P], ident)
                    pe.transpose(ps[:, 4 + br, T:T + P], late[:, P:T], ident)
                    mm = pe.transpose(ps[0:N_CMP, 4 + br, 384:512], S[:, 768 + 16 * br:768 + 16 * br + N_CMP], ident)
                mm.then_inc(s_tr, 1)

            def n_values(hd):
                pp, ch, g = head_parts(hd)
                pe.wait_ge(s_trev, hd + 1)
                pe.wait_ge(s_trev2, hd + 1)
                if hd % 2 == 0 and ch >= 2:
                    pe.wait_ge(s_ov, ch - 1)
                b = hd % 2
                o = ps[pp, 6 + ch % 2, 0:T]
                for br in range(2):
                    pe.matmul(o, v_n[:, br, 0, g * HD:g * HD + HD], n_pT[:, b, br, 0:T], start=br == 0, stop=False)
                    pe.matmul(o[:, P:T], v_n[:, br, 1, g * HD:g * HD + HD], n_pT[:, b, br, T:T + P],
                              start=False, stop=False)
                pe.matmul(o, vc[:, g, :], n_pc[0:N_CMP, b, :], start=False, stop=True).then_inc(s_pv, 1)

            pe.wait_ge(nq_ev, 5)
            pe.wait_ge(c_kvev, 2)
            pe.wait_ge(kd_in, 128)
            for hd in range(3):
                n_scores(hd)
            for hd in range(HEADS):
                n_turn(hd)
                if hd + 3 < HEADS:
                    n_scores(hd + 3)
                n_values(hd)
            pe.wait_ge(s_add, HEADS)
            for u in range(4):
                row_pair(U_NO, u, 4, X_NO, 0)
            norm(N_POST1)
            norm(N_CTX)
            norm(N_PREF1)
            ffn(1, U_F1, X_F1)
            norm(N_POSTF1)

            norm(N_IN2)
            for u in range(4):
                if u >= 2:
                    pe.wait_ge(va_ev, u - 1)
                col_tok(U_IN2 + u, 5 + 2 * (u % 2), x0=X_IN2 if u == 0 else None)
            for u in range(4):
                pe.wait_ge(*((ua_ev, u - 1) if u >= 2 else (va_ev, 3 + u)))
                col_T(U_IN2 + 4 + u, 5 + 2 * (u % 2))

            def turn_pairs(n, src):
                pe.wait_ge(qw_ev, n + 1)
                if n:
                    pe.wait_ge(q_sin, n)
                for c in range(2):
                    mm = pe.matmul(ps[:, 6, c * T:c * T + T], tab("perm"), src[:, c * T:c * T + T],
                                   start=True, stop=True)
                mm.then_inc(qp_mm, 1)

            for u in range(5):
                pe.wait_ge(*((qw_ev, u - 1) if u >= 2 else (ua_ev, 3 + u)))
                if u < 4:
                    col_T(U_IN2 + 8 + u, 5 + 2 * (u % 2))
                else:
                    take(U_IN2 + 12)
                    for src, bank in ((xn, 5), (ctxn, 7)):
                        if bank == 7:
                            pe.wait_ge(qw_ev, 4)
                        for b in range(2):
                            for k in range(8):
                                mm = pe.matmul(ps[:, bank, b * T:b * T + T],
                                               slot8(U_IN2 + 12)[:, k, b * P:b * P + P], src[:, k, :],
                                               start=k == 0, stop=k == 7)
                        mm.then_inc(kw_mm if bank == 5 else used, 1)
                if u:
                    turn_pairs(u - 1, q_w[:, 2 * u - 2:2 * u, :].rearrange("p a t -> p (a t)"))
            turn_pairs(4, kw_raw[:, 0, :])
            pe.wait_ge(ln_seq, LN_END)
            pe.wait_ge(ln_in, 64)
            for g in range(A_GROUPS):
                for t in range(2):
                    mm = pe.matmul(ps[:, g // 2, (g % 2) * T + t * P:(g % 2) * T + t * P + P],
                                   va[:, t, g * P:g * P + P], ws[:, g, :], start=True, stop=True)
                if g % 2:
                    mm.then_inc(sp_mm, 1)
            for s in range(2):
                pe.wait_ge(qw_ev, 5 + s)
                src = xn if s == 0 else ctxn
                if s == 0:
                    take(U_IN2 + 13)
                for t in range(2):
                    for k in range(8):
                        mm = pe.matmul(ps[:, 5 + 2 * s, t * T:t * T + T], src[:, k, t * P:t * P + P],
                                       slot8(U_IN2 + 13)[:, k, :], start=k == 0, stop=k == 7)
                mm.then_inc(vw_mm if s == 0 else used, 1)
            for u in range(8):
                pe.wait_ge(*((gt_ev, u - 1) if u >= 2 else (vw_ev, 1 + u)))
                col_T(U_IN2 + 14 + u, 5 + 2 * (u % 2))

            def w_scores(hd):
                pp, ch, g = head_parts(hd)
                b = 2 * (hd % 2)
                n = HEADS + hd
                pe.wait_ge(*((s_exp, n - 1) if hd >= 2 else (sp_add, 4)))
                for t in range(2):
                    mm = pe.matmul(ps[:, b + t, :], q_w[pp, ch, t * P:t * P + P], kd2[pp, g, :, :],
                                   start=True, stop=True)
                mm.then_inc(s_mm, 1)

            def w_turn(hd):
                n = HEADS + hd
                pe.wait_ge(s_p, n + 1)
                if hd:
                    pe.wait_ge(s_trev, n)
                    pe.wait_ge(s_trev2, n)
                for kb in range(4):
                    for t in range(2):
                        mm = pe.transpose(ps[:, 4 + kb // 2, (kb % 2) * T + t * P:(kb % 2) * T + t * P + P],
                                          w_s[hd % 3][:, t, kb * P:kb * P + P], ident)
                mm.then_inc(s_tr, 1)

            def w_values(hd):
                pp, ch, g = head_parts(hd)
                n = HEADS + hd
                pe.wait_ge(s_trev, n + 1)
                pe.wait_ge(s_trev2, n + 1)
                if hd % 2 == 0:
                    pe.wait_ge(*((s_ov, 8 + ch - 1) if ch >= 2 else (gt_ev, 8)))
                o = ps[pp, 6 + ch % 2, 0:T]
                for kb in range(4):
                    mm = pe.matmul(o, vw_tok[:, kb, g * HD:g * HD + HD], w_pT(hd)[:, kb, :],
                                   start=kb == 0, stop=kb == 3)
                mm.then_inc(s_pv, 1)

            pe.wait_ge(kd2_in, 128)
            pe.wait_ge(q_rot, 5)
            pe.wait_ge(gt_ev, 8)
            for hd in range(3):
                w_scores(hd)
            for hd in range(HEADS):
                w_turn(hd)
                if hd + 3 < HEADS:
                    w_scores(hd + 3)
                w_values(hd)
            pe.wait_ge(s_exp, 2 * HEADS)
            pe.wait_ge(ya_done, 4)
            for u in range(4):
                row_pair(U_PA, u, 4, X_PA, 0)
            pe.wait_ge(s_ov, 16)
            for u in range(4):
                row_pair(U_PB, u, 4, X_PB, 4)
            for u in range(4):
                row_pair(U_WO, u, 4, X_WO, 0)
            norm(N_MOE)

            pe.wait_ge(xn_ready, XN[N_MOE] + 8)
            for t in range(2):
                for k in range(8):
                    mm = pe.matmul(ps[:, 5, t * EXPERTS:(t + 1) * EXPERTS], xn[:, k, t * P:t * P + P],
                                   w_router[:, k, :], start=k == 0, stop=k == 7)
            mm.then_inc(lg_mm, 1)
            for b in range(4):
                t, half = b // 2, b % 2
                for k in range(4):
                    mm = pe.transpose(ps[:, b, k * P:k * P + P], xn[:, 4 * half + k, t * P:t * P + P], ident)
                mm.then_inc(tok_mm, 1)
            pe.wait_ge(r_seq, R_AFF)
            for t in range(2):
                mm = pe.transpose(ps[0:EXPERTS, 6, t * P:t * P + P], aff[:, t, :], ident)
            mm.then_inc(r_tr, 1)
            pe.wait_ge(r_seq, R_MASK)
            for t in range(2):
                mm = pe.transpose(ps[:, 7, t * EXPERTS:(t + 1) * EXPERTS], rank_work[0:EXPERTS, 1, t * P:t * P + P],
                                  ident[0:EXPERTS, 0:EXPERTS])
            mm.then_inc(r_tr, 1)
            pe.wait_ge(r_seq, R_MASKT)
            m = [e_small[:, 1, t * EXPERTS:(t + 1) * EXPERTS] for t in range(2)]
            pe.matmul(ps[:, 5, 0:EXPERTS], tab("tri"), m[0], start=True, stop=True)
            pe.matmul(ps[:, 5, EXPERTS:2 * EXPERTS], ones[:], m[0], start=True, stop=False)
            pe.matmul(ps[:, 5, EXPERTS:2 * EXPERTS], tab("tri"), m[1], start=False, stop=True).then_inc(r_pos, 1)
            pe.wait_ge(pick_set, 1)
            pe.wait_ge(tok_ev, 4)
            for k in range(8):
                for t in range(2):
                    mm = pe.matmul(ps[:, k, :], h2[:, t, k * P:k * P + P], pick[:, t, :],
                                   start=t == 0, stop=t == 1)
                mm.then_inc(xe_mm, 1)
            pe.wait_ge(xe_ev, 8)
            pe.wait_ge(r_seq, R_ZERO)
            for b in range(4):
                pe.matmul(ps[:, b, :], ones[:], zeros_row, start=True, stop=False, skip_group_check=True)

            def moe(n):
                pe.wait_ge(ed_ev, n)
                for b in range(4):
                    for half in range(2):
                        c = 4 * half + b
                        pp = slice(64 * half, 64 * half + 64)
                        mm = pe.matmul(ps[:, c // 2, (c % 2) * T:(c % 2) * T + T], e_y[pp, b * P:b * P + P],
                                       e_pT[pp, :], start=False, stop=False, skip_group_check=True)
                mm.then_inc(moe_mm, 1)

            def expert(e):
                first = isinstance(e, int)

                def etake(w):
                    pe.wait_ge(e_landed[w % ERING], e * 64 + 16 * (w // ERING + 1))

                pe.wait_ge(cur_set, e * 2 + 2)
                if not first:
                    pe.wait_ge(e_act, e)
                for part, bank in ((0, 4), (1, 5)):
                    if part and not first:
                        moe(e)
                        pe.wait_ge(e_hset, e)
                    for q in range(4):
                        w = 4 * part + q
                        etake(w)
                        sl = eslot(w, 2)
                        for c in range(2):
                            k = 2 * q + c
                            for j in range(4):
                                mm = pe.matmul(ps[32 * j:32 * j + 32, bank, :], xcur[:, k, :],
                                               sl[:, c, 512 * j:512 * j + 512], start=k == 0, stop=k == 7)
                        mm.then_inc(e_used, 1)
                if not first:
                    pe.wait_ge(eh_ev, e)
                for t in range(2):
                    mm = pe.transpose(ps[:, 7, t * P:t * P + P], pcur[:, t, :, :].rearrange("p r s -> p (r s)"),
                                      ident)
                mm.then_inc(ep_tr, 1)
                pe.wait_ge(e_hset, e + 1)
                pe.wait_ge(ep_ev, e + 1)
                for m in range(4):
                    mm = pe.transpose(ps[:, 7, m * P:m * P + P], e_hid[:, m * P:m * P + P], ident)
                mm.then_inc(eh_tr, 1)
                pe.wait_ge(eh_ev, e + 1)
                for w in range(8, 12):
                    etake(w)
                    sl = eslot(w, 4)
                    for m in range(4):
                        for half in range(2):
                            g = 2 * half + m % 2
                            mm = pe.matmul(ps[32 * g:32 * g + 32, 6, :],
                                           e_hidT[:, m * P + 32 * (w - 8):m * P + 32 * (w - 8) + 32],
                                           sl[:, m, 512 * half:512 * half + 512],
                                           start=w == 8 and m < 2, stop=w == 11 and m >= 2)
                    mm.then_inc(e_used, 1)

            expert(0)
            with pe.Fori(1, EXPERTS) as e:
                expert(e)
            moe(EXPERTS)
            norm(N_END)

        @block.scalar
        def _(act):
            act.dma_start(h[:], a["xT"].rearrange("(k p) t -> p k t", p=P)).then_inc(x_in, 16)
            act.dma_start(cols[:], a["cols"]).then_inc(cols_in, 16)
            firsts = [(tabs[:], a["tabs"]), (rel[0:32, :], a["rel_bias"]), (bucket_rows, a["bucket_rows"]),
                      (bucket_cmp[0:33, :], a["bucket_cmp"])]
            assert len(firsts) * 16 == FIRST_IN
            for dst, src in firsts:
                act.dma_start(dst, src).then_inc(first_in, 16)
            act.dma_start(decay, a["decay"].rearrange("p (h j) -> p h j", h=RET_HEADS)).then_inc(decay_in, 16)

            def squares(n, src, ready=None):
                for q in range(4):
                    if ready:
                        act.wait_ge(*ready(q))
                    act.activation(sq[:, 2 * q:2 * q + 2, :], src(q), ACT.Square).then_inc(sq_ready, 1)

            def roots(n):
                act.wait_ge(ss_ready, n + 1)
                if n:
                    act.wait_ge(rs_ready, n)
                act.activation(root[:], ps[:, 4, 0:T], ACT.Sqrt, scale=1.0 / D, bias=EPS).then_inc(root_ready, 1)

            def of_h(q):
                return h[:, 2 * q:2 * q + 2, :]

            def of_acc(q):
                return ps[:, q, :].rearrange("p (c t) -> p c t", c=2)

            act.wait_ge(x_in, 16)
            squares(N_PRE0, of_h)
            split_hi(act, U_RET)
            roots(N_PRE0)
            act.wait_ge(cs_set, 1)
            act.wait_ge(cols_in, 16)
            for r, name in enumerate(("c", "c_ctx")):
                ins = act.activation(cs[:, :, r], col(name), ACT.Silu)
            ins.then_inc(cs_set, 1)
            split_tokens_hi(act, xn, XN[N_PRE0])
            act.wait_ge(brow_mm, 2)
            act.activation(bias_rows, ps[0:HEADS, 0, 0:384], ACT.Copy).then_inc(brow_ev, 1)
            act.activation(cbias[:], ps[:, 1, 0:480].rearrange("p (t n h) -> p h t n", t=2, n=N_CMP),
                           ACT.Copy).then_inc(cbias_ev, 1)
            act.wait_ge(brow_ev, 1)
            act.dma_start(bias_dram, bias_rows.unsqueeze(1).to_broadcast([HEADS, P, 384])).then_inc(bias_out, 16)

            def ada_rows_out(r):
                taken(act, U_RET + 16 * r + 15)
                if r:
                    act.wait_ge(ada_tr, r)
                act.activation(ada_rows[:], ps[:, 6, :], ACT.Copy).then_inc(ada_ev, 1)

            for u in range(1, 10):
                split_hi(act, U_RET + 2 * u)
            ada_rows_out(0)
            act.wait_ge(bias_out, 16)
            for u in range(8):
                taken(act, U_RET + 16 + 2 * u)
                act.activation(v_r[:, :, u * T:u * T + T],
                               ps[:, 5 + 2 * (u % 2), :].rearrange("p (t n) -> p t n", t=2), ACT.Copy).then_inc(v_ev, 1)
                split_hi(act, U_RET + 20 + 2 * u)
            ada_rows_out(1)

            def g_out(u):
                taken(act, U_RET + 32 + 2 * u)
                if u >= 2:
                    act.wait_ge(og_done, u - 1)
                else:
                    act.wait_ge(qk_done, 8)
                act.activation(gs[:, u % 2, :], ps[:, 5 + 2 * (u % 2), :], ACT.Silu).then_inc(g_ev, 1)
                if u + 2 < 8:
                    split_hi(act, U_RET + 36 + 2 * u)

            for hd in range(RET_HEADS):
                g_out(2 * hd)
                act.wait_ge(o_mm, hd + 1)
                if hd:
                    act.wait_ge(oss, hd)
                act.activation(sq[:, 0:4, :], ps[:, 2:4, :].rearrange("p b (c t) -> p (b c) t", c=2),
                               ACT.Square).then_inc(osq, 1)
                g_out(2 * hd + 1)
                act.wait_ge(oss, hd + 1)
                act.activation(root[:], ps[:, 4, 0:T], ACT.Sqrt, scale=1.0 / RET_V, bias=EPS).then_inc(oroot, 1)
            ada_rows_out(2)
            for u in range(8):
                act.wait_ge(og_done, u + 1)
                if u >= 4:
                    taken(act, U_RO + u - 4)
                pair_hi(act, u, two_chunks(o_r, u))
                split_hi(act, U_RO + u)

            def post(n, before, U):
                split_hi(act, U)
                taken(act, before)
                squares(n, of_acc)
                roots(n)
                split_hi(act, U + 1)

            def pre(n, posted):
                squares(n, of_h, lambda q: (h_ready, POST[posted] + 2 * q + 2))
                roots(n)

            post(N_POST0, U_F0 - 1, U_F0)
            rests = [(w_gate, a["nsa_w_in"].rearrange("(k p) n -> p k n", p=P)[:, :, HEADS * HD:]),
                     (w2k[:, :, 0, :], a["cmp_w2_k"].rearrange("(c p) n -> p c n", p=P)),
                     (w2k[:, :, 1, :], a["cmp_w2_k"].rearrange("(c p) n -> p c n", p=P)),
                     (w2v[:], a["cmp_w2_v"].rearrange("(c p) n -> p c n", p=P)),
                     (w_router[:], a["w_router_2"].rearrange("(k p) n -> p k n", p=P)),
                     (sink[:], a["attn_sink_2"].partition_broadcast(P))]
            assert len(rests) * 16 == REST_IN
            for dst, src in rests:
                act.dma_start(dst, src).then_inc(rest_in, 16)
            act.wait_ge(bias_out, 16)
            act.dma_start(bias, bass.AP(bias_dram.tensor, P - 1, [[383, P], [P * 384, HEADS], [1, T]])) \
               .then_inc(bias_in, 16)
            pre(N_PREF0, N_POST0)
            split_tokens_hi(act, xn, XN[N_PREF0])

            def ffn(f):
                base = f * PAIRS

                def silu(j, r=0):
                    taken(act, gate_unit(f, j), r)
                    if j >= 2:
                        act.wait_ge(f_hidden, r * 2 + (base + j - 1))
                    act.activation(f_silu[:, j % 2, :], ps[:, 4 + 2 * (j % 2), :], ACT.Silu).then_inc(f_act, 1)

                def hidden_hi(j, r=0):
                    act.wait_ge(f_hidden, r * 2 + (base + j + 1))
                    if j:
                        taken(act, out_unit(f, j - 1), r)
                    act.activation(f_hi[:], hidden_of(j), ACT.Copy).then_inc(fhi_ready, 1)

                def silu_and_split(j, r=0):
                    silu(j, r)
                    if j:
                        split_hi(act, out_unit(f, j - 1), r)
                    split_hi(act, gate_unit(f, j + 1), r)
                    split_hi(act, gate_unit(f, j + 1) + 1, r)
                    hidden_hi(j, r)

                silu_and_split(0)
                silu_and_split(1)
                with act.Fori(0, (PAIRS - 3) // 2) as i:
                    silu_and_split(2, i)
                    silu_and_split(3, i)
                silu(10)
                split_hi(act, out_unit(f, 9))
                hidden_hi(10)
                split_hi(act, out_unit(f, 10))

            ffn(0)
            post(N_POSTF0, U_KV - 1, U_KV)
            pre(N_PRE1, N_POSTF0)
            split_tokens_hi(act, xn, XN[N_PRE1])
            for u in range(6):
                taken(act, U_KV + u)
                dst = kv_raw[:, u] if u < 4 else v_n[:, u - 4]
                act.activation(dst, ps[:, 5 + 2 * (u % 2), :].rearrange("p (t n) -> p t n", t=2),
                               ACT.Copy).then_inc(kv_ev, 1)
                if u < 4:
                    split_hi(act, U_KV + u + 2)
                if u in (1, 3):
                    act.wait_ge(kv_ev, u + 1)
                    for half in range(2):
                        for odd in range(2):
                            hp, op = slice(64 * half, 64 * half + 64), slice(64 * odd, 64 * odd + 64)
                            for kind in range(2):
                                if u == 1:
                                    act.dma_start(shifted[hp, kind, odd::2, 0:T - half],
                                                  kv_raw[op, kind, :, half:T]).then_inc(shift_in, 16)
                                else:
                                    act.dma_start(kd[hp, kind, odd::2, :],
                                                  kv_raw[op, 2 + kind, :, :]).then_inc(kd_in, 16)
            split_tokens_hi(act, sq, XN[N_PRE1] + 8)
            for kind in range(2):
                taken(act, U_W1 + 2 * kind + 1)
                act.activation(cmp_hid[0:60, kind * T:kind * T + T], ps[0:60, kind, 0:T],
                               ACT.Silu).then_inc(c_act, 1)
                split_hi(act, U_NQ + kind)
            for u in range(4):
                taken(act, U_NQ + u)
                act.activation(q_n[:, 2 * u:2 * u + 2, :],
                               ps[:, 5 + 2 * (u % 2), :].rearrange("p (c t) -> p c t", c=2), ACT.Copy,
                               scale=HD ** -0.5).then_inc(nq_ev, 1)
                if u < 2:
                    split_hi(act, U_NQ + u + 2)
            act.wait_ge(nq_mm, 1)
            act.activation(gates[:], ps[:, 5, 0:96].rearrange("p (t n) -> p t n", t=2),
                           ACT.Sigmoid).then_inc(nq_ev, 1)

            def n_exp(hd):
                S, s = n_s[hd % 3], st[:, hd % 3, :]
                act.wait_ge(s_neg, hd + 1)
                for i, part in enumerate([S[:, 0:T], S[:, T:512], S[:, 512:640], S[:, 640:768],
                                          S[:, 768:768 + N_CMP], S[:, 784:784 + N_CMP]]):
                    ins = act.activation(part, part, ACT.Exp, bias=s[:, 6 + i:7 + i], accum_out=s[:, 12 + i:13 + i])
                ins.then_inc(s_exp, 1)

            def n_pout(hd):
                act.wait_ge(s_tr, hd + 1)
                if hd >= 2:
                    act.wait_ge(s_pv, hd - 1)
                act.activation(n_pT[:, hd % 2, :, :], ps[:, 4:6, 0:384], ACT.Copy).then_inc(s_trev, 1)
                act.activation(n_pc[0:N_CMP, hd % 2, :].rearrange("p (t j) -> p t j", t=2),
                               ps[0:N_CMP, 4:6, 384:512], ACT.Copy).then_inc(s_trev2, 1)

            n_exp(0)
            for hd in range(HEADS):
                if hd + 1 < HEADS:
                    n_exp(hd + 1)
                n_pout(hd)
                if hd >= HEADS - 2:
                    split_hi(act, U_NO + hd - (HEADS - 2))
            act.dma_start(ctxn, a["ctxT"].rearrange("(k p) t -> p k t", p=P)).then_inc(ctx_in, 16)
            for u in range(4):
                act.wait_ge(s_ov, 2 * u + 2)
                pair_hi(act, u, two_chunks(o_n, u))
            for u in range(2, 4):
                split_hi(act, U_NO + u)
            post(N_POST1, U_F1 - 1, U_F1)
            act.wait_ge(ctx_in, 16)
            squares(N_CTX, lambda q: ctxn[:, 2 * q:2 * q + 2, :])
            roots(N_CTX)
            pre(N_PREF1, N_POST1)
            split_tokens_hi(act, xn, XN[N_PREF1])
            ffn(1)
            post(N_POSTF1, U_IN2 - 1, U_IN2)
            act.dma_start(ln_g, a["gmlp_ln_g_2"].partition_broadcast(P)).then_inc(ln_in, 16)
            act.dma_start(ln_b, a["gmlp_ln_b_2"].partition_broadcast(P)).then_inc(ln_in, 16)
            act.dma_start(bs, a["b_spatial_2"].partition_broadcast(P)).then_inc(ln_in, 16)
            act.dma_start(ws, a["w_spatialT"]).then_inc(ln_in, 16)
            pre(N_IN2, N_POSTF1)
            split_tokens_hi(act, xn, XN[N_IN2])
            for u in range(4):
                taken(act, U_IN2 + u)
                act.activation(va[:, :, u * T:u * T + T],
                               ps[:, 5 + 2 * (u % 2), :].rearrange("p (t n) -> p t n", t=2),
                               ACT.Gelu_apprx_tanh).then_inc(va_ev, 1)
                split_hi(act, U_IN2 + u + 2)
            for u in range(4):
                taken(act, U_IN2 + 4 + u)
                act.activation(ya[:, 2 * u:2 * u + 2, :],
                               ps[:, 5 + 2 * (u % 2), :].rearrange("p (c t) -> p c t", c=2),
                               ACT.Gelu_apprx_tanh).then_inc(ua_ev, 1)
                split_hi(act, U_IN2 + u + 6)
                if u == 1:
                    act.wait_ge(ln_seq, 2)
                    act.activation(st[:, 0, 28:30], st[:, 0, 24:28].rearrange("p (t c) -> p t c", c=2)[:, :, 1],
                                   ACT.Sqrt, bias=EPS).then_inc(ln_root, 1)
            for n in range(6):
                if n == 4:
                    act.wait_ge(kw_mm, 1)
                else:
                    taken(act, U_IN2 + 8 + min(n, 4))
                dst = q_w[:, 2 * n:2 * n + 2, :].rearrange("p a t -> p (a t)") if n < 4 else kw_raw[:, n - 4, :]
                act.activation(dst, ps[:, 5 + 2 * (n % 2), :], ACT.Copy,
                               scale=HD ** -0.5 if n < 4 else 1.0).then_inc(qw_ev, 1)
                if n in (0, 1, 2, 5):
                    split_hi(act, U_IN2 + {0: 10, 1: 11, 2: 14, 5: 15}[n])
            for s in range(2):
                if s == 0:
                    act.wait_ge(vw_mm, 1)
                else:
                    taken(act, U_IN2 + 13)
                act.activation(vw_tok[:, 2 * s:2 * s + 2, :],
                               ps[:, 5 + 2 * s, :].rearrange("p (t n) -> p t n", t=2), ACT.Copy).then_inc(vw_ev, 1)
            act.wait_ge(q_rot, 5)
            act.wait_ge(qw_ev, 6)
            for half in range(2):
                for odd in range(2):
                    hp, op = slice(64 * half, 64 * half + 64), slice(64 * odd, 64 * odd + 64)
                    for s in range(2):
                        act.dma_start(kd2[hp, odd::2, s, :],
                                      kw_raw[op, s, :].rearrange("p (g t) -> p g t", g=2)).then_inc(kd2_in, 16)
            for u in range(8):
                taken(act, U_IN2 + 14 + u)
                if u == 0:
                    act.wait_ge(sp_mm, 4)
                for c in range(2):
                    dst = (ga if u < 4 else gb)[:, (2 * u + c) % 8, :]
                    ins = act.activation(dst, ps[:, 5 + 2 * (u % 2), c * T:c * T + T], ACT.Sigmoid,
                                         bias=col("b_merge", 2 * u + c))
                ins.then_inc(gt_ev, 1)
                if u < 6:
                    split_hi(act, U_IN2 + 16 + u)

            def w_exp(hd):
                S, s, b = w_s[hd % 3], st[:, hd % 3, :], 2 * (hd % 2)
                act.wait_ge(s_neg, HEADS + hd + 1)
                for t in range(2):
                    act.activation(S[:, t, 0:T], S[:, t, 0:T], ACT.Exp, bias=s[:, 6 + t:7 + t],
                                   accum_out=s[:, 12 + t:13 + t])
                    act.activation(S[:, t, T:512], ps[:, b + t, T:512], ACT.Exp, bias=s[:, 6 + t:7 + t],
                                   accum_out=s[:, 14 + t:15 + t])
                act.activation(s[:, 16:18], s[:, 6:8], ACT.Exp, bias=sink[:, hd:hd + 1]).then_inc(s_exp, 1)

            def w_pout(hd):
                n = HEADS + hd
                act.wait_ge(s_tr, n + 1)
                if hd >= 2:
                    act.wait_ge(s_pv, n - 1)
                act.activation(w_pT(hd)[:, 0:2, :], ps[:, 4, :].rearrange("p (k t) -> p k t", k=2),
                               ACT.Copy).then_inc(s_trev, 1)

            act.wait_ge(rest_in, REST_IN)
            w_exp(0)
            for hd in range(HEADS):
                if hd + 1 < HEADS:
                    w_exp(hd + 1)
                w_pout(hd)
                if hd < 4:
                    act.wait_ge(ya_done, hd + 1)
                    pair_hi(act, hd, two_chunks(ya, hd))
                if hd >= HEADS - 2:
                    split_hi(act, U_PA + hd - (HEADS - 2))
            act.wait_ge(s_ov, 16)
            for u in range(4):
                split_hi(act, U_PA + 2 + u)
                taken(act, U_PA + u)
                pair_hi(act, u, two_chunks(o_w, u))
            for u in range(4):
                split_hi(act, U_PB + 2 + u)
            for u in range(4):
                act.wait_ge(merged, u + 1)
                pair_hi(act, u, two_chunks(gb, u))
                if u == 0:
                    split_hi(act, U_WO + 2)
            split_hi(act, U_WO + 3)
            squares(N_MOE, of_h, lambda q: (x2_done, q + 1))
            roots(N_MOE)
            for b in range(4):
                act.wait_ge(tok_mm, b + 1)
                act.activation(h2[:, b // 2, (b % 2) * 512:(b % 2) * 512 + 512], ps[:, b, :],
                               ACT.Copy).then_inc(tok_ev, 1)
            act.wait_ge(r_seq, 2)
            for t in range(2):
                ins = act.activation(aff[:, t, :], ps[:, 5, t * EXPERTS:(t + 1) * EXPERTS], ACT.Exp,
                                     bias=st[:, 0, 2 + t:3 + t], accum_out=st[:, 0, 4 + t:5 + t])
            ins.then_inc(r_exp, 1)
            for k in range(8):
                act.wait_ge(xe_mm, k + 1)
                act.activation(xe[:, k, :], ps[:, k, :], ACT.Copy).then_inc(xe_ev, 1)

            def expert(e):
                first = isinstance(e, int)
                act.wait_ge(e_used, e * E_UNITS + 4)
                if not first:
                    act.wait_ge(e_hset, e)
                act.activation(e_silu, ps[:, 4, :], ACT.Silu).then_inc(e_act, 1)
                act.wait_ge(ep_tr, e + 1)
                if not first:
                    act.wait_ge(moe_mm, e)
                act.activation(e_pT, ps[:, 7, 0:T], ACT.Copy).then_inc(ep_ev, 1)
                act.wait_ge(e_used, e * E_UNITS + 12)
                act.activation(e_y, ps[:, 6, :], ACT.Copy).then_inc(ed_ev, 1)

            expert(0)
            with act.Fori(1, EXPERTS) as e:
                expert(e)
            squares(N_END, of_h, lambda q: (moe_done, 2 * q + 2))
            roots(N_END)

        @block.vector
        def _(dve):
            dve.memset(ones[:], 1.0).then_inc(ones_set, 1)
            dve.memset(cs[:], 0.0).then_inc(cs_set, 1)

            def inverse(n):
                dve.wait_ge(root_ready, n + 1)
                dve.reciprocal(rs[:], root[:]).then_inc(rs_ready, 1)
                dve.wait_ge(rs_ready, n + 1)

            def tokens_lo(x0, src, make=None):
                for k in range(10 if make else 8):
                    if make and k < 8:
                        make(k)
                    if not make or k >= 2:
                        token_lo(dve, x0, src, k - 2 if make else k)

            def pre(n, gains, dst=xn, x0=None):
                def one(k):
                    dve.scalar_tensor_tensor(out=dst[:, k, :], in0=h[:, k, :], scalar=gains(k), in1=rs[:],
                                             op0=ALU.mult, op1=ALU.mult).then_inc(xn_ready, 1)

                if x0 is None:
                    for k in range(8):
                        one(k)
                else:
                    tokens_lo(x0, dst, one)

            def gain_of(name):
                return lambda k: col(name, k)

            dve.wait_ge(cols_in, 16)
            inverse(N_PRE0)
            pre(N_PRE0, gain_of("mix_pre0"), x0=X_RET)
            split_lo(dve, U_RET)

            def ada_out(r):
                dve.wait_ge(ada_tr, r + 1)
                for row in range(2):
                    o = COLS["b_ada"][0] + 16 * r
                    ins = dve.tensor_tensor(
                        mod[:, row, 16 * r:16 * r + 16].rearrange("p (j m) -> p j m", j=4),
                        ps[:, 6, :].rearrange("p (m j s) -> p j m s", m=4, j=4)[:, :, :, row],
                        cols[:, o:o + 16].rearrange("p (j m) -> p j m", j=4), ALU.add)
                ins.then_inc(ada_mod, 1)

            dve.wait_ge(first_in, FIRST_IN)
            for u in range(8):
                split_lo(dve, U_RET + 2 * u + 2)
                taken(dve, U_RET + 2 * u)
                if u >= 2:
                    dve.wait_ge(qk_done, u - 1)
                src = ps[:, 5 + 2 * (u % 2), :]
                dve.tensor_tensor(rot[:, u % 2, 0, :].rearrange("p (c t) -> p c t", c=2),
                                  src.rearrange("p (c t) -> p c t", c=2),
                                  tab("ret_cos").unsqueeze(1).to_broadcast([P, 2, T]), ALU.mult)
                dve.tensor_tensor(rot[:, u % 2, 1, 0:T], src[:, T:512], tab("ret_nsin"), ALU.mult)
                dve.tensor_tensor(rot[:, u % 2, 1, T:512], src[:, 0:T], tab("ret_sin"), ALU.mult).then_inc(qk_rot, 1)
            split_lo(dve, U_RET + 18)
            ada_out(0)
            for u in range(10, 18):
                split_lo(dve, U_RET + 2 * u)

            def ret_norm(hd):
                dve.wait_ge(oroot, hd + 1)
                dve.reciprocal(rs[:], root[:]).then_inc(ors, 1)
                dve.wait_ge(ors, hd + 1)
                dve.tensor_tensor(o_r[:, 4 * hd:4 * hd + 4, :],
                                  ps[:, 2:4, :].rearrange("p b (c t) -> p (b c) t", c=2),
                                  rs[:].unsqueeze(1).to_broadcast([P, 4, T]), ALU.mult).then_inc(on_ev, 1)

            dve.wait_ge(decay_in, 16)
            dve.wait_ge(qk_done, 8)
            for hd in range(RET_HEADS):
                dve.wait_ge(sc_mm, hd + 1)
                if hd >= 2:
                    dve.wait_ge(o_mm, hd - 1)
                dve.tensor_tensor(sT[:, hd % 2, :], ps[:, hd % 2, 0:384], decay[:, hd, :], ALU.mult).then_inc(sc_ev, 1)
                if hd == 0:
                    ada_out(1)
                if hd:
                    ret_norm(hd - 1)
                if hd < 3:
                    split_lo(dve, U_RET + 36 + 4 * hd)
                    split_lo(dve, U_RET + 38 + 4 * hd)
            ret_norm(RET_HEADS - 1)
            ada_out(2)
            dve.wait_ge(ada_mod, 3)
            for i, (row, o, name) in enumerate(((0, 8, "norm1"), (1, 8, "norm1"), (0, 32, "norm2"))):
                ins = dve.scalar_tensor_tensor(out=gain[:, i, :], in0=mod[:, row, o:o + 8], scalar=1.0,
                                               in1=col(name), op0=ALU.add, op1=ALU.mult)
            ins.then_inc(gains_set, 1)

            for u in range(8):
                pair_lo(dve, X_RO, u, two_chunks(o_r, u))
                split_lo(dve, U_RO + u)

            def post(n, name, U):
                split_lo(dve, U)
                inverse(n)
                for k in range(8):
                    dve.scalar_tensor_tensor(out=xn[:, k, :], in0=ps[:, k // 2, (k % 2) * T:(k % 2) * T + T],
                                             scalar=col(name, k), in1=rs[:], op0=ALU.mult,
                                             op1=ALU.mult).then_inc(scaled, 1)
                split_lo(dve, U + 1)

            post(N_POST0, "mix_post0", U_F0)
            inverse(N_PREF0)
            pre(N_PREF0, gain_of("ffn_pre0"), x0=X_F0)

            def ffn(f):
                base = f * PAIRS

                def hidden(j, r=0):
                    dve.wait_ge(f_act, r * 2 + (base + j + 1))
                    taken(dve, gate_unit(f, j) + 1, r)
                    dve.tensor_tensor(f_hid[:, j % 2, :], f_silu[:, j % 2, :], ps[:, 5 + 2 * (j % 2), :],
                                      ALU.mult).then_inc(f_hidden, 1)

                def hidden_lo(j, r=0):
                    dve.wait_ge(fhi_ready, r * 2 + (base + j + 1))
                    dve.tensor_tensor(f_lo[:], hidden_of(j), f_hi[:], ALU.subtract).then_inc(flo_ready, 1)

                def hidden_and_split(j, r=0):
                    if j:
                        split_lo(dve, out_unit(f, j - 1), r)
                        hidden(j, r)
                    split_lo(dve, gate_unit(f, j + 1), r)
                    if not j:
                        hidden(j, r)
                    split_lo(dve, gate_unit(f, j + 1) + 1, r)
                    hidden_lo(j, r)

                hidden_and_split(0)
                hidden_and_split(1)
                with dve.Fori(0, (PAIRS - 3) // 2) as i:
                    hidden_and_split(2, i)
                    hidden_and_split(3, i)
                split_lo(dve, out_unit(f, 9))
                hidden(10)
                hidden_lo(10)
                split_lo(dve, out_unit(f, 10))

            ffn(0)
            post(N_POSTF0, "ffn_post0", U_KV)
            inverse(N_PRE1)
            pre(N_PRE1, gain_of("kv_norm"), x0=X_KV)
            pre(N_PRE1, gain_of("mix_pre1"), dst=sq)
            for u in range(2, 6):
                split_lo(dve, U_KV + u)
            dve.wait_ge(shift_in, 128)
            for kind, name in enumerate(("pe_k", "pe_v")):
                win = shifted[:, kind].rearrange("p g (n s) -> p s g n", s=16)
                for w in range(2):
                    dve.tensor_tensor(blocks[:, kind, 8 * w:8 * w + 8, :].rearrange("p c (g n) -> p c g n", g=GROUPS),
                                      win[:, 0:16:2, :, w:w + N_CMP],
                                      col(name)[:, 8 * w:8 * w + 8].unsqueeze(2).unsqueeze(3)
                                      .to_broadcast([P, 8, GROUPS, N_CMP]), ALU.add).then_inc(blocks_set, 1)
            tokens_lo(X_NQ, sq)
            for u in range(3):
                split_lo(dve, U_NQ + u)
            dve.wait_ge(c_tr, 1)
            dve.tensor_copy(hidT[:, 0:240], ps[:, 2, 0:240]).then_inc(c_trev, 1)
            split_lo(dve, U_NQ + 3)
            dve.wait_ge(c_kv, 1)
            dve.tensor_copy(kc.rearrange("p g n -> p (g n)"), ps[:, 3, 0:60]).then_inc(c_kvev, 1)
            dve.tensor_copy(vc.rearrange("p g n -> p (g n)"), ps[0:N_CMP, 3, 64:320]).then_inc(c_kvev, 1)
            dve.wait_ge(bias_in, 16)
            dve.wait_ge(nq_ev, 5)

            def two(v):
                return v.unsqueeze(1).to_broadcast([P, 2, v.shape[1]])

            def parts(S):
                return (S[:, 0:512].rearrange("p (r j) -> p r j", r=2),
                        S[:, 512:768].rearrange("p (r j) -> p r j", r=2),
                        S[:, 768:800].rearrange("p (r j) -> p r j", r=2)[:, :, 0:N_CMP])

            def n_max(hd):
                S, s, b = n_s[hd % 3], st[:, hd % 3, :], 2 * (hd % 2)
                late, early, comp = parts(S)
                dve.wait_ge(s_mm, hd + 1)
                if hd >= 3:
                    dve.wait_ge(s_tr, hd - 2)
                dve.tensor_tensor(late, ps[:, b, :].rearrange("p (r j) -> p r j", r=2), two(bias[:, hd, :]), ALU.add)
                dve.tensor_tensor(early, ps[:, b + 1, 0:T].rearrange("p (r j) -> p r j", r=2),
                                  two(bias[:, hd, P:T]), ALU.add)
                dve.tensor_tensor(comp, ps[:, b + 1, T:T + 32].rearrange("p (r j) -> p r j", r=2)[:, :, 0:N_CMP],
                                  cbias[:, hd, :, :], ALU.add).then_inc(s_add, 1)
                dve.wait_ge(s_add, hd + 1)
                dve.tensor_reduce(s[:, 0:2], late, AX_X, ALU.max)
                dve.tensor_reduce(s[:, 2:4], early, AX_X, ALU.max)
                dve.tensor_reduce(s[:, 4:6], comp, AX_X, ALU.max).then_inc(s_max, 1)
                dve.wait_ge(s_max, hd + 1)
                dve.tensor_scalar(s[:, 6:12], s[:, 0:6], -1.0, LEAST, ALU.mult, ALU.min).then_inc(s_neg, 1)

            def n_scale(hd):
                S, s = n_s[hd % 3], st[:, hd % 3, :]
                dve.wait_ge(s_exp, hd + 1)
                dve.tensor_scalar(s[:, 18:24], s[:, 12:18], TINY, None, ALU.max).then_inc(s_sum, 1)
                dve.wait_ge(s_sum, hd + 1)
                dve.reciprocal(s[:, 24:30], s[:, 18:24]).then_inc(s_inv, 1)
                dve.wait_ge(s_inv, hd + 1)
                dve.tensor_tensor(s[:, 18:20], s[:, 24:26], gates[:, 1, 3 * hd + 1:3 * hd + 3], ALU.mult)
                dve.tensor_tensor(s[:, 20:22], s[:, 26:28], gates[:, 0, 3 * hd + 1:3 * hd + 3], ALU.mult)
                dve.tensor_tensor(s[:, 22:24], s[:, 28:30], gates[:, :, 3 * hd], ALU.mult).then_inc(s_fac, 1)
                dve.wait_ge(s_fac, hd + 1)
                for i, part in enumerate(parts(S)):
                    ins = dve.tensor_tensor(part, part, s[:, 18 + 2 * i:20 + 2 * i].unsqueeze(2)
                                            .to_broadcast([P, 2, part.shape[2]]), ALU.mult)
                ins.then_inc(s_p, 1)

            def o_out(dst, ch, n0):
                dve.wait_ge(s_pv, n0 + 2 * ch + 2)
                dve.tensor_copy(dst[:, ch, :], ps[:, 6 + ch % 2, 0:T]).then_inc(s_ov, 1)

            n_max(0)
            n_max(1)
            for hd in range(HEADS):
                n_scale(hd)
                if hd + 2 < HEADS:
                    n_max(hd + 2)
                if hd % 2 == 1 and hd >= 3:
                    o_out(o_n, (hd - 3) // 2, 0)
            o_out(o_n, 7, 0)
            for u in range(2):
                split_lo(dve, U_NO + u)
            for u in range(4):
                pair_lo(dve, X_NO, u, two_chunks(o_n, u))
            for u in range(2, 4):
                split_lo(dve, U_NO + u)
            def shift(n, dst, row, o):
                def one(k):
                    dve.wait_ge(mod_scaled, MODP[n] + k + 1)
                    dve.tensor_scalar(dst[:, k, :], dst[:, k, :], mod[:, row, o + k:o + k + 1], None,
                                      ALU.add).then_inc(xn_ready, 1)

                if n == N_IN2:
                    tokens_lo(X_IN2, dst, one)
                else:
                    for k in range(8):
                        one(k)

            def mod_norm(n, src, dst, i, row, o):
                if n == N_CTX:
                    dve.wait_ge(gains_set, 1)
                    dve.wait_ge(scaled, POST[N_POST1] + 8)
                else:
                    dve.wait_ge(mod_scaled, MODP[n])
                inverse(n)
                for k in range(8):
                    dve.scalar_tensor_tensor(out=dst[:, k, :], in0=src[:, k, :], scalar=gain[:, i, k:k + 1],
                                             in1=rs[:], op0=ALU.mult, op1=ALU.mult).then_inc(mod_scaled, 1)
                shift(n, dst, row, o)

            post(N_POST1, "mix_post1", U_F1)
            mod_norm(N_CTX, ctxn, ctxn, 1, 1, 0)
            inverse(N_PREF1)
            pre(N_PREF1, gain_of("ffn_pre1"), x0=X_F1)
            ffn(1)
            post(N_POSTF1, "ffn_post1", U_IN2)

            mod_norm(N_IN2, h, xn, 0, 0, 0)
            for u in range(2, 6):
                split_lo(dve, U_IN2 + u)
            dve.wait_ge(va_ev, 4)
            for t in range(2):
                for c in range(2):
                    ins = dve.bn_stats(st[:, 0, 6 * (2 * t + c):6 * (2 * t + c) + 6], va[:, t, 512 * c:512 * c + 512])
            ins.then_inc(ln_seq, 1)
            dve.wait_ge(ln_seq, 1)
            for t in range(2):
                ins = dve.bn_aggr(st[:, 0, 24 + 2 * t:26 + 2 * t], st[:, 0, 12 * t:12 * t + 12])
            ins.then_inc(ln_seq, 1)
            split_lo(dve, U_IN2 + 6)
            split_lo(dve, U_IN2 + 7)
            dve.wait_ge(ln_root, 1)
            dve.reciprocal(st[:, 0, 30:32], st[:, 0, 28:30]).then_inc(ln_seq, 1)
            dve.wait_ge(ln_seq, 3)
            dve.wait_ge(ln_in, 64)
            for t in range(2):
                ins = dve.tensor_scalar(va[:, t, :], va[:, t, :], st[:, 0, 24 + 2 * t:25 + 2 * t],
                                        st[:, 0, 30 + t:31 + t], ALU.subtract, ALU.mult)
            ins.then_inc(ln_seq, 1)
            split_lo(dve, U_IN2 + 8)
            dve.wait_ge(ln_seq, 4)
            for t in range(2):
                ins = dve.tensor_tensor(va[:, t, :], va[:, t, :], ln_g, ALU.mult)
            ins.then_inc(ln_seq, 1)
            split_lo(dve, U_IN2 + 9)
            dve.wait_ge(ln_seq, 5)
            for t in range(2):
                ins = dve.tensor_tensor(va[:, t, :], va[:, t, :], ln_b, ALU.add)
            ins.then_inc(ln_seq, 1)

            def rotate(n, src):
                v = src.rearrange("p (c t) -> p c t", c=2)
                dve.wait_ge(qp_mm, n + 1)
                if n:
                    dve.wait_ge(q_rot, n)
                dve.tensor_tensor(rot2.rearrange("p (c t) -> p c t", c=2),
                                  ps[:, 6, :].rearrange("p (c t) -> p c t", c=2), two(tab("rope_sin")),
                                  ALU.mult).then_inc(q_sin, 1)
                dve.tensor_tensor(v, v, two(tab("rope_cos")), ALU.mult).then_inc(q_cos, 1)
                dve.wait_ge(q_cos, n + 1)
                dve.wait_ge(q_sin, n + 1)
                dve.tensor_tensor(src, src, rot2, ALU.add).then_inc(q_rot, 1)

            split_lo(dve, U_IN2 + 10)
            split_lo(dve, U_IN2 + 11)
            for n in range(5):
                if n == 2:
                    split_lo(dve, U_IN2 + 14)
                rotate(n, q_w[:, 2 * n:2 * n + 2, :].rearrange("p a t -> p (a t)") if n < 4 else kw_raw[:, 0, :])
            for b in range(4):
                dve.wait_ge(sp_mm, b + 1)
                src = ps[:, b, :].rearrange("p (g t q) -> p g t q", g=2, t=2)
                spatial = sq[:, 2 * b:2 * b + 2, :].rearrange("p g (t q) -> p g t q", t=2)
                dve.tensor_tensor(spatial, src,
                                  bs[:, 2 * b:2 * b + 2, :].unsqueeze(2).to_broadcast([P, 2, 2, P]),
                                  ALU.add).then_inc(sp_add, 1)
                dve.wait_ge(sp_add, b + 1)
                y = ya[:, 2 * b:2 * b + 2, :].rearrange("p g (t q) -> p g t q", t=2)
                dve.tensor_tensor(y, y, spatial, ALU.mult).then_inc(ya_done, 1)
            for u in range(15, 22):
                split_lo(dve, U_IN2 + u)

            def w_max(hd):
                n = HEADS + hd
                S, s, b = w_s[hd % 3], st[:, hd % 3, :], 2 * (hd % 2)
                dve.wait_ge(s_mm, n + 1)
                if hd >= 3:
                    dve.wait_ge(s_tr, n - 2)
                dve.tensor_tensor(S[:, :, 0:T], ps[:, b:b + 2, 0:T], tab("band").rearrange("p (t j) -> p t j", t=2),
                                  ALU.add).then_inc(s_add, 1)
                dve.tensor_reduce(s[:, 2:4], ps[:, b:b + 2, T:512], AX_X, ALU.max)
                dve.wait_ge(s_add, n + 1)
                dve.tensor_reduce(s[:, 0:2], S[:, :, 0:T], AX_X, ALU.max).then_inc(s_max, 1)
                dve.wait_ge(s_max, n + 1)
                dve.scalar_tensor_tensor(out=s[:, 4:6], in0=s[:, 0:2], scalar=sink[:, hd:hd + 1], in1=s[:, 2:4],
                                         op0=ALU.max, op1=ALU.max).then_inc(s_fac, 1)
                dve.wait_ge(s_fac, n + 1)
                dve.tensor_scalar(s[:, 6:8], s[:, 4:6], -1.0, None, ALU.mult).then_inc(s_neg, 1)

            def w_scale(hd):
                n = HEADS + hd
                S, s = w_s[hd % 3], st[:, hd % 3, :]
                dve.wait_ge(s_exp, n + 1)
                dve.tensor_tensor(s[:, 18:20], s[:, 12:14], s[:, 14:16], ALU.add).then_inc(w_sum, 1)
                dve.wait_ge(w_sum, hd + 1)
                dve.tensor_tensor(s[:, 20:22], s[:, 18:20], s[:, 16:18], ALU.add).then_inc(s_sum, 1)
                dve.wait_ge(s_sum, n + 1)
                dve.reciprocal(s[:, 24:26], s[:, 20:22]).then_inc(s_inv, 1)
                dve.wait_ge(s_inv, n + 1)
                dve.tensor_tensor(S, S, s[:, 24:26].unsqueeze(2).to_broadcast([P, 2, 512]),
                                  ALU.mult).then_inc(s_p, 1)

            def w_out(hd):
                n = HEADS + hd
                dve.wait_ge(s_tr, n + 1)
                if hd >= 2:
                    dve.wait_ge(s_pv, n - 1)
                dve.tensor_copy(w_pT(hd)[:, 2:4, :],
                                ps[:, 5, :].rearrange("p (k t) -> p k t", k=2)).then_inc(s_trev2, 1)

            dve.wait_ge(rest_in, REST_IN)
            w_max(0)
            w_max(1)
            for hd in range(HEADS):
                w_scale(hd)
                if hd + 2 < HEADS:
                    w_max(hd + 2)
                w_out(hd)
                if hd % 2 == 1 and hd >= 3:
                    o_out(o_w, (hd - 3) // 2, HEADS)
                if hd < 4:
                    pair_lo(dve, X_PA, hd, two_chunks(ya, hd))
            o_out(o_w, 7, HEADS)
            for u in range(2):
                split_lo(dve, U_PA + u)
            for u in range(4):
                split_lo(dve, U_PA + 2 + u)
                pair_lo(dve, X_PB, u, two_chunks(o_w, u))
            for i, (bank, g) in enumerate(((0, ga), (4, gb))):
                if i:
                    for u in range(3):
                        split_lo(dve, U_PB + 2 + u)
                taken(dve, (U_PA, U_PB)[i] + 3)
                for b in range(4):
                    v = g[:, 2 * b:2 * b + 2, :]
                    dve.tensor_tensor(v, v, ps[:, bank + b, :].rearrange("p (c t) -> p c t", c=2),
                                      ALU.mult).then_inc(pab_ev, 1)
            split_lo(dve, U_WO + 1)
            for u in range(4):
                pair_lo(dve, X_WO, u, two_chunks(gb, u))
                if u == 0:
                    split_lo(dve, U_WO + 2)
            split_lo(dve, U_WO + 3)
            taken(dve, U_WO + 3)
            for k in range(8):
                ins = dve.scalar_tensor_tensor(out=h[:, k, :], in0=ps[:, k // 2, (k % 2) * T:(k % 2) * T + T],
                                               scalar=mod[:, 0, 16 + k:17 + k], in1=h[:, k, :], op0=ALU.mult,
                                               op1=ALU.add)
                if k % 2:
                    ins.then_inc(x2_done, 1)
            mod_norm(N_MOE, h, xn, 2, 0, 24)

            seq = [0]

            def step(ins):
                seq[0] += 1
                ins.then_inc(r_seq, 1)
                dve.wait_ge(r_seq, seq[0])

            s = st[:, 0, :]
            dve.wait_ge(lg_mm, 1)
            step(dve.tensor_reduce(s[:, 0:2], ps[:, 5, 0:32].rearrange("p (t e) -> p t e", t=2), AX_X, ALU.max))
            step(dve.tensor_scalar(s[:, 2:4], s[:, 0:2], -1.0, None, ALU.mult))
            dve.wait_ge(r_exp, 1)
            step(dve.reciprocal(s[:, 6:8], s[:, 4:6]))
            step(dve.tensor_tensor(aff, aff, s[:, 6:8].unsqueeze(2).to_broadcast([P, 2, EXPERTS]), ALU.mult))
            assert seq[0] == R_AFF
            dve.wait_ge(r_tr, 1)
            work = rank_work[0:EXPERTS, 0, :]
            step(dve.tensor_copy(work, ps[0:EXPERTS, 6, 0:T]))
            top = e_small[0:EXPERTS, 0, 32:40]
            for _r in range(CAP // 8):
                step(dve.max(top, work))
                step(dve.match_replace(work, top, work, -1.0))
            step(dve.tensor_scalar(rank_work[0:EXPERTS, 1, :], work, 0.0, None, ALU.is_lt))
            assert seq[0] == R_MASK
            dve.wait_ge(r_tr, 2)
            step(dve.tensor_copy(e_small[:, 1, 0:32], ps[:, 7, 0:32]))
            assert seq[0] == R_MASKT
            dve.wait_ge(r_pos, 1)
            step(dve.tensor_scalar(e_small[:, 0, 0:32], e_small[:, 1, 0:32], -1.0, 1000.0, ALU.add, ALU.mult))
            step(dve.tensor_tensor(e_small[:, 1, 32:64], e_small[:, 0, 0:32], ps[:, 5, 0:32], ALU.add))
            p4 = pick.rearrange("p t (e s) -> p (t e) s", e=EXPERTS)
            dve.tensor_tensor(p4, e_small[:, 1, 32:64].unsqueeze(2).to_broadcast([P, 32, CAP]),
                              tab("slot").unsqueeze(1).to_broadcast([P, 32, CAP]), ALU.is_equal).then_inc(pick_set, 1)
            dve.wait_ge(pick_set, 1)
            dve.tensor_tensor(wpick.rearrange("p t (e s) -> p (t e) s", e=EXPERTS), p4,
                              aff.rearrange("p t e -> p (t e)").unsqueeze(2).to_broadcast([P, 32, CAP]),
                              ALU.mult).then_inc(pick_set, 1)
            step(dve.memset(zeros_row, 0.0))
            assert seq[0] == R_ZERO

            def expert(e):
                first = isinstance(e, int)
                dve.wait_ge(e_act, e + 1)
                dve.wait_ge(e_used, e * E_UNITS + 8)
                if not first:
                    dve.wait_ge(eh_tr, e)
                dve.tensor_tensor(e_hid, e_silu, ps[:, 5, :], ALU.mult).then_inc(e_hset, 1)
                dve.wait_ge(eh_tr, e + 1)
                if not first:
                    dve.wait_ge(e_used, e * E_UNITS)
                dve.tensor_copy(e_hidT, ps[:, 7, :]).then_inc(eh_ev, 1)

            expert(0)
            with dve.Fori(1, EXPERTS) as e:
                expert(e)
            dve.wait_ge(moe_mm, EXPERTS)
            for k in range(8):
                dve.scalar_tensor_tensor(out=h[:, k, :], in0=ps[:, k // 2, (k % 2) * T:(k % 2) * T + T],
                                         scalar=mod[:, 0, 40 + k:41 + k], in1=h[:, k, :], op0=ALU.mult,
                                         op1=ALU.add).then_inc(moe_done, 1)
            inverse(N_END)
            pre(N_END, gain_of("final"))

        @block.gpsimd
        def _(pool):
            pool.memset(rel[32:33, :], NEG).then_inc(rel_set, 1)
            for u in range(8):
                pool.wait_ge(qk_rot, u + 1)
                dst = (q_r if u % 2 == 0 else k_r)[:, u // 2, :, :].rearrange("p c t -> p (c t)")
                pool.tensor_tensor(dst, rot[:, u % 2, 0, :], rot[:, u % 2, 1, :], ALU.add).then_inc(qk_done, 1)
            for u in range(8):
                pool.wait_ge(g_ev, u + 1)
                pool.wait_ge(on_ev, u // 2 + 1)
                v = o_r[:, 2 * u:2 * u + 2, :].rearrange("p c t -> p (c t)")
                pool.tensor_tensor(v, v, gs[:, u % 2, :], ALU.mult).then_inc(og_done, 1)

            def residual(n):
                for k in range(8):
                    pool.wait_ge(scaled, POST[n] + k + 1)
                    pool.tensor_tensor(h[:, k, :], h[:, k, :], xn[:, k, :], ALU.add).then_inc(h_ready, 1)

            for n in (N_POST0, N_POSTF0, N_POST1, N_POSTF1):
                residual(n)
            for b in range(4):
                pool.wait_ge(pab_ev, 4 + b + 1)
                pool.tensor_tensor(gb[:, 2 * b:2 * b + 2, :], gb[:, 2 * b:2 * b + 2, :], ga[:, 2 * b:2 * b + 2, :],
                                   ALU.add).then_inc(merged, 1)
            pool.wait_ge(pick_set, 2)
            pool.wait_ge(xe_ev, 8)

            def expert(e):
                if isinstance(e, int):
                    x, p = xe[:, :, 0:CAP], wpick[:, :, 0:CAP]
                else:
                    pool.wait_ge(ep_tr, e)
                    x, p = xe[:, :, bass.ds(e * CAP, CAP)], wpick[:, :, bass.ds(e * CAP, CAP)]
                pool.tensor_copy(xcur, x).then_inc(cur_set, 1)
                pool.tensor_copy(pcur, p.unsqueeze(2).to_broadcast([P, 2, 4, CAP])).then_inc(cur_set, 1)

            expert(0)
            with pool.Fori(1, EXPERTS) as e:
                expert(e)


def rotary_tables():
    f = np.float32
    pos = np.arange(T, dtype=f)
    theta = (f(1.0) / f(10000.0) ** np.linspace(0.0, 1.0, RET_QK // 2, dtype=f)).astype(f)
    ret = (theta[:, None] * pos[None, :]).astype(f)
    freq = (f(10000.0) ** (-np.arange(0, HD // 2, 2, dtype=f) / f(HD // 2))).astype(f)
    tok = np.arange(T)
    rows = freq[:, None] * (tok // GRID_W).astype(f)[None, :]
    cols_ = freq[:, None] * (tok % GRID_W).astype(f)[None, :]
    rope = np.tile(np.concatenate([rows, rows, cols_, cols_], axis=0), (2, 1)).astype(f)
    return ret, rope


def shape_tables():
    f = np.float32
    ret, rope = rotary_tables()
    perm = np.zeros((P, P), f)
    for m in range(P):
        perm[m + 16 if m % 32 < 16 else m - 16, m] = -1.0 if m % 32 < 16 else 1.0
    p = np.arange(P)
    tok, key = np.arange(T).reshape(2, P).T, np.arange(T)
    band = np.where(np.abs(key[None, None, :] - tok[:, :, None]) <= WINDOW, f(0.0), f(NEG)).reshape(P, 2 * T)
    parts = {"ident": np.eye(P), "perm": perm, "tri": p[:, None] < p[None, :],
             "slot": np.tile(np.arange(CAP), (P, 1)), "ret_cos": np.cos(ret), "ret_sin": np.sin(ret),
             "ret_nsin": -np.sin(ret), "rope_cos": np.cos(rope), "rope_sin": np.sin(rope), "band": band}
    return np.concatenate([parts[n].astype(f) for n in TABS], axis=1)


def decay_table():
    log_gamma = np.log(1.0 - 2.0 ** (-5.0 - np.arange(RET_HEADS)))
    rel = np.arange(T)[None, :] - np.arange(P)[:, None]
    one = [np.where(rel >= 0, np.exp(np.maximum(rel, 0) * g), 0.0) * RET_QK ** -0.5 for g in log_gamma]
    return np.concatenate([np.concatenate([m, m[:, :P]], axis=1) for m in one], axis=1).astype(np.float32)


def bucket_table(dist):
    f = np.float32
    half = BUCKETS // 2
    n = np.maximum(dist, 0)
    nf = np.maximum(n, 1).astype(f)
    large = half + (np.log(nf / f(half)) / f(np.log(MAX_DIST / half)) * f(BUCKETS - half)).astype(np.int32)
    bucket = np.where(n < half, n, np.minimum(large, BUCKETS - 1))
    bucket = np.where(dist >= 0, bucket, BUCKETS)
    return (np.arange(BUCKETS + 1)[:, None] == bucket.reshape(1, -1)).astype(f)


def kernel(**inputs):
    import concourse.bacc as bacc
    from concourse.bass_utils import run_bass_kernel_spmd

    x = {n: np.asarray(v) for n, v in inputs.items()}

    def by_chunk(v):
        return v.reshape(-1, P).T

    def pairs(pe):
        return pe.reshape(CMP_LEN // 2, 2 * HD).T

    small = {"mix_pre0": x["mix_norm_pre"][0], "mix_pre1": x["mix_norm_pre"][1], "mix_post0": x["mix_norm_post"][0],
             "mix_post1": x["mix_norm_post"][1], "ffn_pre0": x["ffn_norm_pre"][0], "ffn_pre1": x["ffn_norm_pre"][1],
             "ffn_post0": x["ffn_norm_post"][0], "ffn_post1": x["ffn_norm_post"][1], "kv_norm": x["kv_norm"],
             "norm1": x["norm1_g_2"], "norm2": x["norm2_g_2"], "final": x["final_g_2"], "b_ada": x["b_ada_2"],
             "b_merge": x["b_merge_gate_2"], "c": x["c_2"], "c_ctx": x["c_ctx_2"]}
    columns = [by_chunk(small[n]) if n in small else pairs(x["cmp_" + n]) for n in COLS]
    tok = np.arange(P)[None, :]
    cmp_dist = np.concatenate([(P * t + tok - (CMP_STRIDE * n + CMP_LEN - 1)) for t in range(2) for n in range(N_CMP)])
    arrays = {
        "xT": x["x"][0].T, "ctxT": x["ctx_2"][0].T, "cols": np.concatenate(columns, axis=1),
        "tabs": shape_tables(), "decay": decay_table(), "bucket_rows": bucket_table(T - 1 - np.arange(384)),
        "bucket_cmp": bucket_table(cmp_dist), "rel_bias": x["rel_bias"],
        "ret_w_in": x["ret_w_in"][0], "ret_w_out": x["ret_w_out"][0],
        "ffn_w_in0": x["ffn_w_in"][0], "ffn_w_in1": x["ffn_w_in"][1],
        "ffn_w_out0": x["ffn_w_out"][0], "ffn_w_out1": x["ffn_w_out"][1], "kv_w": x["kv_w"],
        "cmp_w1_k": x["cmp_w1_k"], "cmp_w1_v": x["cmp_w1_v"], "cmp_w2_k": x["cmp_w2_k"], "cmp_w2_v": x["cmp_w2_v"],
        "nsa_w_in": x["nsa_w_in"][0], "nsa_w_out": x["nsa_w_out"][0], "w_ada_2": x["w_ada_2"][0],
        "w_in_2": x["w_in_2"][0], "gmlp_ln_g_2": x["gmlp_ln_g_2"][0], "gmlp_ln_b_2": x["gmlp_ln_b_2"][0],
        "w_spatialT": x["w_spatial_2"][0].transpose(2, 0, 1), "b_spatial_2": x["b_spatial_2"][0],
        "attn_sink_2": x["attn_sink_2"][0], "w_proj_a_2": x["w_proj_a_2"][0], "w_proj_b_2": x["w_proj_b_2"][0],
        "w_out_2": x["w_out_2"][0], "w_router_2": x["w_router_2"][0], "w_exp_gate_2": x["w_exp_gate_2"][0],
        "w_exp_up_2": x["w_exp_up_2"][0], "w_exp_down_2": x["w_exp_down_2"][0],
    }
    arrays = {n: np.ascontiguousarray(v) for n, v in arrays.items()}
    nc = bacc.Bacc("TRN2", target_bir_lowering=False, num_devices=1, dynamic_dma_scratch_size=4096)
    aps = {n: nc.dram_tensor("in_" + n, v.shape, mybir.dt.from_np(v.dtype), kind="ExternalInput").ap()
           for n, v in arrays.items()}
    out = nc.dram_tensor("outT", (D, T), F32, kind="ExternalOutput").ap()
    program(nc, aps, out)
    r = run_bass_kernel_spmd(nc, [{"in_" + n: v for n, v in arrays.items()}], core_ids=[0])
    return np.ascontiguousarray(r.results[0]["outT"].T).reshape(1, T, D)
```
